# Optimizing a Trainium2 kernel written in Bass

```python
import jax, jax.numpy as jnp
from jax import lax
import numpy as np

D_MODEL = 1024
BATCH = 1
SEQ = 512
DEPTH = 2

RW_HEADS = 16
RW_HEAD_DIM = 64
RW_WIDTH = RW_HEADS * RW_HEAD_DIM
RW_DECAY_LORA = 64
RW_AAA_LORA = 64
RW_MV_LORA = 32
RW_GATE_LORA = 128
RW_LN_EPS = 64e-5

GM_GROUPS = 8
GM_CHUNK = 128
GM_WIDTH = 1024
GM_GROUP_DIM = GM_WIDTH // GM_GROUPS
GM_LN_EPS = 1e-5

C_IN = 3 * RW_WIDTH + RW_DECAY_LORA + RW_AAA_LORA + RW_GATE_LORA + 2 * GM_WIDTH + 2 * D_MODEL

PEER_HEADS = 8
PEER_KEYS = 128
PEER_EXPERTS = PEER_KEYS * PEER_KEYS
PEER_DKEY = 256
PEER_HALF = PEER_DKEY // 2
PEER_TOPK = 16
PEER_TOKEN_BLOCK = 128

PLE_DIM = 256

RMS_EPS = 1e-6

kernel_name = "hybrid_rwkv7_gmlp_peer_trunk"

def _split_points():
    sizes = (RW_WIDTH, RW_WIDTH, RW_WIDTH, RW_DECAY_LORA, RW_AAA_LORA, RW_GATE_LORA,
             GM_WIDTH, GM_WIDTH, D_MODEL, D_MODEL)
    pts, acc = [], 0
    for s in sizes[:-1]:
        acc += s
        pts.append(acc)
    return tuple(pts)

def _rmsnorm(x, g):
    xf = x.astype(jnp.float32)
    y = xf * lax.rsqrt(jnp.mean(xf * xf, axis=-1, keepdims=True) + RMS_EPS)
    return (y * g.astype(jnp.float32)).astype(x.dtype)

def _layernorm(x, g, b, eps):
    xf = x.astype(jnp.float32)
    mu = jnp.mean(xf, axis=-1, keepdims=True)
    var = jnp.mean(jnp.square(xf - mu), axis=-1, keepdims=True)
    y = (xf - mu) * lax.rsqrt(var + eps) * g.astype(jnp.float32) + b.astype(jnp.float32)
    return y.astype(x.dtype)

def _token_shift(x):
    return jnp.pad(x, ((0, 0), (1, 0), (0, 0)))[:, :-1]

def _wkv7_scan(r, w, k, v, a, b):
    B, S, H, N = r.shape

    def step(state, inp):
        r_t, w_t, k_t, v_t, a_t, b_t = inp
        sa = jnp.einsum('bhvk,bhk->bhv', state, a_t)
        state = (state * w_t[:, :, None, :]
                 + sa[:, :, :, None] * b_t[:, :, None, :]
                 + v_t[:, :, :, None] * k_t[:, :, None, :])
        y_t = jnp.einsum('bhvk,bhk->bhv', state, r_t)
        return state, y_t

    xs = tuple(jnp.moveaxis(t, 1, 0) for t in (r, w, k, v, a, b))
    state0 = jnp.zeros((B, H, N, N), jnp.float32)
    _, ys = lax.scan(step, state0, xs)
    return jnp.moveaxis(ys, 0, 1)

def _rwkv7_branch(zr, zk, zv, zw, za, zg, w0, w2, a0, a2, g2, k_k, k_a, r_k, ln_g, ln_b):
    B, S, _ = zr.shape
    f32 = jnp.float32
    zw, za, zg = zw.astype(f32), za.astype(f32), zg.astype(f32)
    w_log = -jax.nn.softplus(-(w0.astype(f32) + jnp.tanh(zw) @ w2.astype(f32))) - 0.5
    decay = jnp.exp(-jnp.exp(w_log))
    a_rate = jax.nn.sigmoid(a0.astype(f32) + za @ a2.astype(f32))
    gate = jax.nn.sigmoid(zg) @ g2.astype(f32)
    kf = zk.astype(f32)
    kk = kf * k_k.astype(f32)
    k = kf * (1.0 + (a_rate - 1.0) * k_a.astype(f32))

    def heads(t):
        return t.astype(f32).reshape(B, S, RW_HEADS, RW_HEAD_DIM)

    r, k, v, kk, decay, a_rate = heads(zr), heads(k), heads(zv), heads(kk), heads(decay), heads(a_rate)
    kk = kk * lax.rsqrt(jnp.maximum(jnp.sum(kk * kk, axis=-1, keepdims=True), 1e-24))
    y = _wkv7_scan(r, decay, k, v, -kk, kk * a_rate)
    mu = jnp.mean(y, axis=-1, keepdims=True)
    var = jnp.mean(jnp.square(y - mu), axis=-1, keepdims=True)
    y = (y - mu) * lax.rsqrt(var + RW_LN_EPS)
    y = y * ln_g.astype(f32).reshape(RW_HEADS, RW_HEAD_DIM) + ln_b.astype(f32).reshape(RW_HEADS, RW_HEAD_DIM)
    y = y + jnp.sum(r * k * r_k.astype(f32), axis=-1, keepdims=True) * v
    return (y.reshape(B, S, RW_WIDTH) * gate).astype(zr.dtype)

def _gmlp_branch(zu, zv, ln_g, ln_b, ws, bs):
    B, S, _ = zu.shape
    u = jax.nn.gelu(zu)
    v = _layernorm(jax.nn.gelu(zv), ln_g, ln_b, GM_LN_EPS)
    vb = v.reshape(B, S // GM_CHUNK, GM_CHUNK, GM_GROUPS, GM_GROUP_DIM)
    mask = jnp.tril(jnp.ones((GM_CHUNK, GM_CHUNK), dtype=bool))
    w_c = jnp.where(mask[None], ws, jnp.zeros_like(ws))
    s = jnp.einsum('gtp,bnpgc->bntgc', w_c, vb) + bs.T[None, None, :, :, None]
    return u * s.reshape(B, S, GM_WIDTH)

def _peer(x, wq, keys, u_tab, v_tab):
    B, S, D = x.shape
    T = B * S
    xt = x.reshape(T // PEER_TOKEN_BLOCK, PEER_TOKEN_BLOCK, D)

    def block(xb):
        tb = xb.shape[0]
        q = (xb @ wq).reshape(tb, PEER_HEADS, 2, PEER_HALF).astype(jnp.float32)
        sc = jnp.einsum('thpc,hpkc->thpk', q, keys.astype(jnp.float32))
        s_top, i_top = lax.top_k(sc, PEER_TOPK)
        cand = s_top[:, :, 0, :, None] + s_top[:, :, 1, None, :]
        best, pos = lax.top_k(cand.reshape(tb, PEER_HEADS, PEER_TOPK * PEER_TOPK), PEER_TOPK)
        idx = (jnp.take_along_axis(i_top[:, :, 0, :], pos // PEER_TOPK, axis=-1) * PEER_KEYS
               + jnp.take_along_axis(i_top[:, :, 1, :], pos % PEER_TOPK, axis=-1))
        gw = jax.nn.softmax(best, axis=-1).astype(xb.dtype)
        u_sel = u_tab[idx]
        act = jax.nn.gelu(jnp.einsum('thkd,td->thk', u_sel, xb))
        v_sel = v_tab[idx]
        return jnp.einsum('thk,thkd->td', gw * act, v_sel)

    out = lax.map(block, xt)
    return out.reshape(B, S, D)

def setup_inputs(seed: int = 0) -> dict:
    key = jax.random.key(seed)
    ks = jax.random.split(key, 32)

    def nrm(j, shape, scale):
        return scale * jax.random.normal(ks[j], shape, jnp.float32)

    L = DEPTH
    D = D_MODEL
    return {
        "x": nrm(0, (BATCH, SEQ, D), 1.0),
        "p": nrm(1, (DEPTH, BATCH, SEQ, PLE_DIM), 1.0),
        "norm_mix": 1.0 + nrm(2, (L, D), 0.02),
        "norm_ffn": 1.0 + nrm(3, (L, D), 0.02),
        "norm_final": 1.0 + nrm(4, (D,), 0.02),
        "w_in": nrm(5, (L, 2 * D, C_IN), (2 * D) ** -0.5),
        "rw_w0": nrm(6, (L, RW_WIDTH), 0.5),
        "rw_w2": nrm(7, (L, RW_DECAY_LORA, RW_WIDTH), 0.5 * RW_DECAY_LORA ** -0.5),
        "rw_a0": nrm(8, (L, RW_WIDTH), 0.1),
        "rw_a2": nrm(9, (L, RW_AAA_LORA, RW_WIDTH), 0.5 * RW_AAA_LORA ** -0.5),
        "rw_g2": nrm(10, (L, RW_GATE_LORA, RW_WIDTH), RW_GATE_LORA ** -0.5),
        "rw_kk": 0.85 + nrm(11, (L, RW_WIDTH), 0.02),
        "rw_ka": 1.0 + nrm(12, (L, RW_WIDTH), 0.02),
        "rw_rk": nrm(13, (L, RW_HEADS, RW_HEAD_DIM), 0.1),
        "rw_ln_g": 1.0 + nrm(14, (L, RW_WIDTH), 0.02),
        "rw_ln_b": nrm(15, (L, RW_WIDTH), 0.02),
        "rw_mv_w1": nrm(16, (L - 1, 2 * D, RW_MV_LORA), (2 * D) ** -0.5),
        "rw_mv_w2": nrm(17, (L - 1, RW_MV_LORA, RW_WIDTH), RW_MV_LORA ** -0.5),
        "rw_mv_v0": nrm(18, (L - 1, RW_WIDTH), 0.1),
        "gm_ln_g": 1.0 + nrm(19, (L, GM_WIDTH), 0.02),
        "gm_ln_b": nrm(20, (L, GM_WIDTH), 0.02),
        "gm_ws": nrm(21, (L, GM_GROUPS, GM_CHUNK, GM_CHUNK), 0.5 * GM_CHUNK ** -0.5),
        "gm_bs": 1.0 + nrm(22, (L, GM_GROUPS, GM_CHUNK), 0.02),
        "w_proj_a": nrm(23, (L, RW_WIDTH, D), RW_WIDTH ** -0.5),
        "w_proj_b": nrm(24, (L, GM_WIDTH, D), GM_WIDTH ** -0.5),
        "w_out": nrm(25, (L, D, D), D ** -0.5),
        "peer_wq": nrm(26, (L, D, PEER_HEADS * PEER_DKEY), D ** -0.5),
        "peer_keys": nrm(27, (L, PEER_HEADS, 2, PEER_KEYS, PEER_HALF), PEER_HALF ** -0.5),
        "peer_u": nrm(28, (L, PEER_EXPERTS, D), D ** -0.5),
        "peer_v": nrm(29, (L, PEER_EXPERTS, D), 0.1),
        "ple_w": nrm(30, (L, PLE_DIM, D), 0.5 * PLE_DIM ** -0.5),
        "ple_gate": nrm(31, (L, D, D), D ** -0.5),
    }

def reference(x, p, norm_mix, norm_ffn, norm_final, w_in, rw_w0, rw_w2, rw_a0, rw_a2, rw_g2,
              rw_kk, rw_ka, rw_rk, rw_ln_g, rw_ln_b, rw_mv_w1, rw_mv_w2, rw_mv_v0,
              gm_ln_g, gm_ln_b, gm_ws, gm_bs, w_proj_a, w_proj_b, w_out,
              peer_wq, peer_keys, peer_u, peer_v, ple_w, ple_gate):
    split_pts = _split_points()
    h = x
    v_first = None
    for i in range(DEPTH):
        n = _rmsnorm(h, norm_mix[i])
        nx = jnp.concatenate([n, _token_shift(n)], axis=-1)
        z = nx @ w_in[i]
        zr, zk, zv, zw, za, zg, zu, zgv, zga, zgb = jnp.split(z, split_pts, axis=-1)
        if i == 0:
            v_first = zv
        else:
            vmix = jax.nn.sigmoid(rw_mv_v0[i - 1] + (nx @ rw_mv_w1[i - 1]) @ rw_mv_w2[i - 1])
            zv = zv + (v_first - zv) * vmix
        ya = _rwkv7_branch(zr, zk, zv, zw, za, zg, rw_w0[i], rw_w2[i], rw_a0[i], rw_a2[i], rw_g2[i],
                           rw_kk[i], rw_ka[i], rw_rk[i], rw_ln_g[i], rw_ln_b[i])
        yb = _gmlp_branch(zu, zgv, gm_ln_g[i], gm_ln_b[i], gm_ws[i], gm_bs[i])
        merged = (jax.nn.sigmoid(zga) * (ya @ w_proj_a[i])
                  + jax.nn.sigmoid(zgb) * (yb @ w_proj_b[i]))
        h = h + merged @ w_out[i]
        n2 = _rmsnorm(h, norm_ffn[i])
        h = h + _peer(n2, peer_wq[i], peer_keys[i], peer_u[i], peer_v[i])
        h = h + (p[i] @ ple_w[i]) * jax.nn.sigmoid(n2 @ ple_gate[i])
    return _rmsnorm(h, norm_final)


_drawn_inputs = setup_inputs


def setup_inputs(seed=0):
    import zlib

    import numpy as np

    out = dict(_drawn_inputs(seed))
    spreads = {}
    factors = {'norm_ffn': 19.911,
     'norm_final': 23.655,
     'rw_a0': 2.685,
     'rw_kk': 200.0,
     'rw_ka': 5.126,
     'rw_ln_g': 23.561,
     'rw_ln_b': 22.887,
     'rw_mv_v0': 5.654,
     'gm_ln_g': 35.931,
     'gm_ln_b': 35.053,
     'gm_bs': 20.771}
    for name, (base, spread) in spreads.items():
        noise = np.random.default_rng([zlib.crc32(name.encode()), seed]).standard_normal(out[name].shape)
        drawn = base * np.exp(spread * noise) if base else spread * noise
        out[name] = __import__('jax').numpy.asarray(drawn.astype(out[name].dtype))
    for name, factor in factors.items():
        out[name] = (out[name] * factor).astype(out[name].dtype)
    return out
```

```python
from contextlib import ExitStack

import numpy as np

import concourse.bass as bass
from concourse import mybir

F32 = mybir.dt.float32
U32 = mybir.dt.uint32
ACT = mybir.ActivationFunctionType
ALU = mybir.AluOpType
AXX = mybir.AxisListType.X

P = 128
T = 512
D = 1024
L = 2
KB = D // P
TB = T // P
CH = 64
NC = T // CH
PAIRS = KB
SLOT = 2048
NG = 4
JG = P // NG
TG = 16
TOPK = 16
HEADS = 8
RMS_EPS = 1e-6
RW_EPS = 64e-5
GM_EPS = 1e-5
DECAY = float(np.exp(-0.5))
LOWEST = -3.0e38

VEC = ["norm_mix", "w0", "a0", "kk", "ka", "rk", "ln_g", "ln_b", "v0", "norm_ffn", "final"]
LEVELS = 6

RING = [("wa", 1), ("zg", 1), ("mv1", 1), ("rwkv", 4 * KB), ("g2", 1), ("gv", 8), ("zu", KB),
        ("mix", 3 * KB), ("wout", 4), ("plew", 1), ("pleg", 4), ("wq", 8), ("keys", 1),
        ("u0", JG // 2)]
for _g in range(NG):
    if _g + 1 < NG:
        RING.append((f"u{_g + 1}", JG // 2))
    RING.append((f"v{_g}", 2 * KB))
RING_AT, _n = {}, 0
for _name, _c in RING:
    RING_AT[_name] = _n
    _n += _c
RING_LAYER = _n
assert RING_LAYER % 2 == 0
PACKED = [n for n, _ in RING if n[0] != "v" and not n[1:].isdigit() or n in ("g2",)]
PACKED = ["wa", "zg", "mv1", "rwkv", "g2", "gv", "zu", "mix", "wout", "plew", "pleg", "wq", "keys"]
PACK_AT, _n = {}, 0
for _name in PACKED:
    PACK_AT[_name] = _n
    _n += 3 * KB if _name == "rwkv" else dict(RING)[_name]
PACK_LAYER = _n

_all = lambda n: {b: n for b in range(8)}
BANKS = [
    ("norm1", {0: 1}), ("lora", {4: 1, 5: 1, 6: 1}), ("rwkv", _all(KB)),
    ("scan", {0: 7 * NC, 1: 7 * NC, 2: 9 * NC, 3: 9 * NC, 4: 7 * NC, 5: 7 * NC, 6: 3 * NC, 7: 3 * NC}),
    ("head", _all(3)), ("gv", _all(1)), ("zu", {0: 4, 1: 4, 2: 4, 3: 4}), ("mix", _all(4)),
    ("wout", {0: 2, 1: 2, 2: 2, 3: 2}), ("norm2", {0: 1}), ("plew", _all(1)),
    ("pleg", {0: 2, 1: 2, 2: 2, 3: 2}), ("wq", {0: 4, 1: 4, 2: 4, 3: 4}),
    ("keys", {4: 4, 5: 4, 6: 4, 7: 4}), ("h0", {0: 16, 1: 16}), ("idx", {4: 1, 5: 1, 6: 1}),
]
for _g in range(NG):
    BANKS.append((f"build{_g}", {6: 16, 7: 16} | ({0: 16, 1: 16} if _g + 1 < NG else {})))
    BANKS.append((f"down{_g}", {2: 4, 3: 4}))
BANK_AT, BANK_LAYER = {}, [0] * 8
for _name, _uses in BANKS:
    BANK_AT[_name] = list(BANK_LAYER)
    for _b, _c in _uses.items():
        BANK_LAYER[_b] += _c


def use(layer, stage, bank, k=0):
    return layer * BANK_LAYER[bank] + (k + (BANK_AT[stage][bank] + 1))


def ring(layer, section, k, i=0, per=0):
    n = RING_AT[section] + k
    if per:
        return n % 2, layer * (RING_LAYER // 2) + (i * (per // 2) + (n // 2 + 1))
    return n % 2, layer * (RING_LAYER // 2) + (n // 2 + 1)


CONST, _n = {}, 0
for _name, _c in [("ident", P), ("ones", P), ("blk", P), ("reset", T), ("up", P), ("upd", P),
                  ("lvlN", P), ("lvl", LEVELS * P), ("iota", P), ("causal", P)]:
    CONST[_name] = (_n, _n + _c)
    _n += _c
CONST_COLS = _n


def constants():
    c = np.zeros((P, CONST_COLS), np.float32)
    s = np.arange(P)[:, None]
    t = np.arange(P)[None, :]
    same = s // CH == t // CH

    def put(name, a):
        lo, hi = CONST[name]
        c[:, lo:hi] = a

    put("ident", s == t)
    put("ones", 1.0)
    put("blk", same)
    put("reset", np.arange(T)[None, :] % CH != 0)
    put("up", same & (s < t))
    put("upd", same & (s <= t))
    lv = []
    for n in range(1, LEVELS + 1):
        w = 1 << (n - 1)
        lv.append((s // (2 * w) == t // (2 * w)) & (s // w % 2 == 1) & (t // w % 2 == 0))
    put("lvlN", lv[0].T)
    put("lvl", np.concatenate(lv, axis=1))
    put("iota", t)
    put("causal", s <= t)
    return c


class Arena:

    def __init__(self, tensor):
        self.t, self.n = tensor, 0

    def take(self, cols):
        self.n += cols
        return self.n - cols

    def at(self, lo, cols):
        return self.t[:, lo:lo + cols]


def trunk_kernel(nc, x, w, lo, u, v, pt, gm, vec, const, out, vfirst):
    ctx = ExitStack()
    with ctx:
        def sem(name):
            return ctx.enter_context(nc.semaphore(name))

        COLS = 52800
        ar = Arena(ctx.enter_context(nc.sbuf_tensor("arena", [P, COLS], F32)))
        psum = ctx.enter_context(nc.psum_tensor("psum", [P, 8, T], F32))
        ds, ts = bass.ds, bass.ts

        def tile(lo_, *shape):
            n = int(np.prod(shape))
            a = ar.at(lo_, n)
            if len(shape) == 2:
                return a.rearrange("p (a b) -> p a b", a=shape[0])
            if len(shape) == 3:
                return a.rearrange("p (a b c) -> p a b c", a=shape[0], b=shape[1])
            return a

        h = tile(ar.take(KB * T), KB, T)
        cst = tile(ar.take(CONST_COLS), CONST_COLS)
        vecs = tile(ar.take(len(VEC) * KB), len(VEC), KB)
        slots = tile(ar.take(2 * SLOT), 2, SLOT)
        small = ar.take(4 * T)
        wa_in, zg_in, mv_in, rstd = (tile(small + i * T, T) for i in range(4))
        pend = tile(ar.take(KB * NC), KB, NC)
        NW = T + 1
        n_at = ar.take(KB * NW)
        n = tile(n_at, KB, NW)
        field_at = ar.take(6 * KB * T)
        fields = [field_at + i * KB * T for i in range(6)]
        rest = ar.n
        assert COLS - rest >= 10240, COLS - rest

        def cc(name, i=0, width=None):
            a, b = CONST[name]
            return cst[:, a:b] if width is None else cst[:, a + i * width:a + (i + 1) * width]

        ident, ones, blk = cc("ident"), cc("ones"), cc("blk")

        def vcol(name, m):
            return vecs[:, VEC.index(name), ds(m, 1)] if not isinstance(m, int) else vecs[:, VEC.index(name), m:m + 1]

        fa, fb, fk, fr, fv, fbon = (tile(f, KB, T) for f in fields)
        sq_all = fv
        names = ["sg", "ar", "vm", "s", "se", "t", "kkr", "k", "sqk", "rn", "pinc", "pinv", "pexc",
                 "zv", "vf", "b", "rkt"]
        tmp = {q: tile(rest + i * T, T) for i, q in enumerate(names)}
        spots = [n_at + i * KB * P for i in range(4)] + [rest + i * KB * P for i in range(10)]
        bda, bdr, bdb, bdk, bdv, a1, lt, gak, grb, grk, bt, kt, vt, st = (tile(s, KB, P) for s in spots)
        xm, xt, loff, rhs, um = bdb, bdk, bdv, a1, lt
        yc, hsq = fa, fb
        gv = tile(fields[0], TB, D)
        gmp = tile(fields[1], 4 * D)
        wst = gmp[:, 0:D].rearrange("p (g t) -> p g t", g=KB)
        lng, lnb = gmp[:, D:2 * D], gmp[:, 2 * D:3 * D]
        bsb = gmp[:, 3 * D:4 * D].rearrange("p (g t) -> p g t", g=KB)
        yb = tile(fields[2], KB, T)
        merged = tile(fields[4], KB, T)
        ut = tile(rest, 2, T)
        spt = tile(rest + 2 * T, 2, T)
        stats = tile(rest + 4 * T, TB, 2, 6)
        mv2 = tile(rest + 4 * T + 64, TB, 2)
        lrs = tile(rest + 4 * T + 96, TB)
        gates = tile(rest, 4, T)
        mixed = tile(rest + 4 * T, 4, T)
        ppb = tile(fields[0], KB, T)
        ptb = tile(fields[1], 2, T)
        pgb = tile(fields[2], 2, T)
        pmul = tile(small, 2, T)
        gbuf = [tile(fields[0], JG, T), tile(fields[4], JG, T)]
        top_at = fields[4]
        q = tile(top_at, 2 * HEADS, T)
        sc = tile(top_at + 8192, TB, 2 * HEADS * P)
        keep_at = top_at + 16384
        idx = tile(keep_at, 3, T)
        bring = tile(keep_at + 3 * T, TG, JG)
        aring = tile(small, TG, P)
        so = [top_at]

        def scratch(*shape):
            a = tile(so[0], *shape)
            so[0] += int(np.prod(shape))
            return a

        NH = 2 * HEADS
        sw = scratch(NH, P)
        sx = scratch(NH, P)
        tv = scratch(NH, TOPK)
        ti = scratch(NH, TOPK)
        tif = scratch(NH, TOPK)
        bv = scratch(HEADS, TOPK)
        bp = scratch(HEADS, TOPK)
        bq = scratch(2, HEADS * TOPK)
        bqf = scratch(2, HEADS * TOPK)
        hsum = scratch(HEADS)
        hrec = scratch(HEADS)
        pick = scratch(3, P)
        assert so[0] <= top_at + 8192
        cand, cand2, eq = sw, sx, sw
        picks = tile(small, 3, TB * P)
        assert keep_at + 3 * T + TG * JG <= COLS

        landed = [sem(f"slot{i}_landed") for i in range(2)]
        used = [sem(f"slot{i}_used") for i in range(2)]
        ready = [sem(f"bank{b}_ready") for b in range(8)]
        free = [sem(f"bank{b}_free") for b in range(8)]
        x_in, const_in, vec_in, gm_in, pt_in = (sem(s) for s in ("x_in", "const_in", "vec_in", "gm_in", "pt_in"))
        layer_free = sem("layer_free")
        sq_ready, rms_ready, n_ready = sem("squares_ready"), sem("rms_ready"), sem("normed_ready")
        lora_ready = sem("lora_inputs_ready")
        cum_ready, kkr_ready, sqk_ready, rn_ready = (sem(s) for s in ("decay_sums_ready", "kk_ready", "kk_squares_ready", "kk_norm_ready"))
        p_ready, rk_ready, fields_ready = (sem(s) for s in ("decay_products_ready", "rk_ready", "fields_ready"))
        vf_out, vf_in = sem("v_first_out"), sem("v_first_in")
        bd_dve, bd_act, bd_pool, bd_zero = (sem(s) for s in ("diag_dve_ready", "diag_act_ready", "diag_pool_ready", "diag_zeroed"))
        gram_ready, tr_ready, l_ready, loff_ready = (sem(s) for s in ("gram_ready", "transposed_ready", "l_ready", "l_level_ready"))
        x_ready, a1_ready, rhs_ready, u_ready, s_ready = (sem(s) for s in ("inverse_ready", "half_step_ready", "rhs_ready", "u_ready", "state_ready"))
        y_ready, yc_ready, ysq_ready, yvar_ready, ysd_ready, ya_ready = (sem(s) for s in ("y_ready", "y_centred", "y_squares", "y_var", "y_sd", "ya_ready"))
        gelu_v, gvar_ready, gsd_ready, gvn_ready, ws_ready, ug_ready, yb_ready = (sem(s) for s in ("gelu_v_ready", "gm_var_ready", "gm_sd_ready", "gm_v_ready", "ws_masked", "gelu_u_ready", "yb_ready"))
        gate_ready, merged_ready = sem("gates_ready"), sem("merged_ready")
        pp_ready, pg_ready, q_ready = sem("ple_ready"), sem("ple_gate_ready"), sem("q_ready")
        sc_ready, ex_in, ex_out, picks_ready, idx_ready = (sem(s) for s in ("scores_ready", "softmax_in", "softmax_exp", "picks_ready", "idx_ready"))
        act_ready = sem("expert_act_ready")
        hot_ready, hot_used, gated = sem("one_hots_ready"), sem("one_hots_used"), sem("gated_ready")
        pg_used = sem("ple_gate_used")
        out_done = sem("out_written")

        HB = (0, 1)

        def half(t_, hf):
            return t_[:, 4 * hf:4 * hf + 4, :]

        def bank(b):
            return psum[:, b, :]

        def bank4(b):
            return psum[:, b, :].rearrange("p (a c) -> p a c", a=4)

        block = ctx.enter_context(nc.Block())

        @block.sync
        def _(sp):
            sp.dma_start(cst, const).then_inc(const_in, 16)
            sp.dma_start(h, x).then_inc(x_in, 16)

            def send(layer, section, k, src, i=0, per=0, cols=SLOT):
                s, count = ring(layer, section, k, i, per)
                dst = slots[:, s, 0:cols]
                count = sp.snap(count)
                sp.wait_ge(used[s], count)
                sp.dma_start(dst, src).then_inc(landed[s], 16)

            def packed(layer, section, count, per):
                at = PACK_AT[section]
                if count == per:
                    for k in range(count):
                        send(layer, section, k, w[ds(sp.snap(layer * PACK_LAYER + (at + k)), 1), :, :])
                    return
                with sp.Fori(0, count // per) as i:
                    for k in range(per):
                        send(layer, section, k, w[ds(sp.snap(layer * PACK_LAYER + (i * per + (at + k))), 1), :, :], i, per)

            with sp.Fori(0, L) as layer:
                for s in ("wa", "zg", "mv1"):
                    packed(layer, s, 1, 1)
                with sp.Fori(0, KB) as m:
                    send(layer, "rwkv", 0, lo[ds(sp.snap(layer * KB + m), 1), :, :], m, 4, 3 * P)
                    for k in range(3):
                        send(layer, "rwkv", 1 + k,
                             w[ds(sp.snap(layer * PACK_LAYER + (m * 3 + (PACK_AT["rwkv"] + k))), 1), :, :], m, 4)
                packed(layer, "g2", 1, 1)
                packed(layer, "gv", 8, 2)
                packed(layer, "zu", 8, 2)
                packed(layer, "mix", 24, 2)
                packed(layer, "wout", 4, 2)
                packed(layer, "plew", 1, 1)
                packed(layer, "pleg", 4, 2)
                packed(layer, "wq", 8, 2)
                packed(layer, "keys", 1, 1)
                for g in range(-1, NG):
                    if g + 1 < NG:
                        with sp.Fori(0, JG // 4) as i:
                            for k in range(2):
                                row = sp.snap(layer * (P // 2) + (i * 2 + ((g + 1) * JG // 2 + k)))
                                send(layer, f"u{g + 1}", k, u[ds(row, 1), :, :], i, 2)
                    if g >= 0:
                        with sp.Fori(0, KB) as i:
                            for k in range(2):
                                row = sp.snap(layer * (NG * 2 * KB) + (i * 2 + (g * 2 * KB + k)))
                                send(layer, f"v{g}", k, v[ds(row, 1), :, :], i, 2)
            sp.wait_ge(n_ready, 3 * L + 1)
            sp.dma_start(out, n[:, :, 1:NW]).then_inc(out_done, 16)
            sp.wait_ge(out_done, 16)

        @block.tensor
        def _(pe):
            mm = nc.tensor.matmul
            for s in range(2):
                pe.sem_inc(used[s], 1)
            for b in range(8):
                pe.sem_inc(free[b], 1)

            def take(layer, section, k, i=0, per=0):
                s, count = ring(layer, section, k, i, per)
                pe.wait_ge(landed[s], count * 16)
                return s, slots[:, s, :]

            def done(layer, section, k):
                return used[(RING_AT[section] + k) % 2]

            def open_(layer, stage, b, k=0):
                pe.wait_ge(free[b], use(layer, stage, b, k))

            def norm_sums(layer, stage, count):
                open_(layer, stage, 0)
                pe.wait_ge(sq_ready, count)
                for k in range(KB):
                    last = mm(bank(0), ones, sq_all[:, k, :], start=k == 0, stop=k == KB - 1)
                last.then_inc(ready[0], 1)

            def shifted(k, lo_=0, cols=T):
                off = (1 if k < KB else 0) + lo_
                return n[:, k % KB, off:off + cols]

            def z_block(layer, stage, b, k, ws, cols=P, m=P):
                open_(layer, stage, b, k)
                for kk in range(2 * KB):
                    last = mm(psum[0:m, b, :], ws[:, kk * cols:kk * cols + m], shifted(kk),
                              start=kk == 0, stop=kk == 2 * KB - 1)
                last.then_inc(ready[b], 1)
                return last

            def release(layer, section, k):
                return done(layer, section, k)

            pe.wait_ge(const_in, 16)
            with pe.Fori(0, L) as layer:
                norm_sums(layer, "norm1", layer * 2 + 1)
                pe.wait_ge(n_ready, layer * 3 + 1)
                for section, b, m, cols in (("wa", 4, P, P), ("zg", 5, P, P), ("mv1", 6, 32, 32)):
                    s, ws = take(layer, section, 0)
                    z_block(layer, "lora", b, 0, ws, cols, m)
                    pe.drain().then_inc(used[s], 1)

                with pe.Fori(0, KB) as m:
                    pe.wait_ge(lora_ready, layer * 4 + 4)
                    s, ws = take(layer, "rwkv", 0, m, 4)
                    for b, k in ((3, 0), (4, 1), (5, 2)):
                        open_(layer, "rwkv", b, m)
                        rows = 32 if b == 5 else P
                        src = mv_in[0:32] if b == 5 else wa_in
                        mm(bank(b), ws[0:rows, k * P:(k + 1) * P], src, start=True, stop=True).then_inc(ready[b], 1)
                    pe.drain().then_inc(used[s], 1)
                    q8 = layer * KB + m
                    for b, k in ((0, 1), (1, 2), (2, 3)):
                        s, ws = take(layer, "rwkv", k, m, 4)
                        z_block(layer, "rwkv", b, m, ws)
                        pe.drain().then_inc(used[s], 1)
                        if b == 1:
                            open_(layer, "rwkv", 6, m)
                            pe.wait_ge(sqk_ready, q8 + 1)
                            mm(bank(6), blk, tmp["sqk"], start=True, stop=True).then_inc(ready[6], 1)
                    open_(layer, "rwkv", 7, m)
                    pe.wait_ge(rk_ready, q8 + 1)
                    mm(bank(7), blk, tmp["rkt"], start=True, stop=True).then_inc(ready[7], 1)

                with pe.Fori(0, NC) as c:
                    pe.wait_ge(bd_zero, layer + 1)
                    qc = layer * NC + c
                    pe.wait_ge(bd_dve, qc + 1)
                    pe.wait_ge(bd_act, qc + 1)
                    pe.wait_ge(bd_pool, qc + 1)

                    def pairs(b0, k, per, terms, transpose=False):
                        for hf in HB:
                            b = b0 + hf
                            open_(layer, "scan", b, c * per + k)
                            for j in range(4):
                                pr = 4 * hf + j
                                for e, (l_, r_) in enumerate(terms):
                                    if transpose:
                                        last = nc.tensor.transpose(psum[:, b, j * P:(j + 1) * P], l_[:, pr, :], ident)
                                    else:
                                        last = mm(psum[:, b, j * P:(j + 1) * P], l_[:, pr, :], r_[:, pr, :],
                                                  start=e == 0, stop=e == len(terms) - 1)
                            last.then_inc(ready[b], 1)

                    pairs(0, 0, 7, [(bdb, bda)])
                    pairs(2, 0, 9, [(bda, bdb)])
                    pairs(4, 0, 7, [(bdb, None)], True)
                    pairs(6, 0, 3, [(bdb, bdr)])
                    pairs(2, 1, 9, [(bdk, None)], True)
                    pairs(4, 1, 7, [(bdk, bda)])
                    pairs(6, 1, 3, [(bdk, bdr)])
                    pairs(2, 2, 9, [(bdv, None)], True)
                    for lv in range(2, LEVELS + 1):
                        pe.wait_ge(loff_ready, qc * 5 + (lv - 1))
                        for hf in HB:
                            pe.wait_ge(x_ready, qc * 12 + ((lv - 2) * 2 + hf + 1))
                            b = hf
                            open_(layer, "scan", b, c * 7 + (lv - 1))
                            for j in range(4):
                                pr = 4 * hf + j
                                last = mm(psum[:, b, j * P:(j + 1) * P], loff[:, pr, :], xm[:, pr, :], start=True, stop=True)
                            last.then_inc(ready[b], 1)
                        for hf in HB:
                            pe.wait_ge(a1_ready, qc * 10 + ((lv - 2) * 2 + hf + 1))
                            for b, k, per, l_, r_ in ((2 + hf, lv + 1, 9, xt, a1), (4 + hf, lv, 7, a1, xt)):
                                if b >= 4 and lv == LEVELS:
                                    continue
                                open_(layer, "scan", b, c * per + k)
                                for j in range(4):
                                    pr = 4 * hf + j
                                    last = mm(psum[:, b, j * P:(j + 1) * P], l_[:, pr, :], r_[:, pr, :], start=True, stop=True)
                                last.then_inc(ready[b], 1)
                    pe.wait_ge(gram_ready, qc * 6 + 6)
                    pe.wait_ge(tr_ready, qc * 6 + 6)
                    pe.wait_ge(s_ready, layer * 18 + (c * 2 + 2))
                    pairs(6, 2, 3, [(bda, st), (gak, vt)])
                    pe.wait_ge(x_ready, qc * 12 + 12)
                    pe.wait_ge(rhs_ready, qc * 2 + 2)
                    pairs(0, 6, 7, [(xm, rhs)])
                    pe.wait_ge(u_ready, qc * 2 + 2)
                    pairs(2, 8, 9, [(st, bdr), (um, grb), (vt, grk)])
                    pairs(4, 6, 7, [(bt, um), (kt, vt)])

                for k, sem_, src in ((0, y_ready, fr), (1, ysq_ready, hsq)):
                    pe.wait_ge(sem_, layer + 1)
                    for m in range(KB):
                        open_(layer, "head", m, k)
                        mm(bank(m), blk, src[:, m, :], start=True, stop=True).then_inc(ready[m], 1)
                s, ws = take(layer, "g2", 0)
                for m in range(KB):
                    open_(layer, "head", m, 2)
                    last = mm(bank(m), ws[:, m * P:(m + 1) * P], zg_in, start=True, stop=True).then_inc(ready[m], 1)
                pe.drain().then_inc(used[s], 1)

                pe.wait_ge(n_ready, layer * 3 + 2)
                for hf in HB:
                    for tb in range(TB):
                        open_(layer, "gv", 4 * hf + tb)
                    for qt in range(4):
                        s, ws = take(layer, "gv", 4 * hf + qt)
                        for tb in range(TB):
                            for kk in range(4):
                                k = 4 * qt + kk
                                last = mm(bank(4 * hf + tb), shifted(k, tb * P, P), ws[:, kk * T:(kk + 1) * T],
                                          start=k == 0, stop=k == 2 * KB - 1)
                            if qt == 3:
                                last.then_inc(ready[4 * hf + tb], 1)
                        pe.drain().then_inc(used[s], 1)
                pe.wait_ge(ws_ready, layer + 1)
                for g in range(KB):
                    s, ws = take(layer, "zu", g)
                    z_block(layer, "zu", g % 2, g // 2, ws)
                    pe.drain().then_inc(used[s], 1)
                    if g == 0:
                        pe.wait_ge(gvn_ready, layer * TB + TB)
                    b = 2 + g % 2
                    open_(layer, "zu", b, g // 2)
                    for tb in range(TB):
                        last = mm(psum[:, b, tb * P:(tb + 1) * P], gv[:, tb, g * P:(g + 1) * P], wst[:, g, :],
                                  start=True, stop=True)
                    last.then_inc(ready[b], 1)

                with pe.Fori(0, KB // 2) as i:
                    pe.wait_ge(ya_ready, layer + 1)
                    pe.wait_ge(yb_ready, layer * KB + KB)
                    for e in range(2):
                        for k in range(2):
                            s, ws = take(layer, "mix", 3 * e + k, i, 6)
                            z_block(layer, "mix", 4 * e + k, i, ws)
                            pe.drain().then_inc(used[s], 1)
                        s, ws = take(layer, "mix", 3 * e + 2, i, 6)
                        for k, src in ((0, fr), (1, yb)):
                            b = 4 * e + 2 + k
                            open_(layer, "mix", b, i)
                            for kk in range(KB):
                                last = mm(bank(b), ws[:, (k * KB + kk) * P:(k * KB + kk + 1) * P], src[:, kk, :],
                                          start=kk == 0, stop=kk == KB - 1)
                            last.then_inc(ready[b], 1)
                        pe.drain().then_inc(used[s], 1)

                def two_blocks(stage, section, count, src, src_ready, value):
                    with pe.Fori(0, count // 4) as i:
                        pe.wait_ge(src_ready, value)
                        for e in range(2):
                            s, ws = take(layer, section, e, i, 2)
                            for o in range(2):
                                b = 2 * e + o
                                open_(layer, stage, b, i)
                                for kk in range(KB):
                                    last = mm(bank(b), ws[:, (o * KB + kk) * P:(o * KB + kk + 1) * P], src(kk),
                                              start=kk == 0, stop=kk == KB - 1)
                                last.then_inc(ready[b], 1)
                            pe.drain().then_inc(used[s], 1)

                two_blocks("wout", "wout", KB, lambda kk: merged[:, kk, :], merged_ready, layer * KB + KB)
                norm_sums(layer, "norm2", layer * 2 + 2)

                pe.wait_ge(pt_in, layer * 16 + 16)
                s, ws = take(layer, "plew", 0)
                for m in range(KB):
                    open_(layer, "plew", m)
                    for kk in range(2):
                        last = mm(bank(m), ws[:, kk * D + m * P:kk * D + (m + 1) * P], ptb[:, kk, :],
                                  start=kk == 0, stop=kk == 1)
                    last.then_inc(ready[m], 1)
                pe.drain().then_inc(used[s], 1)
                two_blocks("pleg", "pleg", KB, lambda kk: n[:, kk, 1:NW], n_ready, layer * 3 + 3)
                two_blocks("wq", "wq", 2 * HEADS, lambda kk: n[:, kk, 1:NW], n_ready, layer * 3 + 3)
                pe.wait_ge(q_ready, layer * 16 + 16)
                s, ws = take(layer, "keys", 0)
                for tb in range(TB):
                    for e in range(4):
                        open_(layer, "keys", 4 + e, tb)
                        for j in range(4):
                            hp = 4 * e + j
                            last = mm(psum[:, 4 + e, j * P:(j + 1) * P], q[:, hp, tb * P:(tb + 1) * P],
                                      ws[:, hp * P:(hp + 1) * P], start=True, stop=True)
                        last.then_inc(ready[4 + e], 1)
                pe.drain().then_inc(used[s], 1)

                def up(stage, section, k, i, per_bank, per):
                    s, ws = take(layer, section, k, i, per)
                    for o in range(2):
                        open_(layer, stage, o, i * per_bank + k)
                        for kk in range(KB):
                            last = mm(bank(o), ws[:, (o * KB + kk) * P:(o * KB + kk + 1) * P], n[:, kk, 1:NW],
                                      start=kk == 0, stop=kk == KB - 1)
                        last.then_inc(ready[o], 1)
                    pe.drain().then_inc(used[s], 1)

                with pe.Fori(0, JG // 4) as i:
                    for k in range(2):
                        up("h0", "u0", k, i, 2, 2)
                pe.wait_ge(picks_ready, layer * TB + TB)
                for a in range(3):
                    open_(layer, "idx", 4 + a)
                    for tb in range(TB):
                        last = nc.tensor.transpose(psum[:, 4 + a, tb * P:(tb + 1) * P], picks[:, a, tb * P:(tb + 1) * P], ident)
                    last.then_inc(ready[4 + a], 1)

                for g in range(NG):
                    with pe.Fori(0, T // TG // 4) as i:
                        for e in range(4):
                            b = 6 + e % 2
                            open_(layer, f"build{g}", b, i * 2 + e // 2)
                            for t4 in range(4):
                                pe.wait_ge(hot_ready, layer * (NG * 128) + (i * 16 + (g * 128 + e * 4 + t4 + 1)))
                                for j in range(4):
                                    tk = 4 * t4 + j
                                    last = mm(psum[:, b, tk * JG:(tk + 1) * JG], aring[:, tk, :], bring[:, tk, :],
                                              start=True, stop=True)
                                if t4 < 3:
                                    last.then_inc(hot_used, 1)
                            last.then_inc(ready[b], 1)
                            pe.drain().then_inc(hot_used, 1)
                            if g + 1 < NG and e % 2 == 0:
                                up(f"build{g}", f"u{g + 1}", e // 2, i, 2, 2)
                    src = gbuf[g % 2]
                    with pe.Fori(0, KB // 2) as i:
                        pe.wait_ge(gated, layer * (NG * 32) + (g + 1) * 32)
                        for e in range(2):
                            b = 2 + e
                            open_(layer, f"down{g}", b, i)
                            for hv in range(2):
                                s, ws = take(layer, f"v{g}", 2 * e + hv, i, 4)
                                for jj in range(JG // 2):
                                    j = hv * (JG // 2) + jj
                                    last = mm(bank(b), ws[:, jj * P:(jj + 1) * P], src[:, j, :],
                                              start=j == 0, stop=j == JG - 1)
                                if hv == 1:
                                    last.then_inc(ready[b], 1)
                                pe.drain().then_inc(used[s], 1)
            norm_sums(L, "norm1", 2 * L + 1)

        @block.vector
        def _(dve):
            V = nc.vector
            sync = dve.drain

            def norm(layer, stage, count, scale):
                dve.wait_ge(ready[0], use(layer, stage, 0))
                V.tensor_scalar(rstd, bank(0), 1.0 / D, RMS_EPS, ALU.mult, ALU.add).then_inc(free[0], 1)
                dve.wait_ge(rms_ready, count)
                V.reciprocal(rstd, rstd)
                sync()
                scaled(scale)

            def scaled(scale):
                V.memset(n[:, :, 0:1], 0.0)
                for k in range(KB):
                    last = V.scalar_tensor_tensor(n[:, k, 1:NW], h[:, k, :], vcol(scale, k), rstd, ALU.mult, ALU.mult)
                last.then_inc(n_ready, 1)

            dve.wait_ge(x_in, 16)
            dve.wait_ge(const_in, 16)
            dve.sem_inc(fields_ready, 1)
            dve.sem_inc(hot_used, 4)
            dve.sem_inc(pg_used, 2)
            V.drain().then_inc(layer_free, 1)
            with dve.Fori(0, L) as layer:
                dve.wait_ge(vec_in, layer * 16 + 16)
                norm(layer, "norm1", layer * 2 + 1, "norm_mix")

                with dve.Fori(0, KB) as m:
                    q8 = layer * KB + m

                    def got(b):
                        dve.wait_ge(ready[b], use(layer, "rwkv", b, m))

                    t_ = tmp
                    dve.wait_ge(free[5], use(layer, "rwkv", 5, m + 1))
                    V.tensor_tensor_scan(t_["s"], cc("reset"), t_["sg"], 0.0, ALU.mult, ALU.add)
                    sync()
                    V.tensor_tensor(t_["se"], t_["s"], t_["sg"], ALU.subtract).then_inc(cum_ready, 1)
                    V.tensor_scalar(t_["t"], t_["ar"], -1.0, vcol("ka", m), ALU.add, ALU.mult)
                    got(0)
                    V.tensor_scalar(t_["kkr"], bank(0), vcol("kk", m), None, ALU.mult).then_inc(kkr_ready, 1)
                    sync()
                    V.scalar_tensor_tensor(t_["k"], t_["t"], 1.0, bank(0), ALU.add, ALU.mult).then_inc(free[0], 1)
                    got(1)
                    V.tensor_copy(t_["zv"], bank(1)).then_inc(free[1], 1)
                    got(6)
                    V.tensor_scalar(t_["rn"], bank(6), 1e-24, None, ALU.max).then_inc(free[6], 1)
                    dve.wait_ge(rn_ready, q8 + 1)
                    V.reciprocal(t_["rn"], t_["rn"])
                    sync()
                    V.tensor_tensor(t_["kkr"], t_["kkr"], t_["rn"], ALU.mult)
                    sync()
                    dve.wait_ge(p_ready, q8 + 1)
                    V.scalar_tensor_tensor(fa[:, ds(m, 1), :], t_["kkr"], -1.0, t_["pexc"], ALU.mult, ALU.mult)
                    V.tensor_tensor(t_["b"], t_["kkr"], t_["ar"], ALU.mult)
                    V.tensor_tensor(fk[:, ds(m, 1), :], t_["k"], t_["pinv"], ALU.mult)
                    sync()
                    V.tensor_tensor(fb[:, ds(m, 1), :], t_["b"], t_["pinv"], ALU.mult)
                    got(2)
                    V.scalar_tensor_tensor(t_["rkt"], bank(2), vcol("rk", m), t_["k"], ALU.mult, ALU.mult).then_inc(rk_ready, 1)
                    V.tensor_tensor(fr[:, ds(m, 1), :], bank(2), t_["pinc"], ALU.mult).then_inc(free[2], 1)
                    dve.wait_ge(vf_in, q8 * 16 + 16)
                    V.tensor_tensor(t_["vf"], t_["vf"], t_["zv"], ALU.subtract)
                    sync()
                    V.tensor_tensor(t_["vf"], t_["vf"], t_["vm"], ALU.mult)
                    sync()
                    V.tensor_tensor(fv[:, ds(m, 1), :], t_["zv"], t_["vf"], ALU.add)
                    sync()
                    got(7)
                    V.tensor_tensor(fbon[:, ds(m, 1), :], bank(7), fv[:, ds(m, 1), :], ALU.mult).then_inc(free[7], 1)
                    V.tensor_copy(pend[:, ds(m, 1), :], t_["pinc"].rearrange("p (c t) -> p c t", t=CH)[:, :, CH - 1:CH].rearrange("p c o -> p o c"))
                    V.drain().then_inc(fields_ready, 1)

                dve.wait_ge(ready[7], use(layer, "rwkv", 7, KB - 1))
                for t_ in (bda, bdr, bdb, bdk, bdv):
                    V.memset(t_, 0.0)
                V.drain().then_inc(bd_zero, 1)
                for hf in HB:
                    V.memset(half(st, hf), 0.0).then_inc(s_ready, 1)
                with dve.Fori(0, NC) as c:
                    qc = layer * NC + c

                    def got(b, k, per):
                        dve.wait_ge(ready[b], use(layer, "scan", b, c * per + k))

                    def wide(name, i=0, width=None):
                        m_ = cc(name, i, width)
                        return m_.rearrange("p (o c) -> p o c", o=1).broadcast_to([P, 4, P])

                    dve.wait_ge(ready[5], use(layer, "scan", 5, c * 7 - 1))
                    for src, dst in ((fa, bda), (fb, bdb)):
                        for e in range(2):
                            r = slice(e * CH, (e + 1) * CH)
                            last = V.tensor_copy(dst[r, :, e * CH:(e + 1) * CH], src[r, :, ts(c, CH)])
                    last.then_inc(bd_dve, 1)
                    for hf in HB:
                        got(6 + hf, 0, 3)
                        V.tensor_tensor(half(grb, hf), bank4(6 + hf), wide("upd"), ALU.mult).then_inc(gram_ready, 1)
                        V.drain().then_inc(free[6 + hf], 1)
                    for hf in HB:
                        got(hf, 0, 7)
                        V.tensor_tensor(half(xm, hf), bank4(hf), wide("lvlN"), ALU.mult).then_inc(free[hf], 1)
                    sync()
                    for hf in HB:
                        V.tensor_tensor(half(xm, hf), half(xm, hf), wide("ident"), ALU.add)
                    for b0, k, per, dst, mask in ((4, 1, 7, gak, "up"), (6, 1, 3, grk, "upd")):
                        for hf in HB:
                            got(b0 + hf, k, per)
                            V.tensor_tensor(half(dst, hf), bank4(b0 + hf), wide(mask), ALU.mult).then_inc(gram_ready, 1)
                            V.drain().then_inc(free[b0 + hf], 1)
                    dve.wait_ge(l_ready, qc * 2 + 2)
                    got(3, 1, 9)
                    for hf in HB:
                        V.tensor_tensor(half(xt, hf), half(lt, hf), wide("lvl", 0, P), ALU.mult)
                    sync()
                    for hf in HB:
                        V.tensor_tensor(half(xt, hf), half(xt, hf), wide("ident"), ALU.add).then_inc(x_ready, 1)
                    for lv in range(2, LEVELS + 1):
                        for hf in HB:
                            got(2 + hf, lv + 1, 9)
                            if lv < LEVELS:
                                got(4 + hf, lv, 7)
                            up_x = V.tensor_tensor(half(xm, hf), half(xm, hf), bank4(2 + hf), ALU.add)
                            up_x.then_inc(free[2 + hf], 1)
                            if lv < LEVELS:
                                V.tensor_tensor(half(xt, hf), half(xt, hf), bank4(4 + hf), ALU.add).then_inc(free[4 + hf], 1)
                            V.drain().then_inc(x_ready, 1)
                    for hf in HB:
                        got(2 + hf, 8, 9)
                        for e in range(2):
                            r = slice(e * CH, (e + 1) * CH)
                            last = V.tensor_copy(fr[r, 4 * hf:4 * hf + 4, ts(c, CH)], bank4(2 + hf)[r, :, e * CH:(e + 1) * CH])
                        last.then_inc(free[2 + hf], 1)
                    for hf in HB:
                        got(4 + hf, 6, 7)
                        V.tensor_tensor(half(st, hf), half(st, hf), bank4(4 + hf), ALU.add).then_inc(free[4 + hf], 1)
                    sync()
                    for hf in HB:
                        V.tensor_tensor(half(st, hf), half(st, hf), pend[:, 4 * hf:4 * hf + 4, ds(c, 1)].broadcast_to([P, 4, P]),
                                        ALU.mult).then_inc(s_ready, 1)

                V.drain().then_inc(y_ready, 1)
                for b in range(8):
                    dve.wait_ge(ready[b], use(layer, "head", b, 0))
                for b in range(8):
                    V.scalar_tensor_tensor(yc[:, b, :], bank(b), -1.0 / CH, fr[:, b, :], ALU.mult, ALU.add).then_inc(free[b], 1)
                V.drain().then_inc(yc_ready, 1)
                for b in range(8):
                    dve.wait_ge(ready[b], use(layer, "head", b, 1))
                    V.tensor_scalar(fk[:, b, :], bank(b), 1.0 / CH, RW_EPS, ALU.mult, ALU.add).then_inc(free[b], 1)
                V.drain().then_inc(yvar_ready, 1)
                dve.wait_ge(ysd_ready, layer + 1)
                V.reciprocal(fk, fk)
                sync()
                V.tensor_tensor(yc, yc, fk, ALU.mult)
                sync()
                for b in range(8):
                    V.tensor_scalar(yc[:, b, :], yc[:, b, :], vcol("ln_g", b), vcol("ln_b", b), ALU.mult, ALU.add)
                sync()
                V.tensor_tensor(yc, yc, fbon, ALU.add)
                sync()
                for b in range(8):
                    dve.wait_ge(ready[b], use(layer, "head", b, 2))
                    V.tensor_tensor(fr[:, b, :], yc[:, b, :], bank(b), ALU.mult).then_inc(free[b], 1)
                V.drain().then_inc(ya_ready, 1)
                scaled("norm_mix")

                for tb in range(TB):
                    dve.wait_ge(gelu_v, layer * 8 + (5 + tb))
                    for hf in HB:
                        V.bn_stats(stats[:, tb, hf, :], gv[:, tb, hf * T:(hf + 1) * T])
                    sync()
                    V.bn_aggr(mv2[:, tb, :], stats[:, tb, :, :])
                    sync()
                    last = V.tensor_scalar(lrs[:, tb:tb + 1], mv2[:, tb, 1:2], GM_EPS, None, ALU.add)
                last.then_inc(gvar_ready, 1)
                dve.wait_ge(gsd_ready, layer + 1)
                dve.wait_ge(gm_in, layer * 16 + 16)
                V.reciprocal(lrs, lrs)
                sync()
                for tb in range(TB):
                    V.scalar_tensor_tensor(gv[:, tb, :], gv[:, tb, :], mv2[:, tb, 0:1], lng, ALU.subtract, ALU.mult)
                sync()
                for tb in range(TB):
                    V.scalar_tensor_tensor(gv[:, tb, :], gv[:, tb, :], lrs[:, tb:tb + 1], lnb, ALU.mult, ALU.add).then_inc(gvn_ready, 1)
                for g in range(KB):
                    b = 2 + g % 2
                    dve.wait_ge(ready[b], use(layer, "zu", b, g // 2))
                    V.tensor_tensor(spt[:, g % 2, :].rearrange("p (b t) -> p b t", b=TB), bank4(b),
                                    bsb[:, g:g + 1, :].broadcast_to([P, TB, P]), ALU.add).then_inc(free[b], 1)
                    sync()
                    dve.wait_ge(ug_ready, layer * KB + (g + 1))
                    V.tensor_tensor(yb[:, g, :], spt[:, g % 2, :], ut[:, g % 2, :], ALU.mult).then_inc(yb_ready, 1)

                with dve.Fori(0, KB // 2) as i:
                    for e in range(2):
                        sync()
                        dve.wait_ge(gate_ready, layer * (2 * KB) + (i * 4 + (2 * e + 2)))
                        for k in range(2):
                            b = 4 * e + 2 + k
                            dve.wait_ge(ready[b], use(layer, "mix", b, i))
                            V.tensor_tensor(mixed[:, 2 * e + k, :], gates[:, 2 * e + k, :], bank(b), ALU.mult).then_inc(free[b], 1)
                        sync()
                        V.tensor_tensor(merged[:, ds(i * 2 + e, 1), :], mixed[:, 2 * e, :], mixed[:, 2 * e + 1, :], ALU.add).then_inc(merged_ready, 1)

                with dve.Fori(0, 2) as i:
                    for b in range(4):
                        dve.wait_ge(ready[b], use(layer, "wout", b, i))
                        hm = h[:, ds(i * 4 + b, 1), :]
                        V.tensor_tensor(hm, hm, bank(b), ALU.add).then_inc(free[b], 1)
                V.drain().then_inc(layer_free, 1)
                norm(layer, "norm2", layer * 2 + 2, "norm_ffn")

                with dve.Fori(0, 2) as i:
                    dve.wait_ge(pp_ready, layer + 1)
                    for b in range(4):
                        dve.wait_ge(pg_ready, layer * KB + (i * 4 + (b + 1)))
                        V.tensor_tensor(pmul[:, b % 2, :], pgb[:, b % 2, :], ppb[:, ds(i * 4 + b, 1), :], ALU.mult).then_inc(pg_used, 1)
                        sync()
                        hm = h[:, ds(i * 4 + b, 1), :]
                        V.tensor_tensor(hm, hm, pmul[:, b % 2, :], ALU.add)
                        sync()

                def top16(rows, wide_, spare, vals, inds, width):
                    for rnd in range(2):
                        src = spare if rnd else wide_
                        r8 = slice(8 * rnd, 8 * rnd + 8)
                        for a in range(rows):
                            V.max(vals[:, a, r8], src[:, a * width:(a + 1) * width])
                        sync()
                        for a in range(rows):
                            V.max_index(inds[:, a, r8], vals[:, a, r8], src[:, a * width:(a + 1) * width])
                            if rnd == 0:
                                V.match_replace(spare[:, a * width:(a + 1) * width], vals[:, a, r8],
                                                src[:, a * width:(a + 1) * width], LOWEST)
                        sync()

                with dve.Fori(0, TB) as tb:
                    dve.wait_ge(sc_ready, layer * 16 + 16)
                    V.tensor_copy(sw.rearrange("p a b -> p (a b)"), sc[:, ds(tb, 1), :].rearrange("p o b -> p (o b)"))
                    sync()
                    flat = lambda t__: t__.rearrange("p a b -> p (a b)")
                    top16(NH, flat(sw), flat(sx), tv, ti.bitcast(U32), P)
                    V.tensor_copy(flat(tif), flat(ti).bitcast(U32))
                    pair = tv.rearrange("p (h c) k -> p h c k", c=2)
                    V.tensor_tensor(flat(cand).rearrange("p (h a b) -> p h a b", h=HEADS, a=TOPK),
                                    pair[:, :, 0, :].rearrange("p h (k o) -> p h k o", o=1).broadcast_to([P, HEADS, TOPK, TOPK]),
                                    pair[:, :, 1, :].rearrange("p h (o k) -> p h o k", o=1).broadcast_to([P, HEADS, TOPK, TOPK]), ALU.add)
                    sync()
                    top16(HEADS, flat(cand), flat(cand2), bv, bp.bitcast(U32), TOPK * TOPK)
                    pw = pick[:, 2, :].rearrange("p (h k) -> p h k", h=HEADS)
                    V.tensor_tensor(pw, bv, bv[:, :, 0:1].broadcast_to([P, HEADS, TOPK]), ALU.subtract)
                    V.drain().then_inc(ex_in, 1)
                    V.tensor_scalar(bq[:, 0, :].bitcast(U32), flat(bp).bitcast(U32), 4, None, ALU.logical_shift_right)
                    V.tensor_scalar(bq[:, 1, :].bitcast(U32), flat(bp).bitcast(U32), 15, None, ALU.bitwise_and)
                    sync()
                    V.tensor_copy(flat(bqf), flat(bq).bitcast(U32))
                    sync()
                    tpair = tif.rearrange("p (h c) k -> p h c k", c=2)
                    NHK = HEADS * TOPK
                    for cpt in range(2):
                        e3 = flat(eq).rearrange("p (a b) -> p a b", a=NHK)
                        V.tensor_tensor(e3, bqf[:, cpt, :].rearrange("p (a o) -> p a o", o=1).broadcast_to([P, NHK, TOPK]),
                                        cc("iota")[:, 0:TOPK].rearrange("p (o a) -> p o a", o=1).broadcast_to([P, NHK, TOPK]), ALU.is_equal)
                        sync()
                        e4 = flat(eq).rearrange("p (h a b) -> p h a b", h=HEADS, a=TOPK)
                        V.tensor_tensor(e4, e4, tpair[:, :, cpt, :].rearrange("p h (o k) -> p h o k", o=1).broadcast_to([P, HEADS, TOPK, TOPK]), ALU.mult)
                        sync()
                        V.tensor_reduce(pick[:, cpt, :], e3, AXX, ALU.add)
                        sync()
                    dve.wait_ge(ex_out, layer * TB + tb + 1)
                    V.tensor_reduce(hsum, pw, AXX, ALU.add)
                    sync()
                    V.reciprocal(hrec, hsum)
                    sync()
                    V.tensor_tensor(pw, pw, hrec.rearrange("p (h o) -> p h o", o=1).broadcast_to([P, HEADS, TOPK]), ALU.mult)
                    sync()
                    V.tensor_copy(picks[:, :, ts(tb, P)], pick).then_inc(picks_ready, 1)
                    sync()
                for a in range(3):
                    dve.wait_ge(ready[4 + a], use(layer, "idx", 4 + a))
                    V.tensor_copy(idx[:, a, :], bank(4 + a)).then_inc(free[4 + a], 1)
                sync()
                for g in range(NG):
                    with dve.Fori(0, T // TG // 4) as i:
                        for e in range(4):
                            for t4 in range(4):
                                hot = layer * (NG * 128) + (i * 16 + (g * 128 + e * 4 + t4 + 1))
                                dve.wait_ge(hot_used, hot)
                                for j in range(4):
                                    tk = 4 * t4 + j
                                    at = i * (4 * TG) + (e * TG + tk)
                                    V.tensor_scalar(aring[:, tk, :], cc("iota"), idx[:, 0, ds(at, 1)], None, ALU.is_equal)
                                    last = V.tensor_scalar(bring[:, tk, :], cc("iota")[:, g * JG:(g + 1) * JG], idx[:, 1, ds(at, 1)],
                                                           idx[:, 2, ds(at, 1)], ALU.is_equal, ALU.mult)
                                last.then_inc(hot_ready, 1)
                            b = 6 + e % 2
                            dve.wait_ge(act_ready, layer * P + (g + 1) * JG)
                            dve.wait_ge(ready[b], use(layer, f"build{g}", b, i * 2 + e // 2))
                            part = gbuf[g % 2][:, :, ds(i * (4 * TG) + e * TG, TG)]
                            V.tensor_tensor(part, part, bank(b).rearrange("p (t j) -> p j t", j=JG), ALU.mult).then_inc(free[b], 1)
                            V.drain().then_inc(gated, 1)
                    with dve.Fori(0, KB // 2) as i:
                        for e in range(2):
                            b = 2 + e
                            dve.wait_ge(ready[b], use(layer, f"down{g}", b, i))
                            hm = h[:, ds(i * 2 + e, 1), :]
                            V.tensor_tensor(hm, hm, bank(b), ALU.add).then_inc(free[b], 1)
                    sync()
                V.drain().then_inc(layer_free, 1)
            norm(L, "norm1", 2 * L + 1, "final")

        @block.scalar
        def _(act):
            A = nc.scalar.activation
            sync = act.drain

            def squares(count, layer, stage):
                act.wait_ge(layer_free, count)
                A(sq_all, h, ACT.Square).then_inc(sq_ready, 1)
                act.wait_ge(free[0], use(layer, stage, 0, 1))
                A(rstd, rstd, ACT.Sqrt).then_inc(rms_ready, 1)

            act.wait_ge(x_in, 16)
            with act.Fori(0, L) as layer:
                act.wait_ge(layer_free, layer * 2 + 1)
                act.dma_start(vecs, vec[ds(act.snap(layer), 1), :, :]).then_inc(vec_in, 16)
                squares(layer * 2 + 1, layer, "norm1")
                act.wait_ge(vec_in, layer * 16 + 16)
                act.wait_ge(ready[4], use(layer, "lora", 4))
                A(wa_in[0:CH], psum[0:CH, 4, :], ACT.Tanh).then_inc(lora_ready, 1)
                A(wa_in[CH:P], psum[CH:P, 4, :], ACT.Copy).then_inc(free[4], 1)
                act.wait_ge(ready[5], use(layer, "lora", 5))
                A(zg_in, bank(5), ACT.Sigmoid).then_inc(free[5], 1)
                act.wait_ge(ready[6], use(layer, "lora", 6))
                A(mv_in[0:32], psum[0:32, 6, :], ACT.Copy).then_inc(free[6], 1)
                act.drain().then_inc(lora_ready, 3)

                with act.Fori(0, KB) as m:
                    q8 = layer * KB + m
                    act.wait_ge(fields_ready, q8 + 1)
                    for b, dst, bias in ((3, "sg", "w0"), (4, "ar", "a0"), (5, "vm", "v0")):
                        act.wait_ge(ready[b], use(layer, "rwkv", b, m))
                        A(tmp[dst], bank(b), ACT.Sigmoid, bias=vcol(bias, m)).then_inc(free[b], 1)
                    act.wait_ge(cum_ready, q8 + 1)
                    A(tmp["pinc"], tmp["s"], ACT.Exp, scale=-DECAY)
                    A(tmp["pinv"], tmp["s"], ACT.Exp, scale=DECAY)
                    A(tmp["pexc"], tmp["se"], ACT.Exp, scale=-DECAY).then_inc(p_ready, 1)
                    act.wait_ge(kkr_ready, q8 + 1)
                    A(tmp["sqk"], tmp["kkr"], ACT.Square).then_inc(sqk_ready, 1)
                    act.wait_ge(free[6], use(layer, "rwkv", 6, m + 1))
                    A(tmp["rn"], tmp["rn"], ACT.Sqrt).then_inc(rn_ready, 1)

                act.wait_ge(fields_ready, layer * KB + (KB + 1))
                act.wait_ge(bd_zero, layer + 1)
                with act.Fori(0, NC) as c:
                    qc = layer * NC + c

                    def got(b, k, per):
                        act.wait_ge(ready[b], use(layer, "scan", b, c * per + k))

                    act.wait_ge(ready[5], use(layer, "scan", 5, c * 7 - 1))
                    for src, dst in ((fk, bdk), (fr, bdr)):
                        for e in range(2):
                            r = slice(e * CH, (e + 1) * CH)
                            last = A(dst[r, :, e * CH:(e + 1) * CH], src[r, :, ts(c, CH)], ACT.Copy)
                    last.then_inc(bd_act, 1)
                    for hf in HB:
                        got(2 + hf, 0, 9)
                        A(half(lt, hf), bank4(2 + hf), ACT.Copy).then_inc(free[2 + hf], 1)
                    act.drain().then_inc(l_ready, 2)
                    for b0, k, per, dst in ((4, 0, 7, bt), (2, 1, 9, kt), (2, 2, 9, vt)):
                        for hf in HB:
                            got(b0 + hf, k, per)
                            A(half(dst, hf), bank4(b0 + hf), ACT.Copy).then_inc(free[b0 + hf], 1)
                    act.drain().then_inc(tr_ready, 6)
                    for lv in range(2, LEVELS + 1):
                        for hf in HB:
                            got(hf, lv - 1, 7)
                            A(half(a1, hf), bank4(hf), ACT.Copy).then_inc(free[hf], 1)
                            act.drain().then_inc(a1_ready, 1)
                    for b0, k, per, dst, s_ in ((6, 2, 3, rhs, rhs_ready), (0, 6, 7, um, u_ready)):
                        for hf in HB:
                            got(b0 + hf, k, per)
                            A(half(dst, hf), bank4(b0 + hf), ACT.Copy).then_inc(free[b0 + hf], 1)
                        act.drain().then_inc(s_, 2)

                act.wait_ge(yc_ready, layer + 1)
                A(hsq, yc, ACT.Square).then_inc(ysq_ready, 1)
                act.wait_ge(yvar_ready, layer + 1)
                A(fk, fk, ACT.Sqrt).then_inc(ysd_ready, 1)
                for b in range(8):
                    act.wait_ge(ready[b], use(layer, "head", b, 1))
                act.dma_start(gmp, gm[ds(act.snap(layer), 1), :, :]).then_inc(gm_in, 16)
                act.wait_ge(ya_ready, layer + 1)
                for hf in HB:
                    for tb in range(TB):
                        b = 4 * hf + tb
                        act.wait_ge(ready[b], use(layer, "gv", b))
                        A(gv[:, tb, hf * T:(hf + 1) * T], bank(b), ACT.Gelu_apprx_tanh).then_inc(free[b], 1)
                        act.drain().then_inc(gelu_v, 1)
                act.wait_ge(gvar_ready, layer + 1)
                A(lrs, lrs, ACT.Sqrt).then_inc(gsd_ready, 1)
                for g in range(KB):
                    b = g % 2
                    act.wait_ge(ready[b], use(layer, "zu", b, g // 2))
                    if g >= 2:
                        act.wait_ge(yb_ready, layer * KB + (g - 1))
                    A(ut[:, b, :], bank(b), ACT.Gelu_apprx_tanh).then_inc(free[b], 1)
                    act.drain().then_inc(ug_ready, 1)
                act.wait_ge(yb_ready, layer * KB + KB)
                with act.Fori(0, KB // 2) as i:
                    for e in range(2):
                        for k in range(2):
                            b = 4 * e + k
                            act.wait_ge(ready[b], use(layer, "mix", b, i))
                            act.wait_ge(free[4 * e + 2 + k], use(layer, "mix", 4 * e + 2 + k, i))
                            A(gates[:, 2 * e + k, :], bank(b), ACT.Sigmoid).then_inc(free[b], 1)
                            act.drain().then_inc(gate_ready, 1)
                squares(layer * 2 + 2, layer, "norm2")
                act.dma_start(ptb, pt[ds(act.snap(layer), 1), :, :].rearrange("o p (k t) -> (o p) k t", k=2)).then_inc(pt_in, 16)
                for b in range(8):
                    act.wait_ge(ready[b], use(layer, "plew", b))
                    A(ppb[:, b, :], bank(b), ACT.Copy).then_inc(free[b], 1)
                act.drain().then_inc(pp_ready, 1)
                with act.Fori(0, 2) as i:
                    for b in range(4):
                        act.wait_ge(ready[b], use(layer, "pleg", b, i))
                        act.wait_ge(pg_used, layer * 8 + (i * 4 + (b + 1)))
                        A(pgb[:, b % 2, :], bank(b), ACT.Sigmoid).then_inc(free[b], 1)
                        act.drain().then_inc(pg_ready, 1)
                with act.Fori(0, 4) as i:
                    for b in range(4):
                        act.wait_ge(ready[b], use(layer, "wq", b, i))
                        A(q[:, ds(i * 4 + b, 1), :], bank(b), ACT.Copy).then_inc(free[b], 1)
                act.drain().then_inc(q_ready, 16)
                for tb in range(TB):
                    for e in range(4):
                        act.wait_ge(ready[4 + e], use(layer, "keys", 4 + e, tb))
                        A(sc[:, tb, e * T:(e + 1) * T], bank(4 + e), ACT.Copy).then_inc(free[4 + e], 1)
                act.drain().then_inc(sc_ready, 16)

                def expert(stage, g, k, i, per_bank, buf):
                    for o in range(2):
                        act.wait_ge(ready[o], use(layer, stage, o, i * per_bank + k))
                        A(buf[:, ds(i * (2 * per_bank) + (2 * k + o), 1), :], bank(o), ACT.Gelu_apprx_tanh).then_inc(free[o], 1)

                act.wait_ge(pg_used, layer * 8 + 10)
                with act.Fori(0, TB) as tb:
                    for e in range(JG // 4 // TB):
                        for k in range(2):
                            expert("h0", 0, k, tb * (JG // 4 // TB) + e, 2, gbuf[0])
                    act.wait_ge(ex_in, layer * TB + tb + 1)
                    A(pick[:, 2, :], pick[:, 2, :], ACT.Exp).then_inc(ex_out, 1)
                act.drain().then_inc(act_ready, JG)
                for g in range(NG - 1):
                    if g == 0:
                        act.wait_ge(free[6], use(layer, "idx", 6, 1))
                    with act.Fori(0, JG // 4) as i:
                        for k in range(2):
                            expert(f"build{g}", g + 1, k, i, 2, gbuf[(g + 1) % 2])
                    act.drain().then_inc(act_ready, JG)
            squares(2 * L + 1, L, "norm1")

        @block.gpsimd
        def _(pool):
            G = nc.gpsimd
            pool.wait_ge(const_in, 16)
            with pool.Fori(0, L) as layer:
                with pool.Fori(0, KB) as m:
                    q8 = layer * KB + m
                    dst = vfirst[ds(pool.snap(q8), 1), :, :]
                    src = vfirst[ds(pool.snap(m), 1), :, :]
                    pool.wait_ge(free[1], use(layer, "rwkv", 1, m + 1))
                    pool.dma_start(dst, tmp["zv"]).then_inc(vf_out, 16)
                    pool.wait_ge(vf_out, q8 * 16 + 16)
                    pool.dma_start(tmp["vf"], src).then_inc(vf_in, 16)
                with pool.Fori(0, NC) as c:
                    qc = layer * NC + c
                    pool.wait_ge(bd_zero, layer + 1)
                    pool.wait_ge(ready[5], use(layer, "scan", 5, c * 7 - 1))
                    for e in range(2):
                        r = slice(e * CH, (e + 1) * CH)
                        last = G.tensor_copy(bdv[r, :, e * CH:(e + 1) * CH], fv[r, :, ts(c, CH)])
                    last.then_inc(bd_pool, 1)
                    pool.wait_ge(l_ready, qc * 2 + 2)
                    pool.wait_ge(ready[3], use(layer, "scan", 3, c * 9 + 2))
                    for lv in range(2, LEVELS + 1):
                        if lv > 2:
                            pool.wait_ge(ready[1], use(layer, "scan", 1, c * 7 + (lv - 2)))
                        mask = cc("lvl", lv - 1, P).rearrange("p (o c) -> p o c", o=1).broadcast_to([P, KB, P])
                        G.tensor_tensor(loff, lt, mask, ALU.mult).then_inc(loff_ready, 1)
                pool.wait_ge(gm_in, layer * 16 + 16)
                G.tensor_tensor(wst, wst, cc("causal").rearrange("p (o c) -> p o c", o=1).broadcast_to([P, KB, P]),
                                ALU.mult).then_inc(ws_ready, 1)


def pack(inputs):
    g = {k: np.ascontiguousarray(a) for k, a in inputs.items()}

    def blocks(a, cols=P):
        k, m = a.shape
        return a.reshape(k // P, P, m // cols, cols).transpose(2, 1, 0, 3)

    def pad(a, cols=SLOT):
        a = a.reshape(a.shape[0], P, -1)
        if a.shape[2] == cols:
            return a
        return np.concatenate([a, np.zeros((a.shape[0], P, cols - a.shape[2]), a.dtype)], axis=2)

    W = 1024
    w_all, lo_all, u_all, v_all, gm_all, vec_all, pt_all = [], [], [], [], [], [], []
    for i in range(L):
        m0 = max(i - 1, 0)
        z = g["w_in"][i]
        c = np.cumsum([0, W, W, W, 64, 64, 128, W, W, W, W])
        zr, zk, zv = (z[:, c[j]:c[j + 1]] for j in range(3))
        part = {
            "wa": pad(blocks(z[:, c[3]:c[5]])), "zg": pad(blocks(z[:, c[5]:c[6]])),
            "mv1": pad(blocks(g["rw_mv_w1"][m0], 32)),
            "rwkv": np.stack([blocks(zk), blocks(zv), blocks(zr)], axis=1).reshape(3 * KB, P, SLOT),
            "g2": pad(g["rw_g2"][i][None]),
        }
        zgv = z[:, c[7]:c[8]].reshape(4, 4, P, 2, T)
        part["gv"] = zgv.transpose(3, 0, 2, 1, 4).reshape(8, P, SLOT)
        part["zu"] = pad(blocks(z[:, c[6]:c[7]]))
        proj = np.concatenate([blocks(g["w_proj_a"][i]), blocks(g["w_proj_b"][i])], axis=2)
        part["mix"] = np.stack([pad(blocks(z[:, c[8]:c[9]])), pad(blocks(z[:, c[9]:c[10]])),
                                proj.reshape(KB, P, SLOT)], axis=1).reshape(3 * KB, P, SLOT)

        def twos(a):
            b = blocks(a)
            return b.reshape(b.shape[0] // 2, 2, P, -1).transpose(0, 2, 1, 3).reshape(-1, P, SLOT)

        part["wout"] = twos(g["w_out"][i])
        part["plew"] = g["ple_w"][i].reshape(2, P, D).transpose(1, 0, 2).reshape(1, P, SLOT)
        part["pleg"] = twos(g["ple_gate"][i])
        part["wq"] = twos(g["peer_wq"][i])
        part["keys"] = g["peer_keys"][i].reshape(2 * HEADS, P, P).transpose(2, 0, 1).reshape(1, P, SLOT)
        w_all += [part[s] for s in PACKED]

        zero = np.zeros((64, W), np.float32)
        lw = np.concatenate([g["rw_w2"][i], zero])
        la = np.concatenate([zero, g["rw_a2"][i]])
        lm = np.concatenate([g["rw_mv_w2"][m0], np.zeros((96, W), np.float32)])
        lo_all.append(np.stack([a.reshape(P, KB, P) for a in (lw, la, lm)], axis=2).transpose(1, 0, 2, 3).reshape(KB, P, 3 * P))
        uu = g["peer_u"][i].reshape(P, P // 2, 2, KB, P)
        u_all.append(uu.transpose(1, 4, 2, 3, 0).reshape(P // 2, P, SLOT))
        vv = g["peer_v"][i].reshape(P, NG, 2, JG // 2, KB, P)
        v_all.append(vv.transpose(1, 4, 2, 0, 3, 5).reshape(NG * KB * 2, P, SLOT))
        rows = lambda a: np.broadcast_to(a.reshape(1, -1), (P, D))
        gm_all.append(np.concatenate([g["gm_ws"][i].transpose(2, 0, 1).reshape(P, D), rows(g["gm_ln_g"][i]),
                                      rows(g["gm_ln_b"][i]), rows(g["gm_bs"][i])], axis=1))
        vs = [g["norm_mix"][i], g["rw_w0"][i], g["rw_a0"][i], g["rw_kk"][i], g["rw_ka"][i], g["rw_rk"][i],
              g["rw_ln_g"][i], g["rw_ln_b"][i], g["rw_mv_v0"][m0], g["norm_ffn"][i], g["norm_final"]]
        vec_all.append(np.stack([a.reshape(KB, P) for a in vs]).transpose(2, 0, 1).reshape(P, -1))
        pt_all.append(g["p"][i, 0].reshape(T, 2, P).transpose(2, 1, 0).reshape(P, 2 * T))
    c_ = np.ascontiguousarray
    return {
        "x": c_(g["x"][0].reshape(T, KB, P).transpose(2, 1, 0)),
        "w": c_(np.concatenate(w_all)), "lo": c_(np.concatenate(lo_all)), "u": c_(np.concatenate(u_all)),
        "v": c_(np.concatenate(v_all)), "pt": c_(np.stack(pt_all)), "gm": c_(np.stack(gm_all)),
        "vec": c_(np.stack(vec_all)), "const": constants(),
    }


def kernel(**inputs):
    import concourse.bacc as bacc
    from concourse.bass_utils import run_bass_kernel_spmd

    nc = bacc.Bacc("TRN2", target_bir_lowering=False, num_devices=1)
    arrays = pack(inputs)
    args = [nc.dram_tensor(f"in_{k}", a.shape, F32, kind="ExternalInput").ap() for k, a in arrays.items()]
    out = nc.dram_tensor("out", (P, KB, T), F32, kind="ExternalOutput").ap()
    vfirst = nc.dram_tensor("v_first", (L * KB, P, T), F32, kind="Internal").ap()
    trunk_kernel(nc, *args, out, vfirst)
    r = run_bass_kernel_spmd(nc, [{f"in_{k}": a for k, a in arrays.items()}], core_ids=[0])
    got = r.results[0]["out"]
    return np.ascontiguousarray(got.transpose(2, 1, 0).reshape(1, T, D))
```

```python
from contextlib import ExitStack

import numpy as np

import concourse.bass as bass
from concourse import mybir

F32 = mybir.dt.float32
BF16 = mybir.dt.bfloat16
U32 = mybir.dt.uint32
ACT = mybir.ActivationFunctionType
ALU = mybir.AluOpType
AXX = mybir.AxisListType.X

P = 128
T = 512
D = 1024
L = 2
KB = D // P
TB = T // P
CH = 64
NC = T // CH
PAIRS = KB
SLOT = 2048
NG = 4
JG = P // NG
TG = 16
TH = TG // 2
TOPK = 16
HEADS = 8
RMS_EPS = 1e-6
RW_EPS = 64e-5
GM_EPS = 1e-5
DECAY = float(np.exp(-0.5))
LOWEST = -3.0e38

VEC = ["norm_mix", "w0", "a0", "kk", "ka", "rk", "ln_g", "ln_b", "v0", "norm_ffn", "final"]
LEVELS = 6

RING = [("wa", 1), ("zg", 1), ("mv1", 1), ("rwkv", 4 * KB), ("gvA", 4), ("g2", 1), ("gvB", 4), ("zu", KB),
        ("mix", 3 * KB), ("wout", 4), ("plew", 1), ("pleg", 4), ("wq", 8), ("keys", 1),
        ("u0", JG // 2), ("u1", JG // 2)]
for _g in range(NG):
    RING.append((f"v{_g}", 2 * KB))
    if _g + 2 < NG:
        RING.append((f"u{_g + 2}", JG // 2))
RING_AT, _n = {}, 0
for _name, _c in RING:
    RING_AT[_name] = _n
    _n += _c
RING_LAYER = _n
assert RING_LAYER % 2 == 0
PACKED = ["wa", "zg", "mv1", "rwkv", "gvA", "g2", "gvB", "zu", "mix", "wout", "plew", "pleg", "wq", "keys"]
PACK_AT, _n = {}, 0
for _name in PACKED:
    PACK_AT[_name] = _n
    _n += 3 * KB if _name == "rwkv" else dict(RING)[_name]
PACK_LAYER = _n

_all = lambda n: {b: n for b in range(8)}
BANKS = [
    ("norm1", {0: 1}), ("lora", {4: 1, 5: 1, 6: 1}), ("rwkv", _all(KB)),
    ("scan", {0: 7 * NC, 1: 7 * NC, 2: 9 * NC, 3: 9 * NC, 4: 7 * NC, 5: 7 * NC, 6: 3 * NC, 7: 3 * NC}),
    ("ysum", _all(1)), ("gvA", {0: 1, 1: 1, 2: 1, 3: 1}), ("g2", {4: 2, 5: 2, 6: 2, 7: 2}),
    ("ysq", {4: 2, 5: 2, 6: 2, 7: 2}), ("gvB", {0: 1, 1: 1, 2: 1, 3: 1}), ("zu", {0: 4, 1: 4, 2: 4, 3: 4}), ("mix", _all(4)),
    ("wout", {0: 2, 1: 2, 2: 2, 3: 2}), ("norm2", {0: 1}), ("plew", _all(1)),
    ("pleg", {0: 2, 1: 2, 2: 2, 3: 2}), ("wq", {0: 4, 1: 4, 2: 4, 3: 4}),
    ("keys", {4: 4, 5: 4, 6: 4, 7: 4}), ("h0", {0: 16, 1: 16}), ("idx", {4: 1, 5: 1, 6: 1}),
]
for _g in range(NG):
    BANKS.append((f"build{_g}", {6: 16, 7: 16}))
    BANKS.append((f"down{_g}", {2: 4, 3: 4}))
    if _g > 0:
        BANKS.append((f"h{_g}", {0: 16, 1: 16}))
BANK_AT, BANK_LAYER = {}, [0] * 8
for _name, _uses in BANKS:
    BANK_AT[_name] = list(BANK_LAYER)
    for _b, _c in _uses.items():
        BANK_LAYER[_b] += _c


def use(layer, stage, bank, k=0):
    return layer * BANK_LAYER[bank] + (k + (BANK_AT[stage][bank] + 1))


def ring(layer, section, k, i=0, per=0):
    n = RING_AT[section] + k
    if per:
        return n % 2, layer * (RING_LAYER // 2) + (i * (per // 2) + (n // 2 + 1))
    return n % 2, layer * (RING_LAYER // 2) + (n // 2 + 1)


CONST, _n = {}, 0
for _name, _c in [("ident", P), ("ones", P), ("blk", P), ("reset", T), ("up", P), ("upd", P),
                  ("lvlN", P), ("lvl", LEVELS * P), ("iota", P), ("causal", P)]:
    CONST[_name] = (_n, _n + _c)
    _n += _c
CONST_COLS = _n


def constants():
    c = np.zeros((P, CONST_COLS), np.float32)
    s = np.arange(P)[:, None]
    t = np.arange(P)[None, :]
    same = s // CH == t // CH

    def put(name, a):
        lo, hi = CONST[name]
        c[:, lo:hi] = a

    put("ident", s == t)
    put("ones", 1.0)
    put("blk", same)
    put("reset", np.arange(T)[None, :] % CH != 0)
    put("up", same & (s < t))
    put("upd", same & (s <= t))
    lv = []
    for n in range(1, LEVELS + 1):
        w = 1 << (n - 1)
        lv.append((s // (2 * w) == t // (2 * w)) & (s // w % 2 == 1) & (t // w % 2 == 0))
    put("lvlN", lv[0].T)
    put("lvl", np.concatenate(lv, axis=1))
    put("iota", t)
    put("causal", s <= t)
    return c


class Arena:

    def __init__(self, tensor):
        self.t, self.n = tensor, 0

    def take(self, cols):
        self.n += cols
        return self.n - cols

    def at(self, lo, cols):
        return self.t[:, lo:lo + cols]


def trunk_kernel(nc, x, w, lo, u, v, pt, gm, vec, const, out, vfirst):
    ctx = ExitStack()
    with ctx:
        def sem(name):
            return ctx.enter_context(nc.semaphore(name))

        COLS = 52800
        ar = Arena(ctx.enter_context(nc.sbuf_tensor("arena", [P, COLS], F32)))
        psum = ctx.enter_context(nc.psum_tensor("psum", [P, 8, T], F32))
        ds, ts = bass.ds, bass.ts

        def tile(lo_, *shape):
            n = int(np.prod(shape))
            a = ar.at(lo_, n)
            if len(shape) == 2:
                return a.rearrange("p (a b) -> p a b", a=shape[0])
            if len(shape) == 3:
                return a.rearrange("p (a b c) -> p a b c", a=shape[0], b=shape[1])
            return a

        h = tile(ar.take(KB * T), KB, T)
        cst = tile(ar.take(CONST_COLS), CONST_COLS)
        vecs = tile(ar.take(len(VEC) * KB), len(VEC), KB)
        slots = tile(ar.take(2 * SLOT), 2, SLOT)
        small = ar.take(4 * T)
        wa_in, zg_in, mv_in, rstd = (tile(small + i * T, T) for i in range(4))
        pend = tile(ar.take(KB * NC), KB, NC)
        NW = T + 1
        n_at = ar.take(KB * NW)
        n = tile(n_at, KB, NW)
        field_at = ar.take(6 * KB * T)
        fields = [field_at + i * KB * T for i in range(6)]
        rest = ar.n
        assert COLS - rest >= 11 * KB * P, COLS - rest

        def cc(name, i=0, width=None):
            a, b = CONST[name]
            return cst[:, a:b] if width is None else cst[:, a + i * width:a + (i + 1) * width]

        ident, ones, blk = cc("ident"), cc("ones"), cc("blk")

        def vcol(name, m):
            return vecs[:, VEC.index(name), ds(m, 1)] if not isinstance(m, int) else vecs[:, VEC.index(name), m:m + 1]

        fa, fb, fk, fr, fv, fbon = (tile(f, KB, T) for f in fields)
        sq_all = fv
        names = ["sg", "ar", "vm", "s", "se", "t", "kkr", "k", "sqk", "rn", "pinc", "pinv", "pexc",
                 "zv", "vf", "b", "rkt"]
        tmp = {q: tile(rest + i * T, T) for i, q in enumerate(names)}
        spots = [n_at + i * KB * P for i in range(4)] + [rest + i * KB * P for i in range(11)]
        bda, bdr, bdb, bdk, bdv, a1, lt, gak, grb, grk, bt, kt, vt, st, rhs = (tile(s, KB, P) for s in spots)
        xm, xt, loff, um = bdb, bdk, bdv, lt
        yc, hsq, yvar, ygate = fa, fb, fk, fv
        gv = tile(rest, TB, D)
        gmp = tile(rest + TB * D, 4 * D)
        wst = gmp[:, 0:D].rearrange("p (g t) -> p g t", g=KB)
        lng, lnb = gmp[:, D:2 * D], gmp[:, 2 * D:3 * D]
        bsb = gmp[:, 3 * D:4 * D].rearrange("p (g t) -> p g t", g=KB)
        yb = tile(fields[2], KB, T)
        merged = tile(fields[4], KB, T)
        ut = tile(rest + 8 * D, 2, T)
        spt = tile(rest + 9 * D, 2, T)
        stats = tile(small, TB, 2, 6)
        mv2 = tile(small + 64, TB, 2)
        lrs = tile(small + 96, TB)
        gates = tile(rest, 4, T)
        mixed = tile(rest + 4 * T, 4, T)
        ppb = tile(fields[0], KB, T)
        ptb = tile(fields[1], 2, T)
        pgb = tile(fields[2], 2, T)
        pmul = tile(small, 2, T)
        gbuf = [tile(fields[0], JG, T), tile(fields[4], JG, T)]
        top_at = fields[4]
        q = tile(top_at, 2 * HEADS, T)
        sc = tile(top_at + 8192, TB, 2 * HEADS * P)
        keep_at = top_at + 16384
        idx = tile(keep_at, 3, T)
        PARTS = 3
        wparts = ar.at(keep_at + 3 * T, PARTS * T // 2).bitcast(BF16).rearrange("p (a t) -> p a t", a=PARTS)
        wrest = tile(keep_at + 3 * T + PARTS * T // 2, T)
        aring = ar.at(small, TG * P // 2).bitcast(BF16).rearrange("p (t k) -> p t k", t=TG)
        bring = ar.at(small + 2 * T, TG * PARTS * JG // 2).bitcast(BF16).rearrange("p (t a k) -> p t a k", t=TG, a=PARTS)
        bhot = ar.at(small + 3 * T + T // 2, TG * JG // 2).bitcast(BF16).rearrange("p (t k) -> p t k", t=TG)
        so = [top_at]

        def scratch(*shape):
            a = tile(so[0], *shape)
            so[0] += int(np.prod(shape))
            return a

        NH = 2 * HEADS
        sw = scratch(NH, P)
        sx = scratch(NH, P)
        tv = scratch(NH, TOPK)
        ti = scratch(NH, TOPK)
        tif = scratch(NH, TOPK)
        bv = scratch(HEADS, TOPK)
        bp = scratch(HEADS, TOPK)
        bq = scratch(2, HEADS * TOPK)
        bqf = scratch(2, HEADS * TOPK)
        hsum = scratch(HEADS)
        hrec = scratch(HEADS)
        pick = scratch(3, P)
        assert so[0] <= top_at + 8192
        cand, cand2, eq = sw, sx, sw
        picks = tile(small, 3, TB * P)
        assert keep_at + 3 * T + PARTS * T // 2 + T <= COLS

        landed = [sem(f"slot{i}_landed") for i in range(2)]
        used = [sem(f"slot{i}_used") for i in range(2)]
        ready = [sem(f"bank{b}_ready") for b in range(8)]
        free = [sem(f"bank{b}_free") for b in range(8)]
        x_in, const_in, vec_in, gm_in, pt_in = (sem(s) for s in ("x_in", "const_in", "vec_in", "gm_in", "pt_in"))
        layer_free = sem("layer_free")
        sq_ready, rms_ready, n_ready = sem("squares_ready"), sem("rms_ready"), sem("normed_ready")
        lora_ready = sem("lora_inputs_ready")
        cum_ready, kkr_ready, sqk_ready, rn_ready = (sem(s) for s in ("decay_sums_ready", "kk_ready", "kk_squares_ready", "kk_norm_ready"))
        p_ready, rk_ready, fields_ready = (sem(s) for s in ("decay_products_ready", "rk_ready", "fields_ready"))
        vf_out, vf_in = sem("v_first_out"), sem("v_first_in")
        bd_dve, bd_act, bd_pool, bd_zero = (sem(s) for s in ("diag_dve_ready", "diag_act_ready", "diag_pool_ready", "diag_zeroed"))
        gram_ready, tr_ready, l_ready, loff_ready = (sem(s) for s in ("gram_ready", "transposed_ready", "l_ready", "l_level_ready"))
        x_ready, a1_ready, rhs_ready, u_ready, s_ready = (sem(s) for s in ("inverse_ready", "half_step_ready", "rhs_ready", "u_ready", "state_ready"))
        y_ready, yc_ready, ysq_ready, yvar_ready, ysd_ready, ya_ready = (sem(s) for s in ("y_ready", "y_centred", "y_squares", "y_var", "y_sd", "ya_ready"))
        ygate_ready = sem("y_gate_ready")
        gelu_v, gvar_ready, gsd_ready, gvn_ready, ws_ready, ug_ready, yb_ready = (sem(s) for s in ("gelu_v_ready", "gm_var_ready", "gm_sd_ready", "gm_v_ready", "ws_masked", "gelu_u_ready", "yb_ready"))
        gate_ready, merged_ready = sem("gates_ready"), sem("merged_ready")
        pp_ready, pg_ready, q_ready = sem("ple_ready"), sem("ple_gate_ready"), sem("q_ready")
        sc_ready, ex_in, ex_out, picks_ready, idx_ready = (sem(s) for s in ("scores_ready", "softmax_in", "softmax_exp", "picks_ready", "idx_ready"))
        act_ready = sem("expert_act_ready")
        hot_ready, hot_used, gated = sem("one_hots_ready"), sem("one_hots_used"), sem("gated_ready")
        pg_used = sem("ple_gate_used")
        out_done = sem("out_written")

        HB = (0, 1)

        def half(t_, hf):
            return t_[:, 4 * hf:4 * hf + 4, :]

        def bank(b):
            return psum[:, b, :]

        def bank4(b):
            return psum[:, b, :].rearrange("p (a c) -> p a c", a=4)

        block = ctx.enter_context(nc.Block())

        @block.sync
        def _(sp):
            sp.dma_start(cst, const).then_inc(const_in, 16)
            sp.dma_start(h, x).then_inc(x_in, 16)

            def send(layer, section, k, src, i=0, per=0, cols=SLOT):
                s, count = ring(layer, section, k, i, per)
                dst = slots[:, s, 0:cols]
                count = sp.snap(count)
                sp.wait_ge(used[s], count)
                sp.dma_start(dst, src).then_inc(landed[s], 16)

            def packed(layer, section, count, per):
                at = PACK_AT[section]
                if count == per:
                    for k in range(count):
                        send(layer, section, k, w[ds(sp.snap(layer * PACK_LAYER + (at + k)), 1), :, :])
                    return
                with sp.Fori(0, count // per) as i:
                    for k in range(per):
                        send(layer, section, k, w[ds(sp.snap(layer * PACK_LAYER + (i * per + (at + k))), 1), :, :], i, per)

            with sp.Fori(0, L) as layer:
                for s in ("wa", "zg", "mv1"):
                    packed(layer, s, 1, 1)
                with sp.Fori(0, KB) as m:
                    send(layer, "rwkv", 0, lo[ds(sp.snap(layer * KB + m), 1), :, :], m, 4, 3 * P)
                    for k in range(3):
                        send(layer, "rwkv", 1 + k,
                             w[ds(sp.snap(layer * PACK_LAYER + (m * 3 + (PACK_AT["rwkv"] + k))), 1), :, :], m, 4)
                packed(layer, "gvA", 4, 2)
                packed(layer, "g2", 1, 1)
                packed(layer, "gvB", 4, 2)
                packed(layer, "zu", 8, 2)
                packed(layer, "mix", 24, 2)
                packed(layer, "wout", 4, 2)
                packed(layer, "plew", 1, 1)
                packed(layer, "pleg", 4, 2)
                packed(layer, "wq", 8, 2)
                packed(layer, "keys", 1, 1)

                def experts_in(g):
                    with sp.Fori(0, JG // 4) as i:
                        for k in range(2):
                            row = sp.snap(layer * (P // 2) + (i * 2 + (g * JG // 2 + k)))
                            send(layer, f"u{g}", k, u[ds(row, 1), :, :], i, 2)

                experts_in(0)
                experts_in(1)
                for g in range(NG):
                    with sp.Fori(0, KB) as i:
                        for k in range(2):
                            row = sp.snap(layer * (NG * 2 * KB) + (i * 2 + (g * 2 * KB + k)))
                            send(layer, f"v{g}", k, v[ds(row, 1), :, :], i, 2)
                    if g + 2 < NG:
                        experts_in(g + 2)
            sp.wait_ge(n_ready, 3 * L + 1)
            sp.dma_start(out, n[:, :, 1:NW]).then_inc(out_done, 16)
            sp.wait_ge(out_done, 16)

        @block.tensor
        def _(pe):
            mm = nc.tensor.matmul
            for s in range(2):
                pe.sem_inc(used[s], 1)
            for b in range(8):
                pe.sem_inc(free[b], 1)

            def take(layer, section, k, i=0, per=0):
                s, count = ring(layer, section, k, i, per)
                pe.wait_ge(landed[s], count * 16)
                return s, slots[:, s, :]

            def done(layer, section, k):
                return used[(RING_AT[section] + k) % 2]

            def open_(layer, stage, b, k=0):
                pe.wait_ge(free[b], use(layer, stage, b, k))

            def norm_sums(layer, stage, count):
                open_(layer, stage, 0)
                pe.wait_ge(sq_ready, count)
                for k in range(KB):
                    last = mm(bank(0), ones, sq_all[:, k, :], start=k == 0, stop=k == KB - 1)
                last.then_inc(ready[0], 1)

            def shifted(k, lo_=0, cols=T):
                off = (1 if k < KB else 0) + lo_
                return n[:, k % KB, off:off + cols]

            def z_block(layer, stage, b, k, ws, cols=P, m=P):
                open_(layer, stage, b, k)
                for kk in range(2 * KB):
                    last = mm(psum[0:m, b, :], ws[:, kk * cols:kk * cols + m], shifted(kk),
                              start=kk == 0, stop=kk == 2 * KB - 1)
                last.then_inc(ready[b], 1)
                return last

            def release(layer, section, k):
                return done(layer, section, k)

            pe.wait_ge(const_in, 16)
            with pe.Fori(0, L) as layer:
                norm_sums(layer, "norm1", layer * 2 + 1)
                pe.wait_ge(n_ready, layer * 3 + 1)
                for section, b, m, cols in (("wa", 4, P, P), ("zg", 5, P, P), ("mv1", 6, 32, 32)):
                    s, ws = take(layer, section, 0)
                    z_block(layer, "lora", b, 0, ws, cols, m)
                    pe.drain().then_inc(used[s], 1)

                with pe.Fori(0, KB) as m:
                    pe.wait_ge(lora_ready, layer * 4 + 4)
                    s, ws = take(layer, "rwkv", 0, m, 4)
                    for b, k in ((3, 0), (4, 1), (5, 2)):
                        open_(layer, "rwkv", b, m)
                        rows = 32 if b == 5 else P
                        src = mv_in[0:32] if b == 5 else wa_in
                        mm(bank(b), ws[0:rows, k * P:(k + 1) * P], src, start=True, stop=True).then_inc(ready[b], 1)
                    pe.drain().then_inc(used[s], 1)
                    q8 = layer * KB + m
                    for b, k in ((0, 1), (1, 2), (2, 3)):
                        s, ws = take(layer, "rwkv", k, m, 4)
                        z_block(layer, "rwkv", b, m, ws)
                        pe.drain().then_inc(used[s], 1)
                        if b == 1:
                            open_(layer, "rwkv", 6, m)
                            pe.wait_ge(sqk_ready, q8 + 1)
                            mm(bank(6), blk, tmp["sqk"], start=True, stop=True).then_inc(ready[6], 1)
                    open_(layer, "rwkv", 7, m)
                    pe.wait_ge(rk_ready, q8 + 1)
                    mm(bank(7), blk, tmp["rkt"], start=True, stop=True).then_inc(ready[7], 1)

                with pe.Fori(0, NC) as c:
                    pe.wait_ge(bd_zero, layer + 1)
                    qc = layer * NC + c
                    pe.wait_ge(bd_dve, layer * (NC + 1) + (c + 1))
                    pe.wait_ge(bd_act, qc + 1)

                    def pairs(b0, k, per, terms, transpose=False):
                        for hf in HB:
                            b = b0 + hf
                            open_(layer, "scan", b, c * per + k)
                            for j in range(4):
                                pr = 4 * hf + j
                                for e, (l_, r_) in enumerate(terms):
                                    if transpose:
                                        last = nc.tensor.transpose(psum[:, b, j * P:(j + 1) * P], l_[:, pr, :], ident)
                                    else:
                                        last = mm(psum[:, b, j * P:(j + 1) * P], l_[:, pr, :], r_[:, pr, :],
                                                  start=e == 0, stop=e == len(terms) - 1)
                            last.then_inc(ready[b], 1)

                    pairs(0, 0, 7, [(bdb, bda)])
                    pairs(2, 0, 9, [(bda, bdb)])
                    pairs(4, 0, 7, [(bdb, None)], True)
                    pe.wait_ge(bd_pool, qc + 1)
                    pairs(6, 0, 3, [(bdb, bdr)])
                    pairs(2, 1, 9, [(bdk, None)], True)
                    pairs(4, 1, 7, [(bdk, bda)])
                    pairs(6, 1, 3, [(bdk, bdr)])
                    pairs(2, 2, 9, [(bdv, None)], True)
                    pe.wait_ge(gram_ready, qc * 6 + 6)
                    pe.wait_ge(tr_ready, qc * 6 + 6)
                    pe.wait_ge(s_ready, layer * 18 + (c * 2 + 2))
                    pairs(6, 2, 3, [(bda, st), (gak, vt)])
                    for lv in range(2, LEVELS + 1):
                        pe.wait_ge(loff_ready, qc * 5 + (lv - 1))
                        for hf in HB:
                            pe.wait_ge(x_ready, qc * 12 + ((lv - 2) * 2 + hf + 1))
                            b = hf
                            open_(layer, "scan", b, c * 7 + (lv - 1))
                            for j in range(4):
                                pr = 4 * hf + j
                                last = mm(psum[:, b, j * P:(j + 1) * P], loff[:, pr, :], xm[:, pr, :], start=True, stop=True)
                            last.then_inc(ready[b], 1)
                        for hf in HB:
                            pe.wait_ge(a1_ready, qc * 10 + ((lv - 2) * 2 + hf + 1))
                            for b, k, per, l_, r_ in ((2 + hf, lv + 1, 9, xt, a1), (4 + hf, lv, 7, a1, xt)):
                                if b >= 4 and lv == LEVELS:
                                    continue
                                open_(layer, "scan", b, c * per + k)
                                for j in range(4):
                                    pr = 4 * hf + j
                                    last = mm(psum[:, b, j * P:(j + 1) * P], l_[:, pr, :], r_[:, pr, :], start=True, stop=True)
                                last.then_inc(ready[b], 1)
                    pe.wait_ge(x_ready, qc * 12 + 12)
                    pe.wait_ge(rhs_ready, qc * 2 + 2)
                    pairs(0, 6, 7, [(xm, rhs)])
                    pe.wait_ge(u_ready, qc * 2 + 2)
                    pairs(2, 8, 9, [(st, bdr), (um, grb), (vt, grk)])
                    pairs(4, 6, 7, [(bt, um), (kt, vt)])

                pe.wait_ge(y_ready, layer + 1)
                for m in range(KB):
                    open_(layer, "ysum", m)
                    mm(bank(m), blk, fr[:, m, :], start=True, stop=True).then_inc(ready[m], 1)

                def gmlp_v(section):
                    for tb in range(TB):
                        open_(layer, section, tb)
                    for qt in range(4):
                        s, ws = take(layer, section, qt)
                        for tb in range(TB):
                            for kk in range(4):
                                k = 4 * qt + kk
                                last = mm(bank(tb), shifted(k, tb * P, P), ws[:, kk * T:(kk + 1) * T],
                                          start=k == 0, stop=k == 2 * KB - 1)
                            if qt == 3:
                                last.then_inc(ready[tb], 1)
                        pe.drain().then_inc(used[s], 1)

                pe.wait_ge(n_ready, layer * 3 + 2)
                gmlp_v("gvA")
                s, ws = take(layer, "g2", 0)
                for m in range(KB):
                    b = 4 + m % 4
                    open_(layer, "g2", b, m // 4)
                    mm(bank(b), ws[:, m * P:(m + 1) * P], zg_in, start=True, stop=True).then_inc(ready[b], 1)
                pe.drain().then_inc(used[s], 1)
                pe.wait_ge(ysq_ready, layer + 1)
                for m in range(KB):
                    b = 4 + m % 4
                    open_(layer, "ysq", b, m // 4)
                    mm(bank(b), blk, hsq[:, m, :], start=True, stop=True).then_inc(ready[b], 1)
                gmlp_v("gvB")
                pe.wait_ge(ws_ready, layer + 1)

                def spatial(g):
                    b = 2 + g % 2
                    open_(layer, "zu", b, g // 2)
                    for tb in range(TB):
                        last = mm(psum[:, b, tb * P:(tb + 1) * P], gv[:, tb, g * P:(g + 1) * P], wst[:, g, :],
                                  start=True, stop=True)
                    last.then_inc(ready[b], 1)

                for g in range(KB):
                    s, ws = take(layer, "zu", g)
                    z_block(layer, "zu", g % 2, g // 2, ws)
                    pe.drain().then_inc(used[s], 1)
                    if g == 1:
                        pe.wait_ge(gvn_ready, layer * TB + TB)
                    if g >= 1:
                        spatial(g - 1)
                spatial(KB - 1)

                with pe.Fori(0, KB // 2) as i:
                    pe.wait_ge(ya_ready, layer + 1)
                    pe.wait_ge(yb_ready, layer * KB + KB)
                    for e in range(2):
                        for k in range(2):
                            s, ws = take(layer, "mix", 3 * e + k, i, 6)
                            z_block(layer, "mix", 4 * e + k, i, ws)
                            pe.drain().then_inc(used[s], 1)
                        s, ws = take(layer, "mix", 3 * e + 2, i, 6)
                        for k, src in ((0, fr), (1, yb)):
                            b = 4 * e + 2 + k
                            open_(layer, "mix", b, i)
                            for kk in range(KB):
                                last = mm(bank(b), ws[:, (k * KB + kk) * P:(k * KB + kk + 1) * P], src[:, kk, :],
                                          start=kk == 0, stop=kk == KB - 1)
                            last.then_inc(ready[b], 1)
                        pe.drain().then_inc(used[s], 1)

                def two_blocks(stage, section, count, src, src_ready, value):
                    with pe.Fori(0, count // 4) as i:
                        pe.wait_ge(src_ready, value)
                        for e in range(2):
                            s, ws = take(layer, section, e, i, 2)
                            for o in range(2):
                                b = 2 * e + o
                                open_(layer, stage, b, i)
                                for kk in range(KB):
                                    last = mm(bank(b), ws[:, (o * KB + kk) * P:(o * KB + kk + 1) * P], src(kk),
                                              start=kk == 0, stop=kk == KB - 1)
                                last.then_inc(ready[b], 1)
                            pe.drain().then_inc(used[s], 1)

                two_blocks("wout", "wout", KB, lambda kk: merged[:, kk, :], merged_ready, layer * KB + KB)
                norm_sums(layer, "norm2", layer * 2 + 2)

                pe.wait_ge(pt_in, layer * 16 + 16)
                s, ws = take(layer, "plew", 0)
                for m in range(KB):
                    open_(layer, "plew", m)
                    for kk in range(2):
                        last = mm(bank(m), ws[:, kk * D + m * P:kk * D + (m + 1) * P], ptb[:, kk, :],
                                  start=kk == 0, stop=kk == 1)
                    last.then_inc(ready[m], 1)
                pe.drain().then_inc(used[s], 1)
                two_blocks("pleg", "pleg", KB, lambda kk: n[:, kk, 1:NW], n_ready, layer * 3 + 3)
                two_blocks("wq", "wq", 2 * HEADS, lambda kk: n[:, kk, 1:NW], n_ready, layer * 3 + 3)
                pe.wait_ge(q_ready, layer * 16 + 16)
                s, ws = take(layer, "keys", 0)
                for tb in range(TB):
                    for e in range(4):
                        open_(layer, "keys", 4 + e, tb)
                        for j in range(4):
                            hp = 4 * e + j
                            last = mm(psum[:, 4 + e, j * P:(j + 1) * P], q[:, hp, tb * P:(tb + 1) * P],
                                      ws[:, hp * P:(hp + 1) * P], start=True, stop=True)
                        last.then_inc(ready[4 + e], 1)
                pe.drain().then_inc(used[s], 1)

                def up(g, j, i):
                    s, ws = take(layer, f"u{g}", j // 2, i, 2)
                    o = j % 2
                    open_(layer, f"h{g}", o, i * 2 + j // 2)
                    for kk in range(KB):
                        last = mm(bank(o), ws[:, (o * KB + kk) * P:(o * KB + kk + 1) * P], n[:, kk, 1:NW],
                                  start=kk == 0, stop=kk == KB - 1)
                    last.then_inc(ready[o], 1)
                    if o == 1:
                        pe.drain().then_inc(used[s], 1)

                def down(g, part, i):
                    b, e = 2 + part // 4, part % 4
                    if e == 0:
                        open_(layer, f"down{g}", b, i)
                    s, ws = take(layer, f"v{g}", part // 2, i, 4)
                    for jj in range(JG // 4):
                        j = e * (JG // 4) + jj
                        at = j % (JG // 2)
                        last = mm(bank(b), ws[:, at * P:(at + 1) * P], gbuf[g % 2][:, j, :], start=j == 0, stop=j == JG - 1)
                    if e == 3:
                        last.then_inc(ready[b], 1)
                    if e % 2 == 1:
                        pe.drain().then_inc(used[s], 1)

                def build(g, e, i, per):
                    b = 6 + e % 2
                    open_(layer, f"build{g}", b, i * (per // 2) + e // 2)
                    for th in range(2):
                        pe.wait_ge(hot_ready, layer * (NG * T // TH) + (i * (2 * per) + (g * T // TH + 2 * e + th + 1)))
                        for j in range(TH):
                            tk = TH * th + j
                            for a in range(PARTS):
                                last = mm(psum[:, b, tk * JG:(tk + 1) * JG], aring[:, tk, :], bring[:, tk, a, :],
                                          start=a == 0, stop=a == PARTS - 1)
                        if th == 0:
                            last.then_inc(hot_used, 1)
                    last.then_inc(ready[b], 1)
                    pe.drain().then_inc(hot_used, 1)

                with pe.Fori(0, JG // 4) as i:
                    for j in range(4):
                        up(0, j, i)
                pe.wait_ge(picks_ready, layer * TB + TB)
                for a in range(3):
                    open_(layer, "idx", 4 + a)
                    for tb in range(TB):
                        last = nc.tensor.transpose(psum[:, 4 + a, tb * P:(tb + 1) * P], picks[:, a, tb * P:(tb + 1) * P], ident)
                    last.then_inc(ready[4 + a], 1)
                with pe.Fori(0, JG // 4) as i:
                    for e in range(4):
                        build(0, e, i, 4)
                        up(1, e, i)
                for g in range(1, NG):
                    with pe.Fori(0, KB // 2) as i:
                        pe.wait_ge(gated, layer * (NG * 32) + g * 32)
                        for e in range(8):
                            build(g, e, i, 8)
                            down(g - 1, e, i)
                    if g + 1 < NG:
                        with pe.Fori(0, JG // 4) as i:
                            for j in range(4):
                                up(g + 1, j, i)
                with pe.Fori(0, KB // 2) as i:
                    pe.wait_ge(gated, layer * (NG * 32) + NG * 32)
                    for e in range(8):
                        down(NG - 1, e, i)
            norm_sums(L, "norm1", 2 * L + 1)

        @block.vector
        def _(dve):
            V = nc.vector
            sync = dve.drain

            def norm(layer, stage, count, scale):
                dve.wait_ge(ready[0], use(layer, stage, 0))
                V.tensor_scalar(rstd, bank(0), 1.0 / D, RMS_EPS, ALU.mult, ALU.add).then_inc(free[0], 1)
                dve.wait_ge(rms_ready, count)
                V.reciprocal(rstd, rstd)
                sync()
                scaled(scale)

            def scaled(scale):
                V.memset(n[:, :, 0:1], 0.0)
                for k in range(KB):
                    last = V.scalar_tensor_tensor(n[:, k, 1:NW], h[:, k, :], vcol(scale, k), rstd, ALU.mult, ALU.mult)
                last.then_inc(n_ready, 1)

            dve.wait_ge(x_in, 16)
            dve.wait_ge(const_in, 16)
            dve.sem_inc(fields_ready, 1)
            dve.sem_inc(hot_used, 2)
            dve.sem_inc(pg_used, 2)
            V.drain().then_inc(layer_free, 1)
            with dve.Fori(0, L) as layer:
                dve.wait_ge(vec_in, layer * 16 + 16)
                norm(layer, "norm1", layer * 2 + 1, "norm_mix")

                with dve.Fori(0, KB) as m:
                    q8 = layer * KB + m

                    def got(b):
                        dve.wait_ge(ready[b], use(layer, "rwkv", b, m))

                    t_ = tmp
                    dve.wait_ge(free[5], use(layer, "rwkv", 5, m + 1))
                    V.tensor_tensor_scan(t_["s"], cc("reset"), t_["sg"], 0.0, ALU.mult, ALU.add)
                    sync()
                    V.tensor_tensor(t_["se"], t_["s"], t_["sg"], ALU.subtract).then_inc(cum_ready, 1)
                    V.tensor_scalar(t_["t"], t_["ar"], -1.0, vcol("ka", m), ALU.add, ALU.mult)
                    got(0)
                    V.tensor_scalar(t_["kkr"], bank(0), vcol("kk", m), None, ALU.mult).then_inc(kkr_ready, 1)
                    sync()
                    V.scalar_tensor_tensor(t_["k"], t_["t"], 1.0, bank(0), ALU.add, ALU.mult).then_inc(free[0], 1)
                    got(1)
                    V.tensor_copy(t_["zv"], bank(1)).then_inc(free[1], 1)
                    got(6)
                    V.tensor_scalar(t_["rn"], bank(6), 1e-24, None, ALU.max).then_inc(free[6], 1)
                    dve.wait_ge(rn_ready, q8 + 1)
                    V.reciprocal(t_["rn"], t_["rn"])
                    sync()
                    V.tensor_tensor(t_["kkr"], t_["kkr"], t_["rn"], ALU.mult)
                    sync()
                    dve.wait_ge(p_ready, q8 + 1)
                    V.scalar_tensor_tensor(fa[:, ds(m, 1), :], t_["kkr"], -1.0, t_["pexc"], ALU.mult, ALU.mult)
                    V.tensor_tensor(t_["b"], t_["kkr"], t_["ar"], ALU.mult)
                    V.tensor_tensor(fk[:, ds(m, 1), :], t_["k"], t_["pinv"], ALU.mult)
                    sync()
                    V.tensor_tensor(fb[:, ds(m, 1), :], t_["b"], t_["pinv"], ALU.mult)
                    got(2)
                    V.scalar_tensor_tensor(t_["rkt"], bank(2), vcol("rk", m), t_["k"], ALU.mult, ALU.mult).then_inc(rk_ready, 1)
                    V.tensor_tensor(fr[:, ds(m, 1), :], bank(2), t_["pinc"], ALU.mult).then_inc(free[2], 1)
                    dve.wait_ge(vf_in, q8 * 16 + 16)
                    V.tensor_tensor(t_["vf"], t_["vf"], t_["zv"], ALU.subtract)
                    sync()
                    V.tensor_tensor(t_["vf"], t_["vf"], t_["vm"], ALU.mult)
                    sync()
                    V.tensor_tensor(fv[:, ds(m, 1), :], t_["zv"], t_["vf"], ALU.add)
                    sync()
                    got(7)
                    V.tensor_tensor(fbon[:, ds(m, 1), :], bank(7), fv[:, ds(m, 1), :], ALU.mult).then_inc(free[7], 1)
                    V.tensor_copy(pend[:, ds(m, 1), :], t_["pinc"].rearrange("p (c t) -> p c t", t=CH)[:, :, CH - 1:CH].rearrange("p c o -> p o c"))
                    V.drain().then_inc(fields_ready, 1)

                dve.wait_ge(ready[7], use(layer, "rwkv", 7, KB - 1))
                for t_ in (bda, bdr, bdb, bdk, bdv):
                    V.memset(t_, 0.0)
                V.drain().then_inc(bd_zero, 1)
                for hf in HB:
                    V.memset(half(st, hf), 0.0).then_inc(s_ready, 1)

                def stage_a(chunk):
                    flat_a = ar.at(fields[0], KB * T + T)
                    for e in range(2):
                        r = slice(e * CH, (e + 1) * CH)
                        src = flat_a[r, ds(chunk * CH, KB * T)].rearrange("p (a t) -> p a t", a=KB)[:, :, 0:CH]
                        last = V.tensor_copy(bda[r, :, e * CH:(e + 1) * CH], src)
                    last.then_inc(bd_dve, 1)

                stage_a(0)
                with dve.Fori(0, NC) as c:
                    qc = layer * NC + c

                    def got(b, k, per):
                        dve.wait_ge(ready[b], use(layer, "scan", b, c * per + k))

                    def wide(name, i=0, width=None):
                        m_ = cc(name, i, width)
                        return m_.rearrange("p (o c) -> p o c", o=1).broadcast_to([P, 4, P])

                    for hf in HB:
                        got(6 + hf, 0, 3)
                        V.tensor_tensor(half(grb, hf), bank4(6 + hf), wide("upd"), ALU.mult).then_inc(gram_ready, 1)
                        V.drain().then_inc(free[6 + hf], 1)
                    for hf in HB:
                        got(hf, 0, 7)
                        V.tensor_tensor(half(xm, hf), bank4(hf), wide("lvlN"), ALU.mult).then_inc(free[hf], 1)
                    sync()
                    for hf in HB:
                        V.tensor_tensor(half(xm, hf), half(xm, hf), wide("ident"), ALU.add)
                    for b0, k, per, dst, mask in ((4, 1, 7, gak, "up"), (6, 1, 3, grk, "upd")):
                        for hf in HB:
                            got(b0 + hf, k, per)
                            V.tensor_tensor(half(dst, hf), bank4(b0 + hf), wide(mask), ALU.mult).then_inc(gram_ready, 1)
                            V.drain().then_inc(free[b0 + hf], 1)
                    dve.wait_ge(l_ready, qc * 2 + 2)
                    got(3, 1, 9)
                    for hf in HB:
                        V.tensor_tensor(half(xt, hf), half(lt, hf), wide("lvl", 0, P), ALU.mult)
                    sync()
                    for hf in HB:
                        V.tensor_tensor(half(xt, hf), half(xt, hf), wide("ident"), ALU.add).then_inc(x_ready, 1)
                    for lv in range(2, LEVELS + 1):
                        for hf in HB:
                            got(2 + hf, lv + 1, 9)
                            if lv < LEVELS:
                                got(4 + hf, lv, 7)
                            up_x = V.tensor_tensor(half(xm, hf), half(xm, hf), bank4(2 + hf), ALU.add)
                            up_x.then_inc(free[2 + hf], 1)
                            if lv < LEVELS:
                                V.tensor_tensor(half(xt, hf), half(xt, hf), bank4(4 + hf), ALU.add).then_inc(free[4 + hf], 1)
                            V.drain().then_inc(x_ready, 1)
                    for hf in HB:
                        got(2 + hf, 8, 9)
                        for e in range(2):
                            r = slice(e * CH, (e + 1) * CH)
                            last = V.tensor_copy(fr[r, 4 * hf:4 * hf + 4, ts(c, CH)], bank4(2 + hf)[r, :, e * CH:(e + 1) * CH])
                        last.then_inc(free[2 + hf], 1)
                    stage_a(c + 1)
                    for hf in HB:
                        got(4 + hf, 6, 7)
                        V.tensor_tensor(half(st, hf), half(st, hf), bank4(4 + hf), ALU.add).then_inc(free[4 + hf], 1)
                    sync()
                    for hf in HB:
                        V.tensor_tensor(half(st, hf), half(st, hf), pend[:, 4 * hf:4 * hf + 4, ds(c, 1)].broadcast_to([P, 4, P]),
                                        ALU.mult).then_inc(s_ready, 1)

                V.drain().then_inc(y_ready, 1)
                scaled("norm_mix")
                for b in range(8):
                    dve.wait_ge(ready[b], use(layer, "ysum", b))
                    V.scalar_tensor_tensor(yc[:, b, :], bank(b), -1.0 / CH, fr[:, b, :], ALU.mult, ALU.add).then_inc(free[b], 1)
                V.drain().then_inc(yc_ready, 1)
                for m in range(KB):
                    b = 4 + m % 4
                    dve.wait_ge(ready[b], use(layer, "ysq", b, m // 4))
                    V.tensor_scalar(yvar[:, m, :], bank(b), 1.0 / CH, RW_EPS, ALU.mult, ALU.add).then_inc(free[b], 1)
                V.drain().then_inc(yvar_ready, 1)
                dve.wait_ge(ysd_ready, layer + 1)
                V.reciprocal(yvar, yvar)
                sync()
                V.tensor_tensor(yc, yc, yvar, ALU.mult)
                sync()
                for m in range(KB):
                    V.tensor_scalar(yc[:, m, :], yc[:, m, :], vcol("ln_g", m), vcol("ln_b", m), ALU.mult, ALU.add)
                sync()
                V.tensor_tensor(yc, yc, fbon, ALU.add)
                sync()
                dve.wait_ge(ygate_ready, layer + 1)
                V.tensor_tensor(fr, yc, ygate, ALU.mult).then_inc(ya_ready, 1)

                for tb in range(TB):
                    dve.wait_ge(gelu_v, layer * 8 + (5 + tb))
                    for hf in HB:
                        V.bn_stats(stats[:, tb, hf, :], gv[:, tb, hf * T:(hf + 1) * T])
                    sync()
                    V.bn_aggr(mv2[:, tb, :], stats[:, tb, :, :])
                    sync()
                    last = V.tensor_scalar(lrs[:, tb:tb + 1], mv2[:, tb, 1:2], GM_EPS, None, ALU.add)
                last.then_inc(gvar_ready, 1)
                dve.wait_ge(gsd_ready, layer + 1)
                dve.wait_ge(gm_in, layer * 16 + 16)
                V.reciprocal(lrs, lrs)
                sync()
                for tb in range(TB):
                    V.scalar_tensor_tensor(gv[:, tb, :], gv[:, tb, :], mv2[:, tb, 0:1], lng, ALU.subtract, ALU.mult)
                sync()
                for tb in range(TB):
                    V.scalar_tensor_tensor(gv[:, tb, :], gv[:, tb, :], lrs[:, tb:tb + 1], lnb, ALU.mult, ALU.add).then_inc(gvn_ready, 1)
                for g in range(KB):
                    b = 2 + g % 2
                    dve.wait_ge(ready[b], use(layer, "zu", b, g // 2))
                    V.tensor_tensor(spt[:, g % 2, :].rearrange("p (b t) -> p b t", b=TB), bank4(b),
                                    bsb[:, g:g + 1, :].broadcast_to([P, TB, P]), ALU.add).then_inc(free[b], 1)
                    sync()
                    dve.wait_ge(ug_ready, layer * KB + (g + 1))
                    V.tensor_tensor(yb[:, g, :], spt[:, g % 2, :], ut[:, g % 2, :], ALU.mult).then_inc(yb_ready, 1)

                with dve.Fori(0, KB // 2) as i:
                    for e in range(2):
                        sync()
                        dve.wait_ge(gate_ready, layer * (2 * KB) + (i * 4 + (2 * e + 2)))
                        for k in range(2):
                            b = 4 * e + 2 + k
                            dve.wait_ge(ready[b], use(layer, "mix", b, i))
                            V.tensor_tensor(mixed[:, 2 * e + k, :], gates[:, 2 * e + k, :], bank(b), ALU.mult).then_inc(free[b], 1)
                        sync()
                        V.tensor_tensor(merged[:, ds(i * 2 + e, 1), :], mixed[:, 2 * e, :], mixed[:, 2 * e + 1, :], ALU.add).then_inc(merged_ready, 1)

                with dve.Fori(0, 2) as i:
                    for b in range(4):
                        dve.wait_ge(ready[b], use(layer, "wout", b, i))
                        hm = h[:, ds(i * 4 + b, 1), :]
                        V.tensor_tensor(hm, hm, bank(b), ALU.add).then_inc(free[b], 1)
                V.drain().then_inc(layer_free, 1)
                norm(layer, "norm2", layer * 2 + 2, "norm_ffn")

                with dve.Fori(0, 2) as i:
                    dve.wait_ge(pp_ready, layer + 1)
                    for b in range(4):
                        dve.wait_ge(pg_ready, layer * KB + (i * 4 + (b + 1)))
                        V.tensor_tensor(pmul[:, b % 2, :], pgb[:, b % 2, :], ppb[:, ds(i * 4 + b, 1), :], ALU.mult).then_inc(pg_used, 1)
                        sync()
                        hm = h[:, ds(i * 4 + b, 1), :]
                        V.tensor_tensor(hm, hm, pmul[:, b % 2, :], ALU.add)
                        sync()

                def top16(rows, wide_, spare, vals, inds, width):
                    for rnd in range(2):
                        src = spare if rnd else wide_
                        r8 = slice(8 * rnd, 8 * rnd + 8)
                        for a in range(rows):
                            V.max(vals[:, a, r8], src[:, a * width:(a + 1) * width])
                        sync()
                        for a in range(rows):
                            V.max_index(inds[:, a, r8], vals[:, a, r8], src[:, a * width:(a + 1) * width])
                            if rnd == 0:
                                V.match_replace(spare[:, a * width:(a + 1) * width], vals[:, a, r8],
                                                src[:, a * width:(a + 1) * width], LOWEST)
                        sync()

                with dve.Fori(0, TB) as tb:
                    dve.wait_ge(sc_ready, layer * 16 + 16)
                    V.tensor_copy(sw.rearrange("p a b -> p (a b)"), sc[:, ds(tb, 1), :].rearrange("p o b -> p (o b)"))
                    sync()
                    flat = lambda t__: t__.rearrange("p a b -> p (a b)")
                    top16(NH, flat(sw), flat(sx), tv, ti.bitcast(U32), P)
                    V.tensor_copy(flat(tif), flat(ti).bitcast(U32))
                    pair = tv.rearrange("p (h c) k -> p h c k", c=2)
                    V.tensor_tensor(flat(cand).rearrange("p (h a b) -> p h a b", h=HEADS, a=TOPK),
                                    pair[:, :, 0, :].rearrange("p h (k o) -> p h k o", o=1).broadcast_to([P, HEADS, TOPK, TOPK]),
                                    pair[:, :, 1, :].rearrange("p h (o k) -> p h o k", o=1).broadcast_to([P, HEADS, TOPK, TOPK]), ALU.add)
                    sync()
                    top16(HEADS, flat(cand), flat(cand2), bv, bp.bitcast(U32), TOPK * TOPK)
                    pw = pick[:, 2, :].rearrange("p (h k) -> p h k", h=HEADS)
                    V.tensor_tensor(pw, bv, bv[:, :, 0:1].broadcast_to([P, HEADS, TOPK]), ALU.subtract)
                    V.drain().then_inc(ex_in, 1)
                    V.tensor_scalar(bq[:, 0, :].bitcast(U32), flat(bp).bitcast(U32), 4, None, ALU.logical_shift_right)
                    V.tensor_scalar(bq[:, 1, :].bitcast(U32), flat(bp).bitcast(U32), 15, None, ALU.bitwise_and)
                    sync()
                    V.tensor_copy(flat(bqf), flat(bq).bitcast(U32))
                    sync()
                    tpair = tif.rearrange("p (h c) k -> p h c k", c=2)
                    NHK = HEADS * TOPK
                    for cpt in range(2):
                        e3 = flat(eq).rearrange("p (a b) -> p a b", a=NHK)
                        V.tensor_tensor(e3, bqf[:, cpt, :].rearrange("p (a o) -> p a o", o=1).broadcast_to([P, NHK, TOPK]),
                                        cc("iota")[:, 0:TOPK].rearrange("p (o a) -> p o a", o=1).broadcast_to([P, NHK, TOPK]), ALU.is_equal)
                        sync()
                        e4 = flat(eq).rearrange("p (h a b) -> p h a b", h=HEADS, a=TOPK)
                        V.tensor_tensor(e4, e4, tpair[:, :, cpt, :].rearrange("p h (o k) -> p h o k", o=1).broadcast_to([P, HEADS, TOPK, TOPK]), ALU.mult)
                        sync()
                        V.tensor_reduce(pick[:, cpt, :], e3, AXX, ALU.add)
                        sync()
                    dve.wait_ge(ex_out, layer * TB + tb + 1)
                    V.tensor_reduce(hsum, pw, AXX, ALU.add)
                    sync()
                    V.reciprocal(hrec, hsum)
                    sync()
                    V.tensor_tensor(pw, pw, hrec.rearrange("p (h o) -> p h o", o=1).broadcast_to([P, HEADS, TOPK]), ALU.mult)
                    sync()
                    V.tensor_copy(picks[:, :, ts(tb, P)], pick).then_inc(picks_ready, 1)
                    sync()
                for a in range(3):
                    dve.wait_ge(ready[4 + a], use(layer, "idx", 4 + a))
                    V.tensor_copy(idx[:, a, :], bank(4 + a)).then_inc(free[4 + a], 1)
                sync()
                left = idx[:, 2, :]
                for a in range(PARTS):
                    V.tensor_copy(wparts[:, a, :], left)
                    sync()
                    if a + 1 < PARTS:
                        V.tensor_tensor(wrest, left, wparts[:, a, :], ALU.subtract)
                        sync()
                    left = wrest

                def build(g, e, i, per):
                    at = i * (per * TG) + e * TG
                    for th in range(2):
                        tok = at + th * TH
                        rows_ = slice(th * TH, (th + 1) * TH)

                        def col(a, width):
                            return idx[:, a, ds(tok, TH)].rearrange("p (t o) -> p t o", o=1).broadcast_to([P, TH, width])

                        weight = wparts[:, :, ds(tok, TH)].rearrange("p a (t o) -> p t a o", o=1).broadcast_to([P, TH, PARTS, JG])
                        hot = bhot[:, rows_, :].rearrange("p t (o k) -> p t o k", o=1).broadcast_to([P, TH, PARTS, JG])

                        def count_to(lo_, width):
                            return cc("iota")[:, lo_:lo_ + width].rearrange("p (o a) -> p o a", o=1).broadcast_to([P, TH, width])

                        dve.wait_ge(hot_used, layer * (NG * T // TH) + (i * (2 * per) + (g * T // TH + 2 * e + th + 1)))
                        V.tensor_tensor(bhot[:, rows_, :], count_to(g * JG, JG), col(1, JG), ALU.is_equal)
                        V.tensor_tensor(aring[:, rows_, :], count_to(0, P), col(0, P), ALU.is_equal)
                        sync()
                        V.tensor_tensor(bring[:, rows_, :, :], hot, weight, ALU.mult).then_inc(hot_ready, 1)

                def gate(g, e, i, per):
                    b = 6 + e % 2
                    dve.wait_ge(act_ready, layer * P + (g + 1) * JG)
                    dve.wait_ge(ready[b], use(layer, f"build{g}", b, i * (per // 2) + e // 2))
                    part = gbuf[g % 2][:, :, ds(i * (per * TG) + e * TG, TG)]
                    V.tensor_tensor(part, part, bank(b).rearrange("p (t j) -> p j t", j=JG), ALU.mult).then_inc(free[b], 1)
                    V.drain().then_inc(gated, 1)

                def add_down(g, e, i):
                    b = 2 + e
                    dve.wait_ge(ready[b], use(layer, f"down{g}", b, i))
                    hm = h[:, ds(i * 2 + e, 1), :]
                    V.tensor_tensor(hm, hm, bank(b), ALU.add).then_inc(free[b], 1)

                with dve.Fori(0, JG // 4) as i:
                    for e in range(5):
                        if e < 4:
                            build(0, e, i, 4)
                        if e > 0:
                            gate(0, e - 1, i, 4)
                for g in range(1, NG):
                    with dve.Fori(0, KB // 2) as i:
                        for e in range(9):
                            if e < 8:
                                build(g, e, i, 8)
                            if e > 0:
                                gate(g, e - 1, i, 8)
                            if e in (5, 8):
                                add_down(g - 1, e // 8, i)
                    sync()
                with dve.Fori(0, KB // 2) as i:
                    for e in range(2):
                        add_down(NG - 1, e, i)
                V.drain().then_inc(layer_free, 1)
            norm(L, "norm1", 2 * L + 1, "final")

        @block.scalar
        def _(act):
            A = nc.scalar.activation
            sync = act.drain

            def squares(count, layer, stage):
                act.wait_ge(layer_free, count)
                A(sq_all, h, ACT.Square).then_inc(sq_ready, 1)
                act.wait_ge(free[0], use(layer, stage, 0, 1))
                A(rstd, rstd, ACT.Sqrt).then_inc(rms_ready, 1)

            act.wait_ge(x_in, 16)
            with act.Fori(0, L) as layer:
                act.wait_ge(layer_free, layer * 2 + 1)
                act.dma_start(vecs, vec[ds(act.snap(layer), 1), :, :]).then_inc(vec_in, 16)
                squares(layer * 2 + 1, layer, "norm1")
                act.wait_ge(vec_in, layer * 16 + 16)
                act.wait_ge(ready[4], use(layer, "lora", 4))
                A(wa_in[0:CH], psum[0:CH, 4, :], ACT.Tanh).then_inc(lora_ready, 1)
                A(wa_in[CH:P], psum[CH:P, 4, :], ACT.Copy).then_inc(free[4], 1)
                act.wait_ge(ready[5], use(layer, "lora", 5))
                A(zg_in, bank(5), ACT.Sigmoid).then_inc(free[5], 1)
                act.wait_ge(ready[6], use(layer, "lora", 6))
                A(mv_in[0:32], psum[0:32, 6, :], ACT.Copy).then_inc(free[6], 1)
                act.drain().then_inc(lora_ready, 3)

                with act.Fori(0, KB) as m:
                    q8 = layer * KB + m
                    act.wait_ge(fields_ready, q8 + 1)
                    for b, dst, bias in ((3, "sg", "w0"), (4, "ar", "a0"), (5, "vm", "v0")):
                        act.wait_ge(ready[b], use(layer, "rwkv", b, m))
                        A(tmp[dst], bank(b), ACT.Sigmoid, bias=vcol(bias, m)).then_inc(free[b], 1)
                    act.wait_ge(cum_ready, q8 + 1)
                    A(tmp["pinc"], tmp["s"], ACT.Exp, scale=-DECAY)
                    A(tmp["pinv"], tmp["s"], ACT.Exp, scale=DECAY)
                    A(tmp["pexc"], tmp["se"], ACT.Exp, scale=-DECAY).then_inc(p_ready, 1)
                    act.wait_ge(kkr_ready, q8 + 1)
                    A(tmp["sqk"], tmp["kkr"], ACT.Square).then_inc(sqk_ready, 1)
                    act.wait_ge(free[6], use(layer, "rwkv", 6, m + 1))
                    A(tmp["rn"], tmp["rn"], ACT.Sqrt).then_inc(rn_ready, 1)

                act.wait_ge(fields_ready, layer * KB + (KB + 1))
                act.wait_ge(bd_zero, layer + 1)
                with act.Fori(0, NC) as c:
                    qc = layer * NC + c

                    def got(b, k, per):
                        act.wait_ge(ready[b], use(layer, "scan", b, c * per + k))

                    for src, dst in ((fb, bdb), (fk, bdk)):
                        for e in range(2):
                            r = slice(e * CH, (e + 1) * CH)
                            last = A(dst[r, :, e * CH:(e + 1) * CH], src[r, :, ts(c, CH)], ACT.Copy)
                    last.then_inc(bd_act, 1)
                    for hf in HB:
                        got(2 + hf, 0, 9)
                        A(half(lt, hf), bank4(2 + hf), ACT.Copy).then_inc(free[2 + hf], 1)
                    act.drain().then_inc(l_ready, 2)
                    for b0, k, per, dst in ((4, 0, 7, bt), (2, 1, 9, kt), (2, 2, 9, vt)):
                        for hf in HB:
                            got(b0 + hf, k, per)
                            A(half(dst, hf), bank4(b0 + hf), ACT.Copy).then_inc(free[b0 + hf], 1)
                    act.drain().then_inc(tr_ready, 6)
                    for hf in HB:
                        got(6 + hf, 2, 3)
                        A(half(rhs, hf), bank4(6 + hf), ACT.Copy).then_inc(free[6 + hf], 1)
                    act.drain().then_inc(rhs_ready, 2)
                    for lv in range(2, LEVELS + 1):
                        for hf in HB:
                            got(hf, lv - 1, 7)
                            A(half(a1, hf), bank4(hf), ACT.Copy).then_inc(free[hf], 1)
                            act.drain().then_inc(a1_ready, 1)
                    for hf in HB:
                        got(hf, 6, 7)
                        A(half(um, hf), bank4(hf), ACT.Copy).then_inc(free[hf], 1)
                    act.drain().then_inc(u_ready, 2)

                act.wait_ge(y_ready, layer + 1)
                act.dma_start(gmp, gm[ds(act.snap(layer), 1), :, :]).then_inc(gm_in, 16)

                def gelu_half(hf, section):
                    for tb in range(TB):
                        act.wait_ge(ready[tb], use(layer, section, tb))
                        A(gv[:, tb, hf * T:(hf + 1) * T], bank(tb), ACT.Gelu_apprx_tanh).then_inc(free[tb], 1)
                        act.drain().then_inc(gelu_v, 1)

                act.wait_ge(yc_ready, layer + 1)
                A(hsq, yc, ACT.Square).then_inc(ysq_ready, 1)
                gelu_half(0, "gvA")
                for m in range(KB):
                    b = 4 + m % 4
                    act.wait_ge(ready[b], use(layer, "g2", b, m // 4))
                    A(ygate[:, m, :], bank(b), ACT.Copy).then_inc(free[b], 1)
                act.drain().then_inc(ygate_ready, 1)
                act.wait_ge(yvar_ready, layer + 1)
                A(yvar, yvar, ACT.Sqrt).then_inc(ysd_ready, 1)
                gelu_half(1, "gvB")
                act.wait_ge(gvar_ready, layer + 1)
                A(lrs, lrs, ACT.Sqrt).then_inc(gsd_ready, 1)
                for g in range(KB):
                    b = g % 2
                    act.wait_ge(ready[b], use(layer, "zu", b, g // 2))
                    if g >= 2:
                        act.wait_ge(yb_ready, layer * KB + (g - 1))
                    A(ut[:, b, :], bank(b), ACT.Gelu_apprx_tanh).then_inc(free[b], 1)
                    act.drain().then_inc(ug_ready, 1)
                act.wait_ge(yb_ready, layer * KB + KB)
                with act.Fori(0, KB // 2) as i:
                    for e in range(2):
                        for k in range(2):
                            b = 4 * e + k
                            act.wait_ge(ready[b], use(layer, "mix", b, i))
                            act.wait_ge(free[4 * e + 2 + k], use(layer, "mix", 4 * e + 2 + k, i))
                            A(gates[:, 2 * e + k, :], bank(b), ACT.Sigmoid).then_inc(free[b], 1)
                            act.drain().then_inc(gate_ready, 1)
                squares(layer * 2 + 2, layer, "norm2")
                act.dma_start(ptb, pt[ds(act.snap(layer), 1), :, :].rearrange("o p (k t) -> (o p) k t", k=2)).then_inc(pt_in, 16)
                for b in range(8):
                    act.wait_ge(ready[b], use(layer, "plew", b))
                    A(ppb[:, b, :], bank(b), ACT.Copy).then_inc(free[b], 1)
                act.drain().then_inc(pp_ready, 1)
                with act.Fori(0, 2) as i:
                    for b in range(4):
                        act.wait_ge(ready[b], use(layer, "pleg", b, i))
                        act.wait_ge(pg_used, layer * 8 + (i * 4 + (b + 1)))
                        A(pgb[:, b % 2, :], bank(b), ACT.Sigmoid).then_inc(free[b], 1)
                        act.drain().then_inc(pg_ready, 1)
                with act.Fori(0, 4) as i:
                    for b in range(4):
                        act.wait_ge(ready[b], use(layer, "wq", b, i))
                        A(q[:, ds(i * 4 + b, 1), :], bank(b), ACT.Copy).then_inc(free[b], 1)
                act.drain().then_inc(q_ready, 16)
                for tb in range(TB):
                    for e in range(4):
                        act.wait_ge(ready[4 + e], use(layer, "keys", 4 + e, tb))
                        A(sc[:, tb, e * T:(e + 1) * T], bank(4 + e), ACT.Copy).then_inc(free[4 + e], 1)
                act.drain().then_inc(sc_ready, 16)

                def expert(g, j, i):
                    o = j % 2
                    act.wait_ge(ready[o], use(layer, f"h{g}", o, i * 2 + j // 2))
                    A(gbuf[g % 2][:, ds(i * 4 + j, 1), :], bank(o), ACT.Gelu_apprx_tanh).then_inc(free[o], 1)

                act.wait_ge(pg_used, layer * 8 + 10)
                with act.Fori(0, TB) as tb:
                    for e in range(JG // 4 // TB):
                        for j in range(4):
                            expert(0, j, tb * (JG // 4 // TB) + e)
                    act.wait_ge(ex_in, layer * TB + tb + 1)
                    A(pick[:, 2, :], pick[:, 2, :], ACT.Exp).then_inc(ex_out, 1)
                act.drain().then_inc(act_ready, JG)
                for g in range(1, NG):
                    if g == 1:
                        act.wait_ge(free[6], use(layer, "idx", 6, 1))
                    with act.Fori(0, JG // 4) as i:
                        for j in range(4):
                            expert(g, j, i)
                    act.drain().then_inc(act_ready, JG)
            squares(2 * L + 1, L, "norm1")

        @block.gpsimd
        def _(pool):
            G = nc.gpsimd
            pool.wait_ge(const_in, 16)
            with pool.Fori(0, L) as layer:
                with pool.Fori(0, KB) as m:
                    q8 = layer * KB + m
                    dst = vfirst[ds(pool.snap(q8), 1), :, :]
                    src = vfirst[ds(pool.snap(m), 1), :, :]
                    pool.wait_ge(free[1], use(layer, "rwkv", 1, m + 1))
                    pool.dma_start(dst, tmp["zv"]).then_inc(vf_out, 16)
                    pool.wait_ge(vf_out, q8 * 16 + 16)
                    pool.dma_start(tmp["vf"], src).then_inc(vf_in, 16)
                with pool.Fori(0, NC) as c:
                    qc = layer * NC + c
                    pool.wait_ge(bd_zero, layer + 1)
                    for src, dst, b, per in ((fv, bdv, 1, 7), (fr, bdr, 3, 9)):
                        pool.wait_ge(ready[b], use(layer, "scan", b, c * per - 1))
                        for e in range(2):
                            r = slice(e * CH, (e + 1) * CH)
                            last = G.tensor_copy(dst[r, :, e * CH:(e + 1) * CH], src[r, :, ts(c, CH)])
                    last.then_inc(bd_pool, 1)
                    pool.wait_ge(l_ready, qc * 2 + 2)
                    pool.wait_ge(ready[3], use(layer, "scan", 3, c * 9 + 2))
                    for lv in range(2, LEVELS + 1):
                        if lv > 2:
                            pool.wait_ge(ready[1], use(layer, "scan", 1, c * 7 + (lv - 2)))
                        mask = cc("lvl", lv - 1, P).rearrange("p (o c) -> p o c", o=1).broadcast_to([P, KB, P])
                        G.tensor_tensor(loff, lt, mask, ALU.mult).then_inc(loff_ready, 1)
                pool.wait_ge(gm_in, layer * 16 + 16)
                G.tensor_tensor(wst, wst, cc("causal").rearrange("p (o c) -> p o c", o=1).broadcast_to([P, KB, P]),
                                ALU.mult).then_inc(ws_ready, 1)


def pack(inputs):
    g = {k: np.ascontiguousarray(a) for k, a in inputs.items()}

    def blocks(a, cols=P):
        k, m = a.shape
        return a.reshape(k // P, P, m // cols, cols).transpose(2, 1, 0, 3)

    def pad(a, cols=SLOT):
        a = a.reshape(a.shape[0], P, -1)
        if a.shape[2] == cols:
            return a
        return np.concatenate([a, np.zeros((a.shape[0], P, cols - a.shape[2]), a.dtype)], axis=2)

    W = 1024
    w_all, lo_all, u_all, v_all, gm_all, vec_all, pt_all = [], [], [], [], [], [], []
    for i in range(L):
        m0 = max(i - 1, 0)
        z = g["w_in"][i]
        c = np.cumsum([0, W, W, W, 64, 64, 128, W, W, W, W])
        zr, zk, zv = (z[:, c[j]:c[j + 1]] for j in range(3))
        part = {
            "wa": pad(blocks(z[:, c[3]:c[5]])), "zg": pad(blocks(z[:, c[5]:c[6]])),
            "mv1": pad(blocks(g["rw_mv_w1"][m0], 32)),
            "rwkv": np.stack([blocks(zk), blocks(zv), blocks(zr)], axis=1).reshape(3 * KB, P, SLOT),
            "g2": pad(g["rw_g2"][i][None]),
        }
        zgv = z[:, c[7]:c[8]].reshape(4, 4, P, 2, T)
        zgv = zgv.transpose(3, 0, 2, 1, 4).reshape(2, 4, P, SLOT)
        part["gvA"], part["gvB"] = zgv[0], zgv[1]
        part["zu"] = pad(blocks(z[:, c[6]:c[7]]))
        proj = np.concatenate([blocks(g["w_proj_a"][i]), blocks(g["w_proj_b"][i])], axis=2)
        part["mix"] = np.stack([pad(blocks(z[:, c[8]:c[9]])), pad(blocks(z[:, c[9]:c[10]])),
                                proj.reshape(KB, P, SLOT)], axis=1).reshape(3 * KB, P, SLOT)

        def twos(a):
            b = blocks(a)
            return b.reshape(b.shape[0] // 2, 2, P, -1).transpose(0, 2, 1, 3).reshape(-1, P, SLOT)

        part["wout"] = twos(g["w_out"][i])
        part["plew"] = g["ple_w"][i].reshape(2, P, D).transpose(1, 0, 2).reshape(1, P, SLOT)
        part["pleg"] = twos(g["ple_gate"][i])
        part["wq"] = twos(g["peer_wq"][i])
        part["keys"] = g["peer_keys"][i].reshape(2 * HEADS, P, P).transpose(2, 0, 1).reshape(1, P, SLOT)
        w_all += [part[s] for s in PACKED]

        zero = np.zeros((64, W), np.float32)
        lw = np.concatenate([g["rw_w2"][i], zero])
        la = np.concatenate([zero, g["rw_a2"][i]])
        lm = np.concatenate([g["rw_mv_w2"][m0], np.zeros((96, W), np.float32)])
        lo_all.append(np.stack([a.reshape(P, KB, P) for a in (lw, la, lm)], axis=2).transpose(1, 0, 2, 3).reshape(KB, P, 3 * P))
        uu = g["peer_u"][i].reshape(P, P // 2, 2, KB, P)
        u_all.append(uu.transpose(1, 4, 2, 3, 0).reshape(P // 2, P, SLOT))
        vv = g["peer_v"][i].reshape(P, NG, 2, JG // 2, KB, P)
        v_all.append(vv.transpose(1, 4, 2, 0, 3, 5).reshape(NG * KB * 2, P, SLOT))
        rows = lambda a: np.broadcast_to(a.reshape(1, -1), (P, D))
        gm_all.append(np.concatenate([g["gm_ws"][i].transpose(2, 0, 1).reshape(P, D), rows(g["gm_ln_g"][i]),
                                      rows(g["gm_ln_b"][i]), rows(g["gm_bs"][i])], axis=1))
        vs = [g["norm_mix"][i], g["rw_w0"][i], g["rw_a0"][i], g["rw_kk"][i], g["rw_ka"][i], g["rw_rk"][i],
              g["rw_ln_g"][i], g["rw_ln_b"][i], g["rw_mv_v0"][m0], g["norm_ffn"][i], g["norm_final"]]
        vec_all.append(np.stack([a.reshape(KB, P) for a in vs]).transpose(2, 0, 1).reshape(P, -1))
        pt_all.append(g["p"][i, 0].reshape(T, 2, P).transpose(2, 1, 0).reshape(P, 2 * T))
    c_ = np.ascontiguousarray
    return {
        "x": c_(g["x"][0].reshape(T, KB, P).transpose(2, 1, 0)),
        "w": c_(np.concatenate(w_all)), "lo": c_(np.concatenate(lo_all)), "u": c_(np.concatenate(u_all)),
        "v": c_(np.concatenate(v_all)), "pt": c_(np.stack(pt_all)), "gm": c_(np.stack(gm_all)),
        "vec": c_(np.stack(vec_all)), "const": constants(),
    }


def kernel(**inputs):
    import concourse.bacc as bacc
    from concourse.bass_utils import run_bass_kernel_spmd

    nc = bacc.Bacc("TRN2", target_bir_lowering=False, num_devices=1)
    arrays = pack(inputs)
    args = [nc.dram_tensor(f"in_{k}", a.shape, F32, kind="ExternalInput").ap() for k, a in arrays.items()]
    out = nc.dram_tensor("out", (P, KB, T), F32, kind="ExternalOutput").ap()
    vfirst = nc.dram_tensor("v_first", (L * KB, P, T), F32, kind="Internal").ap()
    trunk_kernel(nc, *args, out, vfirst)
    r = run_bass_kernel_spmd(nc, [{f"in_{k}": a for k, a in arrays.items()}], core_ids=[0])
    got = r.results[0]["out"]
    return np.ascontiguousarray(got.transpose(2, 1, 0).reshape(1, T, D))
```

```python
from contextlib import ExitStack

import numpy as np

import concourse.bass as bass
from concourse import mybir

F32 = mybir.dt.float32
F32R = mybir.dt.float32r
BF16 = mybir.dt.bfloat16
U32 = mybir.dt.uint32
ACT = mybir.ActivationFunctionType
ALU = mybir.AluOpType
AXX = mybir.AxisListType.X

P = 128
T = 512
D = 1024
L = 2
KB = D // P
TB = T // P
CH = 64
NC = T // CH
PAIRS = KB
SLOT = 2048
NG = 4
JG = P // NG
TG = 16
TH = TG // 2
TOPK = 16
HEADS = 8
RMS_EPS = 1e-6
RW_EPS = 64e-5
GM_EPS = 1e-5
DECAY = float(np.exp(-0.5))
LOWEST = -3.0e38

VEC = ["norm_mix", "w0", "a0", "kk", "ka", "rk", "ln_g", "ln_b", "v0", "norm_ffn", "final"]
LEVELS = 6

RING = [("wa", 1), ("zg", 1), ("mv1", 1), ("rwkv", 4 * KB), ("gvA", 4), ("g2", 1), ("gvB", 4), ("zu", KB),
        ("mix", 3 * KB), ("wout", 4), ("plew", 1), ("pleg", 4), ("wq", 8), ("keys", 1),
        ("u0", JG // 2), ("u1", JG // 2)]
for _g in range(NG):
    RING.append((f"v{_g}", 2 * KB))
    if _g + 2 < NG:
        RING.append((f"u{_g + 2}", JG // 2))
RING_AT, _n = {}, 0
for _name, _c in RING:
    RING_AT[_name] = _n
    _n += _c
RING_LAYER = _n
assert RING_LAYER % 2 == 0
PACKED = ["wa", "zg", "mv1", "rwkv", "gvA", "g2", "gvB", "zu", "mix", "wout", "plew", "pleg", "wq", "keys"]
PACK_AT, _n = {}, 0
for _name in PACKED:
    PACK_AT[_name] = _n
    _n += 3 * KB if _name == "rwkv" else dict(RING)[_name]
PACK_LAYER = _n

QT = SLOT // 4
SPLIT = ["zu", "mix", "pleg", "wq"] + [f"u{_g}" for _g in range(1, NG)]
SPLIT_AT, _n = {}, 0
for _name in SPLIT:
    SPLIT_AT[_name] = _n
    _n += 4 * dict(RING)[_name]
SPLIT_LAYER = _n


def split(layer, section, c, i=0, per=0):
    if per:
        return layer * SPLIT_LAYER + (i * (4 * per) + (SPLIT_AT[section] + c))
    return layer * SPLIT_LAYER + (SPLIT_AT[section] + c)


_all = lambda n: {b: n for b in range(8)}
BANKS = [
    ("norm1", {0: 1}), ("lora", {4: 1, 5: 1, 6: 1}), ("rwkv", _all(KB)),
    ("scan", {0: 7 * NC, 1: 7 * NC, 2: 9 * NC, 3: 9 * NC, 4: 7 * NC, 5: 7 * NC, 6: 3 * NC, 7: 3 * NC}),
    ("ysum", _all(1)), ("gvA", {0: 1, 1: 1, 2: 1, 3: 1}), ("g2", {4: 2, 5: 2, 6: 2, 7: 2}),
    ("ysq", {4: 2, 5: 2, 6: 2, 7: 2}), ("gvB", {0: 1, 1: 1, 2: 1, 3: 1}), ("zu", {0: 4, 1: 4, 2: 4, 3: 4}), ("mix", _all(4)),
    ("wout", {0: 2, 1: 2, 2: 2, 3: 2}), ("norm2", {0: 1}), ("plew", _all(1)),
    ("pleg", {0: 2, 1: 2, 2: 2, 3: 2}), ("wq", {0: 4, 1: 4, 2: 4, 3: 4}),
    ("keys", {4: 4, 5: 4, 6: 4, 7: 4}), ("h0", {0: 16, 1: 16}), ("idx", {4: 1, 5: 1, 6: 1}),
]
for _g in range(NG):
    BANKS.append((f"build{_g}", {6: 16, 7: 16}))
    BANKS.append((f"down{_g}", {2: 4, 3: 4}))
    if _g > 0:
        BANKS.append((f"h{_g}", {0: 16, 1: 16}))
BANK_AT, BANK_LAYER = {}, [0] * 8
for _name, _uses in BANKS:
    BANK_AT[_name] = list(BANK_LAYER)
    for _b, _c in _uses.items():
        BANK_LAYER[_b] += _c


def use(layer, stage, bank, k=0):
    return layer * BANK_LAYER[bank] + (k + (BANK_AT[stage][bank] + 1))


def ring(layer, section, k, i=0, per=0):
    n = RING_AT[section] + k
    if per:
        return n % 2, layer * (RING_LAYER // 2) + (i * (per // 2) + (n // 2 + 1))
    return n % 2, layer * (RING_LAYER // 2) + (n // 2 + 1)


CONST, _n = {}, 0
for _name, _c in [("ident", P), ("ones", P), ("iota", P), ("blk", P), ("reset", T), ("up", P), ("upd", P),
                  ("lvlN", P), ("lvl", LEVELS * P), ("causal", P)]:
    CONST[_name] = (_n, _n + _c)
    _n += _c
MASKS = CONST["blk"][0]
CONST_COLS = max(_n, MASKS + 4 * QT)


def constants():
    c = np.zeros((P, CONST_COLS), np.float32)
    s = np.arange(P)[:, None]
    t = np.arange(P)[None, :]
    same = s // CH == t // CH

    def put(name, a):
        lo, hi = CONST[name]
        c[:, lo:hi] = a

    put("ident", s == t)
    put("ones", 1.0)
    put("blk", same)
    put("reset", np.arange(T)[None, :] % CH != 0)
    put("up", same & (s < t))
    put("upd", same & (s <= t))
    lv = []
    for n in range(1, LEVELS + 1):
        w = 1 << (n - 1)
        lv.append((s // (2 * w) == t // (2 * w)) & (s // w % 2 == 1) & (t // w % 2 == 0))
    put("lvlN", lv[0].T)
    put("lvl", np.concatenate(lv, axis=1))
    put("iota", t)
    put("causal", s <= t)
    return c


class Arena:

    def __init__(self, tensor):
        self.t, self.n = tensor, 0

    def take(self, cols):
        self.n += cols
        return self.n - cols

    def at(self, lo, cols):
        return self.t[:, lo:lo + cols]


def trunk_kernel(nc, x, w, lo, u, v, pt, gm, vec, const, out, vfirst, hdram):
    ctx = ExitStack()
    with ctx:
        def sem(name):
            return ctx.enter_context(nc.semaphore(name))

        COLS = 53200
        base = -(-nc.sbuf_base // 32) * 32
        ar = Arena(ctx.enter_context(nc.sbuf_tensor("arena", [P, COLS], F32)))
        psum = ctx.enter_context(nc.psum_tensor("psum", [P, 8, T], F32))
        ds, ts = bass.ds, bass.ts

        def tile(lo_, *shape):
            n = int(np.prod(shape))
            a = ar.at(lo_, n)
            if len(shape) == 2:
                return a.rearrange("p (a b) -> p a b", a=shape[0])
            if len(shape) == 3:
                return a.rearrange("p (a b c) -> p a b c", a=shape[0], b=shape[1])
            return a

        def rounded(name, lo_, cols):
            at, off = lo_ // 8 * 8, lo_ % 8
            t_ = nc.alloc_sbuf_tensor_at(name, [P, -(-(off + cols) // 8) * 8], F32R, offset=base + 4 * at)
            return t_[:, off:off + cols]

        def rounded_blocks(name, lo_, stride=T, width=T):
            return [rounded(f"{name}{k}", lo_ + k * stride, width) for k in range(KB)]

        h_at = ar.take(KB * T)
        h = tile(h_at, KB, T)
        cst_at = ar.take(CONST_COLS)
        cst = tile(cst_at, CONST_COLS)
        vecs = tile(ar.take(len(VEC) * KB), len(VEC), KB)
        slots = tile(ar.take(2 * SLOT), 2, SLOT)
        small = ar.take(4 * T)
        wa_in, zg_in, mv_in, rstd = (tile(small + i * T, T) for i in range(4))
        pend = tile(ar.take(KB * NC), KB, NC)
        NW = T + 1
        n_at = ar.take(KB * NW)
        n = tile(n_at, KB, NW)
        field_at = ar.take(6 * KB * T)
        fields = [field_at + i * KB * T for i in range(6)]
        rest = ar.n
        assert COLS - rest >= 11 * KB * P, COLS - rest

        def cc(name, i=0, width=None):
            a, b = CONST[name]
            return cst[:, a:b] if width is None else cst[:, a + i * width:a + (i + 1) * width]

        ident, ones, blk = cc("ident"), cc("ones"), cc("blk")

        def vcol(name, m):
            return vecs[:, VEC.index(name), ds(m, 1)] if not isinstance(m, int) else vecs[:, VEC.index(name), m:m + 1]

        fa, fb, fk, fr, fv, fbon = (tile(f, KB, T) for f in fields)
        squared = tile(fields[0], KB, T)
        names = ["sg", "ar", "vm", "s", "se", "t", "kkr", "k", "sqk", "rn", "pinc", "pinv", "pexc",
                 "zv", "vf", "b", "rkt"]
        tmp = {q: tile(rest + i * T, T) for i, q in enumerate(names)}
        spots = [n_at + i * KB * P for i in range(4)] + [rest + i * KB * P for i in range(11)]
        bda, bdr, bdb, bdk, bdv, a1, lt, gak, grb, grk, bt, kt, vt, st, rhs = (tile(s, KB, P) for s in spots)
        xm, xt, loff, um = bdb, bdk, bdv, lt
        yc, hsq, yvar, ygate = fa, fb, fk, fv
        gv = tile(rest, TB, D)
        gmp = tile(rest + TB * D, 4 * D)
        wst = gmp[:, 0:D].rearrange("p (g t) -> p g t", g=KB)
        lng, lnb = gmp[:, D:2 * D], gmp[:, 2 * D:3 * D]
        bsb = gmp[:, 3 * D:4 * D].rearrange("p (g t) -> p g t", g=KB)
        yb = tile(fields[4], KB, T)
        merged = tile(rest + 4 * D, KB, T)
        ut = tile(rest + 8 * D, 2, T)
        spt = tile(rest + 9 * D, 2, T)
        stats = tile(small, TB, 2, 6)
        mv2 = tile(small + 64, TB, 2)
        lrs = tile(small + 96, TB)
        gates = tile(rest, 4, T)
        mixed = tile(rest + 4 * T, 4, T)
        ppb = tile(fields[0], KB, T)
        ptb = tile(fields[1], 2, T)
        pgb = tile(fields[1] + 2 * T, 2, T)
        pmul = tile(small, 2, T)
        gbuf = [tile(fields[0], JG, T), tile(fields[4], JG, T)]
        top_at = fields[4]
        q = tile(top_at, 2 * HEADS, T)
        sc = tile(top_at + 8192, TB, 2 * HEADS * P)
        keep_at = top_at + 16384
        idx = tile(keep_at, 3, T)
        PARTS = 3
        wparts = ar.at(keep_at + 3 * T, PARTS * T // 2).bitcast(BF16).rearrange("p (a t) -> p a t", a=PARTS)
        wrest = tile(keep_at + 3 * T + PARTS * T // 2, T)
        aring = ar.at(small, TG * P // 2).bitcast(BF16).rearrange("p (t k) -> p t k", t=TG)
        bring = ar.at(small + 2 * T, TG * PARTS * JG // 2).bitcast(BF16).rearrange("p (t a k) -> p t a k", t=TG, a=PARTS)
        bhot = ar.at(small + 3 * T + T // 2, TG * JG // 2).bitcast(BF16).rearrange("p (t k) -> p t k", t=TG)
        n1_high = rounded_blocks("n1_high", fields[0], NW, NW)
        n1_low = rounded_blocks("n1_low", fields[0] + KB * NW, NW, NW)
        ya_high, ya_low = rounded_blocks("ya_high", n_at), rounded_blocks("ya_low", fields[3])
        yb_high, yb_low = rounded_blocks("yb_high", fields[5]), rounded_blocks("yb_low", fields[4])
        n_high = rounded_blocks("n_high", h_at)
        n_low = rounded_blocks("n_low", n_at + 1, NW)
        wsplit = rounded("w_split", cst_at + MASKS, 4 * QT).rearrange("p (a b c) -> p a b c", a=2, b=2)
        n2_high = rounded_blocks("n2_high", fields[3])
        n2_low = rounded_blocks("n2_low", fields[2])
        hblk = [idx[:, 2, :], wrest]
        so = [top_at]

        def scratch(*shape):
            a = tile(so[0], *shape)
            so[0] += int(np.prod(shape))
            return a

        NH = 2 * HEADS
        sw = scratch(NH, P)
        sx = scratch(NH, P)
        tv = scratch(NH, TOPK)
        ti = scratch(NH, TOPK)
        tif = scratch(NH, TOPK)
        bv = scratch(HEADS, TOPK)
        bp = scratch(HEADS, TOPK)
        bq = scratch(2, HEADS * TOPK)
        bqf = scratch(2, HEADS * TOPK)
        hsum = scratch(HEADS)
        hrec = scratch(HEADS)
        pick = scratch(3, P)
        assert so[0] <= top_at + 8192
        cand, cand2, eq = sw, sx, sw
        picks = tile(small, 3, TB * P)
        assert keep_at + 3 * T + PARTS * T // 2 + T <= COLS

        landed = [sem(f"slot{i}_landed") for i in range(2)]
        used = [sem(f"slot{i}_used") for i in range(2)]
        ready = [sem(f"bank{b}_ready") for b in range(8)]
        free = [sem(f"bank{b}_free") for b in range(8)]
        x_in, const_in, vec_in, gm_in, pt_in = (sem(s) for s in ("x_in", "const_in", "vec_in", "gm_in", "pt_in"))
        h_ready = sem("h_blocks_ready")
        sq_ready, rms_ready, n_ready = sem("squares_ready"), sem("rms_ready"), sem("normed_ready")
        lora_ready = sem("lora_inputs_ready")
        cum_ready, kkr_ready, sqk_ready, rn_ready = (sem(s) for s in ("decay_sums_ready", "kk_ready", "kk_squares_ready", "kk_norm_ready"))
        p_ready, rk_ready, fields_ready = (sem(s) for s in ("decay_products_ready", "rk_ready", "fields_ready"))
        vf_out, vf_in = sem("v_first_out"), sem("v_first_in")
        bd_dve, bd_act, bd_pool, bd_zero = (sem(s) for s in ("diag_dve_ready", "diag_act_ready", "diag_pool_ready", "diag_zeroed"))
        gram_ready, tr_ready, l_ready, loff_ready = (sem(s) for s in ("gram_ready", "transposed_ready", "l_ready", "l_level_ready"))
        x_ready, a1_ready, rhs_ready, u_ready, s_ready = (sem(s) for s in ("inverse_ready", "half_step_ready", "rhs_ready", "u_ready", "state_ready"))
        y_ready, yc_ready, ysq_ready, yvar_ready, ysd_ready, ya_ready = (sem(s) for s in ("y_ready", "y_centred", "y_squares", "y_var", "y_sd", "ya_ready"))
        ygate_ready = sem("y_gate_ready")
        gelu_v, gvar_ready, gsd_ready, gvn_ready, ws_ready, ug_ready, yb_ready = (sem(s) for s in ("gelu_v_ready", "gm_var_ready", "gm_sd_ready", "gm_v_ready", "ws_masked", "gelu_u_ready", "yb_ready"))
        gate_ready, merged_ready = sem("gates_ready"), sem("merged_ready")
        pp_ready, pg_ready, q_ready = sem("ple_ready"), sem("ple_gate_ready"), sem("q_ready")
        sc_ready, ex_in, ex_out, picks_ready, idx_ready = (sem(s) for s in ("scores_ready", "softmax_in", "softmax_exp", "picks_ready", "idx_ready"))
        act_ready = sem("expert_act_ready")
        hot_ready, hot_used, gated = sem("one_hots_ready"), sem("one_hots_used"), sem("gated_ready")
        pg_used = sem("ple_gate_used")
        out_done = sem("out_written")
        high_ready, low_ready, split_used = sem("high_parts_ready"), sem("low_parts_ready"), sem("split_parts_used")
        ple_added, h_out, h_back, masks_back = sem("ple_added"), sem("h_spilled"), sem("h_back"), sem("masks_back")
        nhigh_ready, nlow_ready = sem("n_high_ready"), sem("n_low_ready")
        n1_high_ready, n1_low_ready = sem("n1_high_ready"), sem("n1_low_ready")
        ya_high_ready, yb_high_ready, y_low_ready = sem("ya_high_ready"), sem("yb_high_ready"), sem("y_low_ready")
        n2_block, n2_high_ready, n2_low_ready = sem("n2_block_ready"), sem("n2_high_ready"), sem("n2_low_ready")
        hblk_in = [sem(f"h_block{e}_in") for e in range(2)]
        hblk_out = [sem(f"h_block{e}_out") for e in range(2)]
        hblk_added = [sem(f"h_block{e}_added") for e in range(2)]

        HB = (0, 1)

        def half(t_, hf):
            return t_[:, 4 * hf:4 * hf + 4, :]

        def bank(b):
            return psum[:, b, :]

        def bank4(b):
            return psum[:, b, :].rearrange("p (a c) -> p a c", a=4)

        block = ctx.enter_context(nc.Block())

        @block.sync
        def _(sp):
            sp.dma_start(cst, const).then_inc(const_in, 16)
            sp.dma_start(h, x).then_inc(x_in, 16)

            def send(layer, section, k, src, i=0, per=0, cols=SLOT):
                s, count = ring(layer, section, k, i, per)
                dst = slots[:, s, 0:cols]
                count = sp.snap(count)
                sp.wait_ge(used[s], count)
                sp.dma_start(dst, src).then_inc(landed[s], 16)

            def packed(layer, section, count, per):
                at = PACK_AT[section]
                if count == per:
                    for k in range(count):
                        send(layer, section, k, w[ds(sp.snap(layer * PACK_LAYER + (at + k)), 1), :, :])
                    return
                with sp.Fori(0, count // per) as i:
                    for k in range(per):
                        send(layer, section, k, w[ds(sp.snap(layer * PACK_LAYER + (i * per + (at + k))), 1), :, :], i, per)

            with sp.Fori(0, L) as layer:
                for s in ("wa", "zg", "mv1"):
                    packed(layer, s, 1, 1)
                with sp.Fori(0, KB) as m:
                    send(layer, "rwkv", 0, lo[ds(sp.snap(layer * KB + m), 1), :, :], m, 4, 3 * P)
                    for k in range(3):
                        send(layer, "rwkv", 1 + k,
                             w[ds(sp.snap(layer * PACK_LAYER + (m * 3 + (PACK_AT["rwkv"] + k))), 1), :, :], m, 4)
                packed(layer, "gvA", 4, 2)
                packed(layer, "g2", 1, 1)
                packed(layer, "gvB", 4, 2)
                packed(layer, "zu", 8, 2)
                packed(layer, "mix", 24, 2)
                packed(layer, "wout", 4, 2)
                packed(layer, "plew", 1, 1)
                packed(layer, "pleg", 4, 2)
                packed(layer, "wq", 8, 2)
                packed(layer, "keys", 1, 1)

                def experts_in(g):
                    with sp.Fori(0, JG // 4) as i:
                        for k in range(2):
                            row = sp.snap(layer * (P // 2) + (i * 2 + (g * JG // 2 + k)))
                            send(layer, f"u{g}", k, u[ds(row, 1), :, :], i, 2)

                experts_in(0)
                experts_in(1)
                for g in range(NG):
                    with sp.Fori(0, KB) as i:
                        for k in range(2):
                            row = sp.snap(layer * (NG * 2 * KB) + (i * 2 + (g * 2 * KB + k)))
                            send(layer, f"v{g}", k, v[ds(row, 1), :, :], i, 2)
                    if g + 2 < NG:
                        experts_in(g + 2)
            sp.wait_ge(n_ready, 3 * L + 1)
            sp.dma_start(out, n[:, :, 1:NW]).then_inc(out_done, 16)
            sp.wait_ge(out_done, 16)

        @block.tensor
        def _(pe):
            mm = nc.tensor.matmul
            for s in range(2):
                pe.sem_inc(used[s], 1)
            for b in range(8):
                pe.sem_inc(free[b], 1)
            pe.sem_inc(split_used, 2)

            def take(layer, section, k, i=0, per=0):
                s, count = ring(layer, section, k, i, per)
                pe.wait_ge(landed[s], count * 16)
                return s, slots[:, s, :]

            def done(layer, section, k):
                return used[(RING_AT[section] + k) % 2]

            def open_(layer, stage, b, k=0):
                pe.wait_ge(free[b], use(layer, stage, b, k))

            def norm_sums(layer, stage, count):
                open_(layer, stage, 0)
                for k in range(KB):
                    pe.wait_ge(sq_ready, (count - 1) * KB + (k + 1))
                    last = mm(bank(0), ones, squared[:, k, :], start=k == 0, stop=k == KB - 1)
                last.then_inc(ready[0], 1)

            def shifted(k, lo_=0, cols=T):
                off = (1 if k < KB else 0) + lo_
                return n[:, k % KB, off:off + cols]

            def z_block(layer, stage, b, k, ws, cols=P, m=P):
                open_(layer, stage, b, k)
                for kk in range(2 * KB):
                    last = mm(psum[0:m, b, :], ws[:, kk * cols:kk * cols + m], shifted(kk),
                              start=kk == 0, stop=kk == 2 * KB - 1)
                last.then_inc(ready[b], 1)
                return last

            def release(layer, section, k):
                return done(layer, section, k)

            pe.wait_ge(const_in, 16)
            with pe.Fori(0, L) as layer:
                norm_sums(layer, "norm1", layer * 2 + 1)
                pe.wait_ge(n_ready, layer * 3 + 1)
                for section, b, m, cols in (("wa", 4, P, P), ("zg", 5, P, P), ("mv1", 6, 32, 32)):
                    s, ws = take(layer, section, 0)
                    z_block(layer, "lora", b, 0, ws, cols, m)
                    pe.drain().then_inc(used[s], 1)

                with pe.Fori(0, KB) as m:
                    pe.wait_ge(lora_ready, layer * 4 + 4)
                    s, ws = take(layer, "rwkv", 0, m, 4)
                    for b, k in ((3, 0), (4, 1), (5, 2)):
                        open_(layer, "rwkv", b, m)
                        rows = 32 if b == 5 else P
                        src = mv_in[0:32] if b == 5 else wa_in
                        mm(bank(b), ws[0:rows, k * P:(k + 1) * P], src, start=True, stop=True).then_inc(ready[b], 1)
                    pe.drain().then_inc(used[s], 1)
                    q8 = layer * KB + m
                    for b, k in ((0, 1), (1, 2), (2, 3)):
                        s, ws = take(layer, "rwkv", k, m, 4)
                        z_block(layer, "rwkv", b, m, ws)
                        pe.drain().then_inc(used[s], 1)
                        if b == 1:
                            open_(layer, "rwkv", 6, m)
                            pe.wait_ge(sqk_ready, q8 + 1)
                            mm(bank(6), blk, tmp["sqk"], start=True, stop=True).then_inc(ready[6], 1)
                    open_(layer, "rwkv", 7, m)
                    pe.wait_ge(rk_ready, q8 + 1)
                    mm(bank(7), blk, tmp["rkt"], start=True, stop=True).then_inc(ready[7], 1)

                with pe.Fori(0, NC) as c:
                    pe.wait_ge(bd_zero, layer + 1)
                    qc = layer * NC + c
                    pe.wait_ge(bd_dve, layer * (NC + 1) + (c + 1))
                    pe.wait_ge(bd_act, qc + 1)

                    def pairs(b0, k, per, terms, transpose=False):
                        for hf in HB:
                            b = b0 + hf
                            open_(layer, "scan", b, c * per + k)
                            for j in range(4):
                                pr = 4 * hf + j
                                for e, (l_, r_) in enumerate(terms):
                                    if transpose:
                                        last = nc.tensor.transpose(psum[:, b, j * P:(j + 1) * P], l_[:, pr, :], ident)
                                    else:
                                        last = mm(psum[:, b, j * P:(j + 1) * P], l_[:, pr, :], r_[:, pr, :],
                                                  start=e == 0, stop=e == len(terms) - 1)
                            last.then_inc(ready[b], 1)

                    pairs(0, 0, 7, [(bdb, bda)])
                    pairs(2, 0, 9, [(bda, bdb)])
                    pairs(4, 0, 7, [(bdb, None)], True)
                    pe.wait_ge(bd_pool, qc + 1)
                    pairs(6, 0, 3, [(bdb, bdr)])
                    pairs(2, 1, 9, [(bdk, None)], True)
                    pairs(4, 1, 7, [(bdk, bda)])
                    pairs(6, 1, 3, [(bdk, bdr)])
                    pairs(2, 2, 9, [(bdv, None)], True)
                    pe.wait_ge(gram_ready, qc * 6 + 6)
                    pe.wait_ge(tr_ready, qc * 6 + 6)
                    pe.wait_ge(s_ready, layer * 18 + (c * 2 + 2))
                    pairs(6, 2, 3, [(bda, st), (gak, vt)])
                    for lv in range(2, LEVELS + 1):
                        pe.wait_ge(loff_ready, qc * 5 + (lv - 1))
                        for hf in HB:
                            pe.wait_ge(x_ready, qc * 12 + ((lv - 2) * 2 + hf + 1))
                            b = hf
                            open_(layer, "scan", b, c * 7 + (lv - 1))
                            for j in range(4):
                                pr = 4 * hf + j
                                last = mm(psum[:, b, j * P:(j + 1) * P], loff[:, pr, :], xm[:, pr, :], start=True, stop=True)
                            last.then_inc(ready[b], 1)
                        for hf in HB:
                            pe.wait_ge(a1_ready, qc * 10 + ((lv - 2) * 2 + hf + 1))
                            for b, k, per, l_, r_ in ((2 + hf, lv + 1, 9, xt, a1), (4 + hf, lv, 7, a1, xt)):
                                if b >= 4 and lv == LEVELS:
                                    continue
                                open_(layer, "scan", b, c * per + k)
                                for j in range(4):
                                    pr = 4 * hf + j
                                    last = mm(psum[:, b, j * P:(j + 1) * P], l_[:, pr, :], r_[:, pr, :], start=True, stop=True)
                                last.then_inc(ready[b], 1)
                    pe.wait_ge(x_ready, qc * 12 + 12)
                    pe.wait_ge(rhs_ready, qc * 2 + 2)
                    pairs(0, 6, 7, [(xm, rhs)])
                    pe.wait_ge(u_ready, qc * 2 + 2)
                    pairs(2, 8, 9, [(st, bdr), (um, grb), (vt, grk)])
                    pairs(4, 6, 7, [(bt, um), (kt, vt)])

                pe.wait_ge(y_ready, layer + 1)
                for m in range(KB):
                    open_(layer, "ysum", m)
                    mm(bank(m), blk, fr[:, m, :], start=True, stop=True).then_inc(ready[m], 1)

                def gmlp_v(section):
                    for tb in range(TB):
                        open_(layer, section, tb)
                    for qt in range(4):
                        s, ws = take(layer, section, qt)
                        for tb in range(TB):
                            for kk in range(4):
                                k = 4 * qt + kk
                                last = mm(bank(tb), shifted(k, tb * P, P), ws[:, kk * T:(kk + 1) * T],
                                          start=k == 0, stop=k == 2 * KB - 1)
                            if qt == 3:
                                last.then_inc(ready[tb], 1)
                        pe.drain().then_inc(used[s], 1)

                pe.wait_ge(n_ready, layer * 3 + 2)
                gmlp_v("gvA")
                s, ws = take(layer, "g2", 0)
                for m in range(KB):
                    b = 4 + m % 4
                    open_(layer, "g2", b, m // 4)
                    mm(bank(b), ws[:, m * P:(m + 1) * P], zg_in, start=True, stop=True).then_inc(ready[b], 1)
                pe.drain().then_inc(used[s], 1)
                pe.wait_ge(ysq_ready, layer + 1)
                for m in range(KB):
                    b = 4 + m % 4
                    open_(layer, "ysq", b, m // 4)
                    mm(bank(b), blk, hsq[:, m, :], start=True, stop=True).then_inc(ready[b], 1)
                gmlp_v("gvB")
                pe.wait_ge(ws_ready, layer + 1)

                def spatial(g):
                    b = 2 + g % 2
                    open_(layer, "zu", b, g // 2)
                    for tb in range(TB):
                        last = mm(psum[:, b, tb * P:(tb + 1) * P], gv[:, tb, g * P:(g + 1) * P], wst[:, g, :],
                                  start=True, stop=True)
                    last.then_inc(ready[b], 1)

                def split_part(section, k, part, i, per, b, high, low, start, stop):
                    s, _ = ring(layer, section, k, i, per)
                    at = split(layer, section, 4 * k + part, i, per)
                    hi_w, lo_w = wsplit[:, part % 2, 0, :], wsplit[:, part % 2, 1, :]
                    pe.wait_ge(high_ready, at + 1)
                    for e in range(4):
                        cols_ = slice(e * P, (e + 1) * P)
                        mm(bank(b), hi_w[:, cols_], high(e), start=start and e == 0, stop=False)
                        mm(bank(b), hi_w[:, cols_], low(e), start=False, stop=False)
                    pe.wait_ge(low_ready, at + 1)
                    for e in range(4):
                        last = mm(bank(b), lo_w[:, e * P:(e + 1) * P], high(e), start=False, stop=stop and e == 3)
                        if part == 3 and e == 0:
                            last.then_inc(used[s], 1)
                    if stop:
                        last.then_inc(ready[b], 1)
                        pe.drain().then_inc(split_used, 1)
                    else:
                        last.then_inc(split_used, 1)

                def z_split(stage, b, use_, k, i=0, per=0):
                    open_(layer, stage, b, use_)

                    def row(parts, kk):
                        off = 1 if kk < KB else 0
                        return parts[kk % KB][:, off:off + T]

                    for part in range(4):
                        split_part(stage, k, part, i, per, b, lambda e: row(n1_high, 4 * part + e),
                                   lambda e: row(n1_low, 4 * part + e), part == 0, part == 3)

                pe.wait_ge(n1_low_ready, layer * KB + KB)
                for g in range(KB):
                    z_split("zu", g % 2, g // 2, g)
                    if g == 1:
                        pe.wait_ge(gvn_ready, layer * TB + TB)
                    if g >= 1:
                        spatial(g - 1)
                spatial(KB - 1)

                with pe.Fori(0, KB // 2) as i:
                    for e in range(2):
                        for k in range(2):
                            z_split("mix", 4 * e + k, i, 3 * e + k, i, 6)
                        pe.wait_ge(y_low_ready, layer * (2 * KB) + 2 * KB)
                        for k, high, low in ((0, ya_high, ya_low), (1, yb_high, yb_low)):
                            b = 4 * e + 2 + k
                            open_(layer, "mix", b, i)
                            for hf in range(2):
                                split_part("mix", 3 * e + 2, 2 * k + hf, i, 6, b, lambda o: high[4 * hf + o],
                                           lambda o: low[4 * hf + o], hf == 0, hf == 1)

                def two_blocks(stage, section, count, src, src_ready, value):
                    with pe.Fori(0, count // 4) as i:
                        pe.wait_ge(src_ready, value)
                        for e in range(2):
                            s, ws = take(layer, section, e, i, 2)
                            for o in range(2):
                                b = 2 * e + o
                                open_(layer, stage, b, i)
                                for kk in range(KB):
                                    last = mm(bank(b), ws[:, (o * KB + kk) * P:(o * KB + kk + 1) * P], src(kk),
                                              start=kk == 0, stop=kk == KB - 1)
                                last.then_inc(ready[b], 1)
                            pe.drain().then_inc(used[s], 1)

                def two_blocks_split(section, count):
                    with pe.Fori(0, count // 4) as i:
                        pe.wait_ge(n2_low_ready, layer * KB + KB)
                        for b in range(4):
                            open_(layer, section, b, i)
                            for hf in range(2):
                                split_part(section, b // 2, 2 * (b % 2) + hf, i, 2, b, lambda e: n2_high[4 * hf + e],
                                           lambda e: n2_low[4 * hf + e], hf == 0, hf == 1)

                two_blocks("wout", "wout", KB, lambda kk: merged[:, kk, :], merged_ready, layer * KB + KB)
                norm_sums(layer, "norm2", layer * 2 + 2)

                pe.wait_ge(pt_in, layer * 16 + 16)
                s, ws = take(layer, "plew", 0)
                for m in range(KB):
                    open_(layer, "plew", m)
                    for kk in range(2):
                        last = mm(bank(m), ws[:, kk * D + m * P:kk * D + (m + 1) * P], ptb[:, kk, :],
                                  start=kk == 0, stop=kk == 1)
                    last.then_inc(ready[m], 1)
                pe.drain().then_inc(used[s], 1)
                two_blocks_split("pleg", KB)
                two_blocks_split("wq", 2 * HEADS)
                pe.wait_ge(q_ready, layer * 16 + 16)
                s, ws = take(layer, "keys", 0)
                for tb in range(TB):
                    for e in range(4):
                        open_(layer, "keys", 4 + e, tb)
                        for j in range(4):
                            hp = 4 * e + j
                            last = mm(psum[:, 4 + e, j * P:(j + 1) * P], q[:, hp, tb * P:(tb + 1) * P],
                                      ws[:, hp * P:(hp + 1) * P], start=True, stop=True)
                        last.then_inc(ready[4 + e], 1)
                pe.drain().then_inc(used[s], 1)

                def up(g, j, i):
                    s, ws = take(layer, f"u{g}", j // 2, i, 2)
                    o = j % 2
                    open_(layer, f"h{g}", o, i * 2 + j // 2)
                    for kk in range(KB):
                        last = mm(bank(o), ws[:, (o * KB + kk) * P:(o * KB + kk + 1) * P], n[:, kk, 1:NW],
                                  start=kk == 0, stop=kk == KB - 1)
                    last.then_inc(ready[o], 1)
                    if o == 1:
                        pe.drain().then_inc(used[s], 1)

                def up_split(g, j, i):
                    o = j % 2
                    open_(layer, f"h{g}", o, i * 2 + j // 2)
                    for hf in range(2):
                        split_part(f"u{g}", j // 2, 2 * o + hf, i, 2, o, lambda e: n_high[4 * hf + e],
                                   lambda e: n_low[4 * hf + e], hf == 0, hf == 1)

                def down(g, part, i):
                    b, e = 2 + part // 4, part % 4
                    if e == 0:
                        open_(layer, f"down{g}", b, i)
                    s, ws = take(layer, f"v{g}", part // 2, i, 4)
                    for jj in range(JG // 4):
                        j = e * (JG // 4) + jj
                        at = j % (JG // 2)
                        last = mm(bank(b), ws[:, at * P:(at + 1) * P], gbuf[g % 2][:, j, :], start=j == 0, stop=j == JG - 1)
                    if e == 3:
                        last.then_inc(ready[b], 1)
                    if e % 2 == 1:
                        pe.drain().then_inc(used[s], 1)

                def build(g, e, i, per):
                    b = 6 + e % 2
                    open_(layer, f"build{g}", b, i * (per // 2) + e // 2)
                    for th in range(2):
                        pe.wait_ge(hot_ready, layer * (NG * T // TH) + (i * (2 * per) + (g * T // TH + 2 * e + th + 1)))
                        for j in range(TH):
                            tk = TH * th + j
                            for a in range(PARTS):
                                last = mm(psum[:, b, tk * JG:(tk + 1) * JG], aring[:, tk, :], bring[:, tk, a, :],
                                          start=a == 0, stop=a == PARTS - 1)
                        if th == 0:
                            last.then_inc(hot_used, 1)
                    last.then_inc(ready[b], 1)
                    pe.drain().then_inc(hot_used, 1)

                with pe.Fori(0, JG // 4) as i:
                    for j in range(4):
                        up(0, j, i)
                pe.wait_ge(picks_ready, layer * TB + TB)
                for a in range(3):
                    open_(layer, "idx", 4 + a)
                    for tb in range(TB):
                        last = nc.tensor.transpose(psum[:, 4 + a, tb * P:(tb + 1) * P], picks[:, a, tb * P:(tb + 1) * P], ident)
                    last.then_inc(ready[4 + a], 1)
                with pe.Fori(0, JG // 4) as i:
                    pe.wait_ge(nlow_ready, layer * KB + KB)
                    for e in range(4):
                        build(0, e, i, 4)
                        up_split(1, e, i)
                for g in range(1, NG):
                    with pe.Fori(0, KB // 2) as i:
                        pe.wait_ge(gated, layer * (NG * 32) + g * 32)
                        for e in range(8):
                            build(g, e, i, 8)
                            down(g - 1, e, i)
                    if g + 1 < NG:
                        with pe.Fori(0, JG // 4) as i:
                            for j in range(4):
                                up_split(g + 1, j, i)
                with pe.Fori(0, KB // 2) as i:
                    pe.wait_ge(gated, layer * (NG * 32) + NG * 32)
                    for e in range(8):
                        down(NG - 1, e, i)
            norm_sums(L, "norm1", 2 * L + 1)

        @block.vector
        def _(dve):
            V = nc.vector
            sync = dve.drain

            def norm(layer, stage, count, scale, block_ready=None):
                dve.wait_ge(ready[0], use(layer, stage, 0))
                V.tensor_scalar(rstd, bank(0), 1.0 / D, RMS_EPS, ALU.mult, ALU.add).then_inc(free[0], 1)
                dve.wait_ge(rms_ready, count)
                V.reciprocal(rstd, rstd)
                sync()
                scaled(scale, block_ready)

            def scaled(scale, block_ready=None):
                V.memset(n[:, :, 0:1], 0.0)
                for k in range(KB):
                    last = V.scalar_tensor_tensor(n[:, k, 1:NW], h[:, k, :], vcol(scale, k), rstd, ALU.mult, ALU.mult)
                    if block_ready and k < KB - 1:
                        last.then_inc(block_ready, 1)
                last.then_inc(n_ready, 1)

            dve.wait_ge(x_in, 16)
            dve.wait_ge(const_in, 16)
            dve.sem_inc(fields_ready, 1)
            dve.sem_inc(hot_used, 2)
            dve.sem_inc(pg_used, 2)
            V.drain().then_inc(h_ready, KB)
            with dve.Fori(0, L) as layer:
                dve.wait_ge(vec_in, layer * 16 + 16)
                norm(layer, "norm1", layer * 2 + 1, "norm_mix")

                with dve.Fori(0, KB) as m:
                    q8 = layer * KB + m

                    def got(b):
                        dve.wait_ge(ready[b], use(layer, "rwkv", b, m))

                    t_ = tmp
                    dve.wait_ge(free[5], use(layer, "rwkv", 5, m + 1))
                    V.tensor_tensor_scan(t_["s"], cc("reset"), t_["sg"], 0.0, ALU.mult, ALU.add)
                    sync()
                    V.tensor_tensor(t_["se"], t_["s"], t_["sg"], ALU.subtract).then_inc(cum_ready, 1)
                    V.tensor_scalar(t_["t"], t_["ar"], -1.0, vcol("ka", m), ALU.add, ALU.mult)
                    got(0)
                    V.tensor_scalar(t_["kkr"], bank(0), vcol("kk", m), None, ALU.mult).then_inc(kkr_ready, 1)
                    sync()
                    V.scalar_tensor_tensor(t_["k"], t_["t"], 1.0, bank(0), ALU.add, ALU.mult).then_inc(free[0], 1)
                    got(1)
                    V.tensor_copy(t_["zv"], bank(1)).then_inc(free[1], 1)
                    got(6)
                    V.tensor_scalar(t_["rn"], bank(6), 1e-24, None, ALU.max).then_inc(free[6], 1)
                    dve.wait_ge(rn_ready, q8 + 1)
                    V.reciprocal(t_["rn"], t_["rn"])
                    sync()
                    V.tensor_tensor(t_["kkr"], t_["kkr"], t_["rn"], ALU.mult)
                    sync()
                    dve.wait_ge(p_ready, q8 + 1)
                    V.scalar_tensor_tensor(fa[:, ds(m, 1), :], t_["kkr"], -1.0, t_["pexc"], ALU.mult, ALU.mult)
                    V.tensor_tensor(t_["b"], t_["kkr"], t_["ar"], ALU.mult)
                    V.tensor_tensor(fk[:, ds(m, 1), :], t_["k"], t_["pinv"], ALU.mult)
                    sync()
                    V.tensor_tensor(fb[:, ds(m, 1), :], t_["b"], t_["pinv"], ALU.mult)
                    got(2)
                    V.scalar_tensor_tensor(t_["rkt"], bank(2), vcol("rk", m), t_["k"], ALU.mult, ALU.mult).then_inc(rk_ready, 1)
                    V.tensor_tensor(fr[:, ds(m, 1), :], bank(2), t_["pinc"], ALU.mult).then_inc(free[2], 1)
                    dve.wait_ge(vf_in, q8 * 16 + 16)
                    V.tensor_tensor(t_["vf"], t_["vf"], t_["zv"], ALU.subtract)
                    sync()
                    V.tensor_tensor(t_["vf"], t_["vf"], t_["vm"], ALU.mult)
                    sync()
                    V.tensor_tensor(fv[:, ds(m, 1), :], t_["zv"], t_["vf"], ALU.add)
                    sync()
                    got(7)
                    V.tensor_tensor(fbon[:, ds(m, 1), :], bank(7), fv[:, ds(m, 1), :], ALU.mult).then_inc(free[7], 1)
                    V.tensor_copy(pend[:, ds(m, 1), :], t_["pinc"].rearrange("p (c t) -> p c t", t=CH)[:, :, CH - 1:CH].rearrange("p c o -> p o c"))
                    V.drain().then_inc(fields_ready, 1)

                dve.wait_ge(ready[7], use(layer, "rwkv", 7, KB - 1))
                for t_ in (bda, bdr, bdb, bdk, bdv):
                    V.memset(t_, 0.0)
                V.drain().then_inc(bd_zero, 1)
                for hf in HB:
                    V.memset(half(st, hf), 0.0).then_inc(s_ready, 1)

                def stage_a(chunk):
                    flat_a = ar.at(fields[0], KB * T + T)
                    for e in range(2):
                        r = slice(e * CH, (e + 1) * CH)
                        src = flat_a[r, ds(chunk * CH, KB * T)].rearrange("p (a t) -> p a t", a=KB)[:, :, 0:CH]
                        last = V.tensor_copy(bda[r, :, e * CH:(e + 1) * CH], src)
                    last.then_inc(bd_dve, 1)

                stage_a(0)
                with dve.Fori(0, NC) as c:
                    qc = layer * NC + c

                    def got(b, k, per):
                        dve.wait_ge(ready[b], use(layer, "scan", b, c * per + k))

                    def wide(name, i=0, width=None):
                        m_ = cc(name, i, width)
                        return m_.rearrange("p (o c) -> p o c", o=1).broadcast_to([P, 4, P])

                    for hf in HB:
                        got(6 + hf, 0, 3)
                        V.tensor_tensor(half(grb, hf), bank4(6 + hf), wide("upd"), ALU.mult).then_inc(gram_ready, 1)
                        V.drain().then_inc(free[6 + hf], 1)
                    for hf in HB:
                        got(hf, 0, 7)
                        V.tensor_tensor(half(xm, hf), bank4(hf), wide("lvlN"), ALU.mult).then_inc(free[hf], 1)
                    sync()
                    for hf in HB:
                        V.tensor_tensor(half(xm, hf), half(xm, hf), wide("ident"), ALU.add)
                    for b0, k, per, dst, mask in ((4, 1, 7, gak, "up"), (6, 1, 3, grk, "upd")):
                        for hf in HB:
                            got(b0 + hf, k, per)
                            V.tensor_tensor(half(dst, hf), bank4(b0 + hf), wide(mask), ALU.mult).then_inc(gram_ready, 1)
                            V.drain().then_inc(free[b0 + hf], 1)
                    dve.wait_ge(l_ready, qc * 2 + 2)
                    got(3, 1, 9)
                    for hf in HB:
                        V.tensor_tensor(half(xt, hf), half(lt, hf), wide("lvl", 0, P), ALU.mult)
                    sync()
                    for hf in HB:
                        V.tensor_tensor(half(xt, hf), half(xt, hf), wide("ident"), ALU.add).then_inc(x_ready, 1)
                    for lv in range(2, LEVELS + 1):
                        for hf in HB:
                            got(2 + hf, lv + 1, 9)
                            if lv < LEVELS:
                                got(4 + hf, lv, 7)
                            up_x = V.tensor_tensor(half(xm, hf), half(xm, hf), bank4(2 + hf), ALU.add)
                            up_x.then_inc(free[2 + hf], 1)
                            if lv < LEVELS:
                                V.tensor_tensor(half(xt, hf), half(xt, hf), bank4(4 + hf), ALU.add).then_inc(free[4 + hf], 1)
                            V.drain().then_inc(x_ready, 1)
                    for hf in HB:
                        got(2 + hf, 8, 9)
                        for e in range(2):
                            r = slice(e * CH, (e + 1) * CH)
                            last = V.tensor_copy(fr[r, 4 * hf:4 * hf + 4, ts(c, CH)], bank4(2 + hf)[r, :, e * CH:(e + 1) * CH])
                        last.then_inc(free[2 + hf], 1)
                    stage_a(c + 1)
                    for hf in HB:
                        got(4 + hf, 6, 7)
                        V.tensor_tensor(half(st, hf), half(st, hf), bank4(4 + hf), ALU.add).then_inc(free[4 + hf], 1)
                    sync()
                    for hf in HB:
                        V.tensor_tensor(half(st, hf), half(st, hf), pend[:, 4 * hf:4 * hf + 4, ds(c, 1)].broadcast_to([P, 4, P]),
                                        ALU.mult).then_inc(s_ready, 1)

                V.drain().then_inc(y_ready, 1)
                scaled("norm_mix")
                for b in range(8):
                    dve.wait_ge(ready[b], use(layer, "ysum", b))
                    V.scalar_tensor_tensor(yc[:, b, :], bank(b), -1.0 / CH, fr[:, b, :], ALU.mult, ALU.add).then_inc(free[b], 1)
                V.drain().then_inc(yc_ready, 1)
                for m in range(KB):
                    b = 4 + m % 4
                    dve.wait_ge(ready[b], use(layer, "ysq", b, m // 4))
                    V.tensor_scalar(yvar[:, m, :], bank(b), 1.0 / CH, RW_EPS, ALU.mult, ALU.add).then_inc(free[b], 1)
                V.drain().then_inc(yvar_ready, 1)
                dve.wait_ge(ysd_ready, layer + 1)
                V.reciprocal(yvar, yvar)
                sync()
                V.tensor_tensor(yc, yc, yvar, ALU.mult)
                sync()
                for m in range(KB):
                    V.tensor_scalar(yc[:, m, :], yc[:, m, :], vcol("ln_g", m), vcol("ln_b", m), ALU.mult, ALU.add)
                sync()
                V.tensor_tensor(yc, yc, fbon, ALU.add)
                sync()
                dve.wait_ge(ygate_ready, layer + 1)
                V.tensor_tensor(fr, yc, ygate, ALU.mult).then_inc(ya_ready, 1)
                for k in range(KB):
                    dve.wait_ge(n1_high_ready, layer * KB + (k + 1))
                    V.tensor_tensor(n1_low[k], n[:, k, :], n1_high[k].bitcast(F32), ALU.subtract).then_inc(n1_low_ready, 1)

                for tb in range(TB):
                    dve.wait_ge(gelu_v, layer * 8 + (5 + tb))
                    for hf in HB:
                        V.bn_stats(stats[:, tb, hf, :], gv[:, tb, hf * T:(hf + 1) * T])
                    sync()
                    V.bn_aggr(mv2[:, tb, :], stats[:, tb, :, :])
                    sync()
                    last = V.tensor_scalar(lrs[:, tb:tb + 1], mv2[:, tb, 1:2], GM_EPS, None, ALU.add)
                last.then_inc(gvar_ready, 1)
                dve.wait_ge(gsd_ready, layer + 1)
                dve.wait_ge(gm_in, layer * 16 + 16)
                V.reciprocal(lrs, lrs)
                sync()
                for tb in range(TB):
                    V.scalar_tensor_tensor(gv[:, tb, :], gv[:, tb, :], mv2[:, tb, 0:1], lng, ALU.subtract, ALU.mult)
                sync()
                for tb in range(TB):
                    V.scalar_tensor_tensor(gv[:, tb, :], gv[:, tb, :], lrs[:, tb:tb + 1], lnb, ALU.mult, ALU.add).then_inc(gvn_ready, 1)
                for g in range(KB):
                    b = 2 + g % 2
                    dve.wait_ge(ready[b], use(layer, "zu", b, g // 2))
                    V.tensor_tensor(spt[:, g % 2, :].rearrange("p (b t) -> p b t", b=TB), bank4(b),
                                    bsb[:, g:g + 1, :].broadcast_to([P, TB, P]), ALU.add).then_inc(free[b], 1)
                    sync()
                    dve.wait_ge(ug_ready, layer * KB + (g + 1))
                    V.tensor_tensor(yb[:, g, :], spt[:, g % 2, :], ut[:, g % 2, :], ALU.mult).then_inc(yb_ready, 1)

                for k in range(KB):
                    dve.wait_ge(ya_high_ready, layer * KB + (k + 1))
                    V.tensor_tensor(ya_low[k], fr[:, k, :], ya_high[k].bitcast(F32), ALU.subtract).then_inc(y_low_ready, 1)
                for k in range(KB):
                    dve.wait_ge(yb_high_ready, layer * KB + (k + 1))
                    V.tensor_tensor(yb_low[k], yb[:, k, :], yb_high[k].bitcast(F32), ALU.subtract).then_inc(y_low_ready, 1)

                with dve.Fori(0, KB // 2) as i:
                    for e in range(2):
                        sync()
                        dve.wait_ge(gate_ready, layer * (2 * KB) + (i * 4 + (2 * e + 2)))
                        for k in range(2):
                            b = 4 * e + 2 + k
                            dve.wait_ge(ready[b], use(layer, "mix", b, i))
                            V.tensor_tensor(mixed[:, 2 * e + k, :], gates[:, 2 * e + k, :], bank(b), ALU.mult).then_inc(free[b], 1)
                        sync()
                        V.tensor_tensor(merged[:, ds(i * 2 + e, 1), :], mixed[:, 2 * e, :], mixed[:, 2 * e + 1, :], ALU.add).then_inc(merged_ready, 1)

                with dve.Fori(0, 2) as i:
                    for b in range(4):
                        dve.wait_ge(ready[b], use(layer, "wout", b, i))
                        hm = h[:, ds(i * 4 + b, 1), :]
                        V.tensor_tensor(hm, hm, bank(b), ALU.add).then_inc(free[b], 1)
                        V.drain().then_inc(h_ready, 1)
                norm(layer, "norm2", layer * 2 + 2, "norm_ffn", n2_block)
                for k in range(KB):
                    dve.wait_ge(n2_high_ready, layer * KB + (k + 1))
                    V.tensor_tensor(n2_low[k], n[:, k, 1:NW], n2_high[k].bitcast(F32), ALU.subtract).then_inc(n2_low_ready, 1)

                with dve.Fori(0, 2) as i:
                    dve.wait_ge(pp_ready, layer + 1)
                    for b in range(4):
                        dve.wait_ge(pg_ready, layer * KB + (i * 4 + (b + 1)))
                        V.tensor_tensor(pmul[:, b % 2, :], pgb[:, b % 2, :], ppb[:, ds(i * 4 + b, 1), :], ALU.mult).then_inc(pg_used, 1)
                        sync()
                        hm = h[:, ds(i * 4 + b, 1), :]
                        V.tensor_tensor(hm, hm, pmul[:, b % 2, :], ALU.add)
                        sync()
                V.drain().then_inc(ple_added, 1)

                def top16(rows, wide_, spare, vals, inds, width):
                    for rnd in range(2):
                        src = spare if rnd else wide_
                        r8 = slice(8 * rnd, 8 * rnd + 8)
                        for a in range(rows):
                            V.max(vals[:, a, r8], src[:, a * width:(a + 1) * width])
                        sync()
                        for a in range(rows):
                            V.max_index(inds[:, a, r8], vals[:, a, r8], src[:, a * width:(a + 1) * width])
                            if rnd == 0:
                                V.match_replace(spare[:, a * width:(a + 1) * width], vals[:, a, r8],
                                                src[:, a * width:(a + 1) * width], LOWEST)
                        sync()

                with dve.Fori(0, TB) as tb:
                    dve.wait_ge(sc_ready, layer * 16 + 16)
                    V.tensor_copy(sw.rearrange("p a b -> p (a b)"), sc[:, ds(tb, 1), :].rearrange("p o b -> p (o b)"))
                    sync()
                    flat = lambda t__: t__.rearrange("p a b -> p (a b)")
                    top16(NH, flat(sw), flat(sx), tv, ti.bitcast(U32), P)
                    V.tensor_copy(flat(tif), flat(ti).bitcast(U32))
                    pair = tv.rearrange("p (h c) k -> p h c k", c=2)
                    V.tensor_tensor(flat(cand).rearrange("p (h a b) -> p h a b", h=HEADS, a=TOPK),
                                    pair[:, :, 0, :].rearrange("p h (k o) -> p h k o", o=1).broadcast_to([P, HEADS, TOPK, TOPK]),
                                    pair[:, :, 1, :].rearrange("p h (o k) -> p h o k", o=1).broadcast_to([P, HEADS, TOPK, TOPK]), ALU.add)
                    sync()
                    top16(HEADS, flat(cand), flat(cand2), bv, bp.bitcast(U32), TOPK * TOPK)
                    pw = pick[:, 2, :].rearrange("p (h k) -> p h k", h=HEADS)
                    V.tensor_tensor(pw, bv, bv[:, :, 0:1].broadcast_to([P, HEADS, TOPK]), ALU.subtract)
                    V.drain().then_inc(ex_in, 1)
                    V.tensor_scalar(bq[:, 0, :].bitcast(U32), flat(bp).bitcast(U32), 4, None, ALU.logical_shift_right)
                    V.tensor_scalar(bq[:, 1, :].bitcast(U32), flat(bp).bitcast(U32), 15, None, ALU.bitwise_and)
                    sync()
                    V.tensor_copy(flat(bqf), flat(bq).bitcast(U32))
                    sync()
                    tpair = tif.rearrange("p (h c) k -> p h c k", c=2)
                    NHK = HEADS * TOPK
                    for cpt in range(2):
                        e3 = flat(eq).rearrange("p (a b) -> p a b", a=NHK)
                        V.tensor_tensor(e3, bqf[:, cpt, :].rearrange("p (a o) -> p a o", o=1).broadcast_to([P, NHK, TOPK]),
                                        cc("iota")[:, 0:TOPK].rearrange("p (o a) -> p o a", o=1).broadcast_to([P, NHK, TOPK]), ALU.is_equal)
                        sync()
                        e4 = flat(eq).rearrange("p (h a b) -> p h a b", h=HEADS, a=TOPK)
                        V.tensor_tensor(e4, e4, tpair[:, :, cpt, :].rearrange("p h (o k) -> p h o k", o=1).broadcast_to([P, HEADS, TOPK, TOPK]), ALU.mult)
                        sync()
                        V.tensor_reduce(pick[:, cpt, :], e3, AXX, ALU.add)
                        sync()
                    dve.wait_ge(ex_out, layer * TB + tb + 1)
                    V.tensor_reduce(hsum, pw, AXX, ALU.add)
                    sync()
                    V.reciprocal(hrec, hsum)
                    sync()
                    V.tensor_tensor(pw, pw, hrec.rearrange("p (h o) -> p h o", o=1).broadcast_to([P, HEADS, TOPK]), ALU.mult)
                    sync()
                    V.tensor_copy(picks[:, :, ts(tb, P)], pick).then_inc(picks_ready, 1)
                    sync()
                for a in range(3):
                    dve.wait_ge(ready[4 + a], use(layer, "idx", 4 + a))
                    V.tensor_copy(idx[:, a, :], bank(4 + a)).then_inc(free[4 + a], 1)
                sync()
                left = idx[:, 2, :]
                for a in range(PARTS):
                    V.tensor_copy(wparts[:, a, :], left)
                    sync()
                    if a + 1 < PARTS:
                        V.tensor_tensor(wrest, left, wparts[:, a, :], ALU.subtract)
                        sync()
                    left = wrest

                def build(g, e, i, per):
                    at = i * (per * TG) + e * TG
                    for th in range(2):
                        tok = at + th * TH
                        rows_ = slice(th * TH, (th + 1) * TH)

                        def col(a, width):
                            return idx[:, a, ds(tok, TH)].rearrange("p (t o) -> p t o", o=1).broadcast_to([P, TH, width])

                        weight = wparts[:, :, ds(tok, TH)].rearrange("p a (t o) -> p t a o", o=1).broadcast_to([P, TH, PARTS, JG])
                        hot = bhot[:, rows_, :].rearrange("p t (o k) -> p t o k", o=1).broadcast_to([P, TH, PARTS, JG])

                        def count_to(lo_, width):
                            return cc("iota")[:, lo_:lo_ + width].rearrange("p (o a) -> p o a", o=1).broadcast_to([P, TH, width])

                        dve.wait_ge(hot_used, layer * (NG * T // TH) + (i * (2 * per) + (g * T // TH + 2 * e + th + 1)))
                        V.tensor_tensor(bhot[:, rows_, :], count_to(g * JG, JG), col(1, JG), ALU.is_equal)
                        V.tensor_tensor(aring[:, rows_, :], count_to(0, P), col(0, P), ALU.is_equal)
                        sync()
                        V.tensor_tensor(bring[:, rows_, :, :], hot, weight, ALU.mult).then_inc(hot_ready, 1)

                def gate(g, e, i, per):
                    b = 6 + e % 2
                    dve.wait_ge(act_ready, layer * P + (g + 1) * JG)
                    dve.wait_ge(ready[b], use(layer, f"build{g}", b, i * (per // 2) + e // 2))
                    part = gbuf[g % 2][:, :, ds(i * (per * TG) + e * TG, TG)]
                    V.tensor_tensor(part, part, bank(b).rearrange("p (t j) -> p j t", j=JG), ALU.mult).then_inc(free[b], 1)
                    V.drain().then_inc(gated, 1)

                def add_down(g, e, i):
                    b = 2 + e
                    if g < 2:
                        dve.wait_ge(hblk_in[e], (layer * 8 + (i + (g * 4 + 1))) * 16)
                        dve.wait_ge(ready[b], use(layer, f"down{g}", b, i))
                        V.tensor_tensor(hblk[e], hblk[e], bank(b), ALU.add).then_inc(free[b], 1)
                        V.drain().then_inc(hblk_added[e], 1)
                        return
                    dve.wait_ge(h_back, layer * 16 + 16)
                    if g + 1 == NG:
                        dve.wait_ge(masks_back, layer * 16 + 16)
                    dve.wait_ge(ready[b], use(layer, f"down{g}", b, i))
                    hm = h[:, ds(i * 2 + e, 1), :]
                    V.tensor_tensor(hm, hm, bank(b), ALU.add).then_inc(free[b], 1)

                with dve.Fori(0, JG // 4) as i:
                    for e in range(5):
                        if e < 4:
                            build(0, e, i, 4)
                        if e > 0:
                            gate(0, e - 1, i, 4)
                for g in range(1, NG):
                    with dve.Fori(0, KB // 2) as i:
                        for e in range(9):
                            if e < 8:
                                build(g, e, i, 8)
                            if e > 0:
                                gate(g, e - 1, i, 8)
                            if e in (5, 8):
                                add_down(g - 1, e // 8, i)
                    sync()
                with dve.Fori(0, KB // 2) as i:
                    for e in range(2):
                        add_down(NG - 1, e, i)
                        V.drain().then_inc(h_ready, 1)
            norm(L, "norm1", 2 * L + 1, "final")

        @block.scalar
        def _(act):
            A = nc.scalar.activation
            sync = act.drain

            def squares(count, layer, stage):
                for k in range(KB):
                    act.wait_ge(h_ready, (count - 1) * KB + (k + 1))
                    A(squared[:, k, :], h[:, k, :], ACT.Square).then_inc(sq_ready, 1)
                act.wait_ge(free[0], use(layer, stage, 0, 1))
                A(rstd, rstd, ACT.Sqrt).then_inc(rms_ready, 1)

            act.wait_ge(x_in, 16)
            with act.Fori(0, L) as layer:
                act.dma_start(vecs, vec[ds(act.snap(layer), 1), :, :]).then_inc(vec_in, 16)
                squares(layer * 2 + 1, layer, "norm1")
                act.wait_ge(vec_in, layer * 16 + 16)
                act.wait_ge(ready[4], use(layer, "lora", 4))
                A(wa_in[0:CH], psum[0:CH, 4, :], ACT.Tanh).then_inc(lora_ready, 1)
                A(wa_in[CH:P], psum[CH:P, 4, :], ACT.Copy).then_inc(free[4], 1)
                act.wait_ge(ready[5], use(layer, "lora", 5))
                A(zg_in, bank(5), ACT.Sigmoid).then_inc(free[5], 1)
                act.wait_ge(ready[6], use(layer, "lora", 6))
                A(mv_in[0:32], psum[0:32, 6, :], ACT.Copy).then_inc(free[6], 1)
                act.drain().then_inc(lora_ready, 3)

                with act.Fori(0, KB) as m:
                    q8 = layer * KB + m
                    act.wait_ge(fields_ready, q8 + 1)
                    for b, dst, bias in ((3, "sg", "w0"), (4, "ar", "a0"), (5, "vm", "v0")):
                        act.wait_ge(ready[b], use(layer, "rwkv", b, m))
                        A(tmp[dst], bank(b), ACT.Sigmoid, bias=vcol(bias, m)).then_inc(free[b], 1)
                    act.wait_ge(cum_ready, q8 + 1)
                    A(tmp["pinc"], tmp["s"], ACT.Exp, scale=-DECAY)
                    A(tmp["pinv"], tmp["s"], ACT.Exp, scale=DECAY)
                    A(tmp["pexc"], tmp["se"], ACT.Exp, scale=-DECAY).then_inc(p_ready, 1)
                    act.wait_ge(kkr_ready, q8 + 1)
                    A(tmp["sqk"], tmp["kkr"], ACT.Square).then_inc(sqk_ready, 1)
                    act.wait_ge(free[6], use(layer, "rwkv", 6, m + 1))
                    A(tmp["rn"], tmp["rn"], ACT.Sqrt).then_inc(rn_ready, 1)

                act.wait_ge(fields_ready, layer * KB + (KB + 1))
                act.wait_ge(bd_zero, layer + 1)
                with act.Fori(0, NC) as c:
                    qc = layer * NC + c

                    def got(b, k, per):
                        act.wait_ge(ready[b], use(layer, "scan", b, c * per + k))

                    for src, dst in ((fb, bdb), (fk, bdk)):
                        for e in range(2):
                            r = slice(e * CH, (e + 1) * CH)
                            last = A(dst[r, :, e * CH:(e + 1) * CH], src[r, :, ts(c, CH)], ACT.Copy)
                    last.then_inc(bd_act, 1)
                    for hf in HB:
                        got(2 + hf, 0, 9)
                        A(half(lt, hf), bank4(2 + hf), ACT.Copy).then_inc(free[2 + hf], 1)
                    act.drain().then_inc(l_ready, 2)
                    for b0, k, per, dst in ((4, 0, 7, bt), (2, 1, 9, kt), (2, 2, 9, vt)):
                        for hf in HB:
                            got(b0 + hf, k, per)
                            A(half(dst, hf), bank4(b0 + hf), ACT.Copy).then_inc(free[b0 + hf], 1)
                    act.drain().then_inc(tr_ready, 6)
                    for hf in HB:
                        got(6 + hf, 2, 3)
                        A(half(rhs, hf), bank4(6 + hf), ACT.Copy).then_inc(free[6 + hf], 1)
                    act.drain().then_inc(rhs_ready, 2)
                    for lv in range(2, LEVELS + 1):
                        for hf in HB:
                            got(hf, lv - 1, 7)
                            A(half(a1, hf), bank4(hf), ACT.Copy).then_inc(free[hf], 1)
                            act.drain().then_inc(a1_ready, 1)
                    for hf in HB:
                        got(hf, 6, 7)
                        A(half(um, hf), bank4(hf), ACT.Copy).then_inc(free[hf], 1)
                    act.drain().then_inc(u_ready, 2)

                act.wait_ge(y_ready, layer + 1)
                act.dma_start(gmp, gm[ds(act.snap(layer), 1), :, :]).then_inc(gm_in, 16)

                def gelu_half(hf, section):
                    for tb in range(TB):
                        act.wait_ge(ready[tb], use(layer, section, tb))
                        A(gv[:, tb, hf * T:(hf + 1) * T], bank(tb), ACT.Gelu_apprx_tanh).then_inc(free[tb], 1)
                        act.drain().then_inc(gelu_v, 1)

                act.wait_ge(yc_ready, layer + 1)
                A(hsq, yc, ACT.Square).then_inc(ysq_ready, 1)
                gelu_half(0, "gvA")
                for m in range(KB):
                    b = 4 + m % 4
                    act.wait_ge(ready[b], use(layer, "g2", b, m // 4))
                    A(ygate[:, m, :], bank(b), ACT.Copy).then_inc(free[b], 1)
                act.drain().then_inc(ygate_ready, 1)
                act.wait_ge(yvar_ready, layer + 1)
                A(yvar, yvar, ACT.Sqrt).then_inc(ysd_ready, 1)

                def high_part(section, k, part, i=0, per=0):
                    s, count = ring(layer, section, k, i, per)
                    act.wait_ge(landed[s], count * 16)
                    act.wait_ge(split_used, split(layer, section, 4 * k + part, i, per) + 1)
                    A(wsplit[:, part % 2, 0, :], slots[:, s, part * QT:(part + 1) * QT], ACT.Copy).then_inc(high_ready, 1)

                def high_parts(section, col, i):
                    for hf in range(2):
                        high_part(section, col // 2, 2 * (col % 2) + hf, i, 2)

                def high_ahead(section, k, i=0, per=0, after=None):
                    for part in (2, 3):
                        high_part(section, k, part, i, per)
                    if after:
                        for part in (0, 1):
                            high_part(*after[:2], part, *after[2:])

                act.wait_ge(ws_ready, layer + 1)
                act.wait_ge(ya_ready, layer + 1)
                for k in range(KB):
                    A(n1_high[k], n[:, k, :], ACT.Copy).then_inc(n1_high_ready, 1)
                for part in (0, 1):
                    high_part("zu", 0, part)
                gelu_half(1, "gvB")
                act.wait_ge(gvar_ready, layer + 1)
                A(lrs, lrs, ACT.Sqrt).then_inc(gsd_ready, 1)
                for g in range(KB):
                    b = g % 2
                    high_ahead("zu", g, after=("zu", g + 1) if g + 1 < KB else ("mix", 0, 0, 6))
                    act.wait_ge(ready[b], use(layer, "zu", b, g // 2))
                    if g >= 2:
                        act.wait_ge(yb_ready, layer * KB + (g - 1))
                    A(ut[:, b, :], bank(b), ACT.Gelu_apprx_tanh).then_inc(free[b], 1)
                    act.drain().then_inc(ug_ready, 1)
                    if g >= 2:
                        A(yb_high[g - 2], yb[:, g - 2, :], ACT.Copy).then_inc(yb_high_ready, 1)
                    if 2 <= g < 6:
                        if g == 2:
                            act.wait_ge(n1_low_ready, layer * KB + KB)
                        for k in (2 * (g - 2), 2 * (g - 2) + 1):
                            A(ya_high[k], fr[:, k, :], ACT.Copy).then_inc(ya_high_ready, 1)
                for k in (KB - 2, KB - 1):
                    act.wait_ge(yb_ready, layer * KB + (k + 1))
                    A(yb_high[k], yb[:, k, :], ACT.Copy).then_inc(yb_high_ready, 1)

                def gate_slots(i, last):
                    for e in range(2):
                        for k in range(3):
                            at = 3 * e + k
                            high_ahead("mix", at, i, 6, None if last and at == 5 else ("mix", at + 1, i, 6))
                            if k == 2:
                                continue
                            b = 4 * e + k
                            act.wait_ge(ready[b], use(layer, "mix", b, i))
                            act.wait_ge(free[4 * e + 2 + k], use(layer, "mix", 4 * e + 2 + k, i))
                            A(gates[:, 2 * e + k, :], bank(b), ACT.Sigmoid).then_inc(free[b], 1)
                            act.drain().then_inc(gate_ready, 1)

                with act.Fori(0, KB // 2 - 1) as i:
                    gate_slots(i, False)
                gate_slots(KB // 2 - 1, True)
                act.dma_start(ptb, pt[ds(act.snap(layer), 1), :, :].rearrange("o p (k t) -> (o p) k t", k=2)).then_inc(pt_in, 16)
                squares(layer * 2 + 2, layer, "norm2")

                for k in range(KB):
                    if k < KB - 1:
                        act.wait_ge(n2_block, layer * (KB - 1) + (k + 1))
                    else:
                        act.wait_ge(n_ready, layer * 3 + 3)
                    A(n2_high[k], n[:, k, 1:NW], ACT.Copy).then_inc(n2_high_ready, 1)
                    if k == 3:
                        high_parts("pleg", 0, 0)
                    act.wait_ge(ready[k], use(layer, "plew", k))
                    A(ppb[:, k, :], bank(k), ACT.Copy).then_inc(free[k], 1)
                act.drain().then_inc(pp_ready, 1)
                for i in range(2):
                    for b in range(4):
                        if i == 0 or b < 3:
                            high_parts("pleg", b + 1, i)
                        else:
                            high_parts("wq", 0, 0)
                        act.wait_ge(ready[b], use(layer, "pleg", b, i))
                        act.wait_ge(pg_used, layer * 8 + (i * 4 + (b + 1)))
                        A(pgb[:, b % 2, :], bank(b), ACT.Sigmoid).then_inc(free[b], 1)
                        act.drain().then_inc(pg_ready, 1)

                def query(i, b):
                    act.wait_ge(ready[b], use(layer, "wq", b, i))
                    A(q[:, ds(i * 4 + b, 1), :], bank(b), ACT.Copy).then_inc(free[b], 1)

                with act.Fori(0, 3) as i:
                    for b in range(4):
                        high_parts("wq", b + 1, i)
                        query(i, b)
                act.wait_ge(ple_added, layer + 1)
                act.dma_start(hdram[ds(act.snap(layer * KB), KB), :, :].rearrange("m p t -> p m t"), h).then_inc(h_out, 16)
                for b in range(4):
                    if b < 3:
                        high_parts("wq", b + 1, 3)
                    query(3, b)
                act.drain().then_inc(q_ready, 16)
                for tb in range(TB):
                    for e in range(4):
                        act.wait_ge(ready[4 + e], use(layer, "keys", 4 + e, tb))
                        A(sc[:, tb, e * T:(e + 1) * T], bank(4 + e), ACT.Copy).then_inc(free[4 + e], 1)
                act.drain().then_inc(sc_ready, 16)

                def expert(g, j, i):
                    o = j % 2
                    act.wait_ge(ready[o], use(layer, f"h{g}", o, i * 2 + j // 2))
                    A(gbuf[g % 2][:, ds(i * 4 + j, 1), :], bank(o), ACT.Gelu_apprx_tanh).then_inc(free[o], 1)

                act.wait_ge(h_out, layer * 16 + 16)
                for k in range(KB):
                    A(n_high[k], n[:, k, 1:NW], ACT.Copy).then_inc(nhigh_ready, 1)
                act.wait_ge(pg_used, layer * 8 + 10)
                with act.Fori(0, TB) as tb:
                    for e in range(JG // 4 // TB):
                        for j in range(4):
                            expert(0, j, tb * (JG // 4 // TB) + e)
                    act.wait_ge(ex_in, layer * TB + tb + 1)
                    A(pick[:, 2, :], pick[:, 2, :], ACT.Exp).then_inc(ex_out, 1)
                act.drain().then_inc(act_ready, JG)

                def experts(g, i, more):
                    for j in range(4):
                        if more or j < 3:
                            high_parts(f"u{g}", j + 1, i)
                        expert(g, j, i)

                def h_row(m):
                    return hdram[ds(act.snap(layer * KB + m), 1), :, :]

                def fetch(e, m):
                    act.dma_start(hblk[e], h_row(m)).then_inc(hblk_in[e], 16)

                def store(g, e, i):
                    act.wait_ge(hblk_added[e], layer * 8 + (i + (g * 4 + 1)))
                    act.dma_start(h_row(i * 2 + e), hblk[e]).then_inc(hblk_out[e], 16)

                for g in range(1, NG):
                    if g == 1:
                        high_parts("u1", 0, 0)
                        act.wait_ge(free[6], use(layer, "idx", 6, 1))
                    with act.Fori(0, JG // 4 - 1) as i:
                        experts(g, i, True)
                    experts(g, JG // 4 - 1, False)
                    act.drain().then_inc(act_ready, JG)
                    if g + 1 == NG:
                        break
                    if g == 1:
                        act.wait_ge(hot_ready, layer * (NG * T // TH) + 1)
                    for e in range(2):
                        if g > 1:
                            act.wait_ge(hblk_out[e], (layer * 8 + (g - 1) * 4) * 16)
                        fetch(e, e)
                    with act.Fori(0, KB // 2 - 1) as i:
                        for e in range(2):
                            store(g - 1, e, i)
                            act.wait_ge(hblk_out[e], (layer * 8 + (i + ((g - 1) * 4 + 1))) * 16)
                            fetch(e, i * 2 + (e + 2))
                    high_parts(f"u{g + 1}", 0, 0)
                    for e in range(2):
                        store(g - 1, e, KB // 2 - 1)
                for e in range(2):
                    act.wait_ge(hblk_out[e], (layer * 8 + 8) * 16)
                act.wait_ge(split_used, (layer + 1) * SPLIT_LAYER + 2)
                act.dma_start(h, hdram[ds(act.snap(layer * KB), KB), :, :].rearrange("m p t -> p m t")).then_inc(h_back, 16)
                act.dma_start(cst[:, MASKS:], const[:, MASKS:]).then_inc(masks_back, 16)
            squares(2 * L + 1, L, "norm1")

        @block.gpsimd
        def _(pool):
            G = nc.gpsimd
            pool.wait_ge(const_in, 16)
            with pool.Fori(0, L) as layer:
                with pool.Fori(0, KB) as m:
                    q8 = layer * KB + m
                    dst = vfirst[ds(pool.snap(q8), 1), :, :]
                    src = vfirst[ds(pool.snap(m), 1), :, :]
                    pool.wait_ge(free[1], use(layer, "rwkv", 1, m + 1))
                    pool.dma_start(dst, tmp["zv"]).then_inc(vf_out, 16)
                    pool.wait_ge(vf_out, q8 * 16 + 16)
                    pool.dma_start(tmp["vf"], src).then_inc(vf_in, 16)
                with pool.Fori(0, NC) as c:
                    qc = layer * NC + c
                    pool.wait_ge(bd_zero, layer + 1)
                    for src, dst, b, per in ((fv, bdv, 1, 7), (fr, bdr, 3, 9)):
                        pool.wait_ge(ready[b], use(layer, "scan", b, c * per - 1))
                        for e in range(2):
                            r = slice(e * CH, (e + 1) * CH)
                            last = G.tensor_copy(dst[r, :, e * CH:(e + 1) * CH], src[r, :, ts(c, CH)])
                    last.then_inc(bd_pool, 1)
                    pool.wait_ge(l_ready, qc * 2 + 2)
                    pool.wait_ge(ready[3], use(layer, "scan", 3, c * 9 + 2))
                    for lv in range(2, LEVELS + 1):
                        if lv > 2:
                            pool.wait_ge(ready[1], use(layer, "scan", 1, c * 7 + (lv - 2)))
                        mask = cc("lvl", lv - 1, P).rearrange("p (o c) -> p o c", o=1).broadcast_to([P, KB, P])
                        G.tensor_tensor(loff, lt, mask, ALU.mult).then_inc(loff_ready, 1)
                pool.wait_ge(gm_in, layer * 16 + 16)
                G.tensor_tensor(wst, wst, cc("causal").rearrange("p (o c) -> p o c", o=1).broadcast_to([P, KB, P]),
                                ALU.mult).then_inc(ws_ready, 1)

                def low_parts(section):
                    with pool.Fori(0, dict(RING)[section] // 2) as i:
                        for k in range(2):
                            for part in range(4):
                                s, _ = ring(layer, section, k, i, 2)
                                pool.wait_ge(high_ready, split(layer, section, 4 * k + part, i, 2) + 1)
                                G.tensor_tensor(wsplit[:, part % 2, 1, :], slots[:, s, part * QT:(part + 1) * QT],
                                                wsplit[:, part % 2, 0, :].bitcast(F32), ALU.subtract).then_inc(low_ready, 1)

                low_parts("zu")
                low_parts("mix")
                low_parts("pleg")
                low_parts("wq")
                pool.wait_ge(nhigh_ready, layer * KB + KB)
                pool.wait_ge(ready[1], use(layer, "h0", 1, 15))
                for k in range(KB):
                    G.tensor_tensor(n_low[k], n[:, k, 1:NW], n_high[k].bitcast(F32), ALU.subtract).then_inc(nlow_ready, 1)

                for section in ("u1", "u2", "u3"):
                    low_parts(section)


def pack(inputs):
    g = {k: np.ascontiguousarray(a) for k, a in inputs.items()}

    def blocks(a, cols=P):
        k, m = a.shape
        return a.reshape(k // P, P, m // cols, cols).transpose(2, 1, 0, 3)

    def pad(a, cols=SLOT):
        a = a.reshape(a.shape[0], P, -1)
        if a.shape[2] == cols:
            return a
        return np.concatenate([a, np.zeros((a.shape[0], P, cols - a.shape[2]), a.dtype)], axis=2)

    W = 1024
    w_all, lo_all, u_all, v_all, gm_all, vec_all, pt_all = [], [], [], [], [], [], []
    for i in range(L):
        m0 = max(i - 1, 0)
        z = g["w_in"][i]
        c = np.cumsum([0, W, W, W, 64, 64, 128, W, W, W, W])
        zr, zk, zv = (z[:, c[j]:c[j + 1]] for j in range(3))
        part = {
            "wa": pad(blocks(z[:, c[3]:c[5]])), "zg": pad(blocks(z[:, c[5]:c[6]])),
            "mv1": pad(blocks(g["rw_mv_w1"][m0], 32)),
            "rwkv": np.stack([blocks(zk), blocks(zv), blocks(zr)], axis=1).reshape(3 * KB, P, SLOT),
            "g2": pad(g["rw_g2"][i][None]),
        }
        zgv = z[:, c[7]:c[8]].reshape(4, 4, P, 2, T)
        zgv = zgv.transpose(3, 0, 2, 1, 4).reshape(2, 4, P, SLOT)
        part["gvA"], part["gvB"] = zgv[0], zgv[1]
        part["zu"] = pad(blocks(z[:, c[6]:c[7]]))
        proj = np.concatenate([blocks(g["w_proj_a"][i]), blocks(g["w_proj_b"][i])], axis=2)
        part["mix"] = np.stack([pad(blocks(z[:, c[8]:c[9]])), pad(blocks(z[:, c[9]:c[10]])),
                                proj.reshape(KB, P, SLOT)], axis=1).reshape(3 * KB, P, SLOT)

        def twos(a):
            b = blocks(a)
            return b.reshape(b.shape[0] // 2, 2, P, -1).transpose(0, 2, 1, 3).reshape(-1, P, SLOT)

        part["wout"] = twos(g["w_out"][i])
        part["plew"] = g["ple_w"][i].reshape(2, P, D).transpose(1, 0, 2).reshape(1, P, SLOT)
        part["pleg"] = twos(g["ple_gate"][i])
        part["wq"] = twos(g["peer_wq"][i])
        part["keys"] = g["peer_keys"][i].reshape(2 * HEADS, P, P).transpose(2, 0, 1).reshape(1, P, SLOT)
        w_all += [part[s] for s in PACKED]

        zero = np.zeros((64, W), np.float32)
        lw = np.concatenate([g["rw_w2"][i], zero])
        la = np.concatenate([zero, g["rw_a2"][i]])
        lm = np.concatenate([g["rw_mv_w2"][m0], np.zeros((96, W), np.float32)])
        lo_all.append(np.stack([a.reshape(P, KB, P) for a in (lw, la, lm)], axis=2).transpose(1, 0, 2, 3).reshape(KB, P, 3 * P))
        uu = g["peer_u"][i].reshape(P, P // 2, 2, KB, P)
        u_all.append(uu.transpose(1, 4, 2, 3, 0).reshape(P // 2, P, SLOT))
        vv = g["peer_v"][i].reshape(P, NG, 2, JG // 2, KB, P)
        v_all.append(vv.transpose(1, 4, 2, 0, 3, 5).reshape(NG * KB * 2, P, SLOT))
        rows = lambda a: np.broadcast_to(a.reshape(1, -1), (P, D))
        gm_all.append(np.concatenate([g["gm_ws"][i].transpose(2, 0, 1).reshape(P, D), rows(g["gm_ln_g"][i]),
                                      rows(g["gm_ln_b"][i]), rows(g["gm_bs"][i])], axis=1))
        vs = [g["norm_mix"][i], g["rw_w0"][i], g["rw_a0"][i], g["rw_kk"][i], g["rw_ka"][i], g["rw_rk"][i],
              g["rw_ln_g"][i], g["rw_ln_b"][i], g["rw_mv_v0"][m0], g["norm_ffn"][i], g["norm_final"]]
        vec_all.append(np.stack([a.reshape(KB, P) for a in vs]).transpose(2, 0, 1).reshape(P, -1))
        pt_all.append(g["p"][i, 0].reshape(T, 2, P).transpose(2, 1, 0).reshape(P, 2 * T))
    c_ = np.ascontiguousarray
    return {
        "x": c_(g["x"][0].reshape(T, KB, P).transpose(2, 1, 0)),
        "w": c_(np.concatenate(w_all)), "lo": c_(np.concatenate(lo_all)), "u": c_(np.concatenate(u_all)),
        "v": c_(np.concatenate(v_all)), "pt": c_(np.stack(pt_all)), "gm": c_(np.stack(gm_all)),
        "vec": c_(np.stack(vec_all)), "const": constants(),
    }


def kernel(**inputs):
    import concourse.bacc as bacc
    from concourse.bass_utils import run_bass_kernel_spmd

    nc = bacc.Bacc("TRN2", target_bir_lowering=False, num_devices=1)
    arrays = pack(inputs)
    args = [nc.dram_tensor(f"in_{k}", a.shape, F32, kind="ExternalInput").ap() for k, a in arrays.items()]
    out = nc.dram_tensor("out", (P, KB, T), F32, kind="ExternalOutput").ap()
    vfirst = nc.dram_tensor("v_first", (L * KB, P, T), F32, kind="Internal").ap()
    hdram = nc.dram_tensor("h_spill", (L * KB, P, T), F32, kind="Internal").ap()
    trunk_kernel(nc, *args, out, vfirst, hdram)
    r = run_bass_kernel_spmd(nc, [{f"in_{k}": a for k, a in arrays.items()}], core_ids=[0])
    got = r.results[0]["out"]
    return np.ascontiguousarray(got.transpose(2, 1, 0).reshape(1, T, D))
```
